# Optimizing a Trainium2 kernel written in Bass

```python
import jax, jax.numpy as jnp
from jax import lax
import numpy as np

D_MODEL = 1024
BATCH = 1
SEQ = 1024
DEPTH = 1
DEC_BATCH = 1
DEC_SEQ = 512
PAST_LEN = 128

MLA_HEADS = 4
MLA_NOPE = 128
MLA_ROPE = 64
MLA_VDIM = 128
MLA_Q_LORA = 256
MLA_KV_LORA = 128
MLA_WIDTH = MLA_HEADS * MLA_VDIM
MLA_SCALE = (MLA_NOPE + MLA_ROPE) ** -0.5
ROPE_BASE = 10000.0
Q_BLOCK = 128
POOL_WINDOWS = (2, 4, 8, 16)
POOL_GROUPS = len(POOL_WINDOWS)
POOL_WIDTH = D_MODEL // 4
POOL_GROUP_DIM = POOL_WIDTH // POOL_GROUPS
GLA_HEADS = 4
GLA_WIDTH = D_MODEL // 4
GLA_KEY = GLA_WIDTH // 2
GLA_DK = GLA_KEY // GLA_HEADS
GLA_DV = GLA_WIDTH // GLA_HEADS
GLA_GATE_RANK = 16
GLA_GATE_NORM = 16.0
GLA_CHUNK = 64

MIX_WIDTH = MLA_WIDTH + POOL_WIDTH + GLA_WIDTH
NORM_EPS = 1e-6

IN_SIZES = (MLA_Q_LORA, MLA_KV_LORA, MLA_ROPE, MLA_WIDTH,
            POOL_WIDTH, POOL_WIDTH,
            GLA_KEY, GLA_KEY, GLA_WIDTH, GLA_GATE_RANK, GLA_GATE_RANK, GLA_WIDTH)
IN_COLS = sum(IN_SIZES)
IN_SPLITS = tuple(int(v) for v in np.cumsum(IN_SIZES)[:-1])

kernel_name = "hymba_mla_pool_gla_encoder"

def rmsnorm(x, g):
    xf = x.astype(jnp.float32)
    y = xf * lax.rsqrt(jnp.mean(xf * xf, axis=-1, keepdims=True) + NORM_EPS)
    return (y * g.astype(jnp.float32)).astype(x.dtype)

def rope_tables(seq):
    inv_freq = 1.0 / (ROPE_BASE ** (jnp.arange(0, MLA_ROPE, 2, dtype=jnp.float32) / MLA_ROPE))
    ang = jnp.arange(seq, dtype=jnp.float32)[:, None] * inv_freq[None, :]
    return jnp.cos(ang), jnp.sin(ang)

def apply_rope(x, cos, sin):
    xf = x.astype(jnp.float32)
    x1, x2 = jnp.split(xf, 2, axis=-1)
    return jnp.concatenate([x1 * cos - x2 * sin, x2 * cos + x1 * sin], axis=-1).astype(x.dtype)

def mla_mixer(c_q, c_kv, k_rope, q_norm_g, w_uq, kv_norm_g, w_ukv):
    B, S, _ = c_q.shape
    q = jnp.einsum('bsr,re->bse', rmsnorm(c_q, q_norm_g), w_uq).reshape(B, S, MLA_HEADS, MLA_NOPE + MLA_ROPE)
    q_nope, q_rope = q[..., :MLA_NOPE], q[..., MLA_NOPE:]
    kv = jnp.einsum('bsr,re->bse', rmsnorm(c_kv, kv_norm_g), w_ukv).reshape(B, S, MLA_HEADS, MLA_NOPE + MLA_VDIM)
    k_nope, v = kv[..., :MLA_NOPE], kv[..., MLA_NOPE:]
    cos, sin = rope_tables(S)
    q_rope = apply_rope(q_rope, cos[None, :, None, :], sin[None, :, None, :])
    k_rope = apply_rope(k_rope, cos[None], sin[None])
    nb = S // Q_BLOCK
    qn_b = q_nope.reshape(B, nb, Q_BLOCK, MLA_HEADS, MLA_NOPE).transpose(1, 0, 2, 3, 4)
    qr_b = q_rope.reshape(B, nb, Q_BLOCK, MLA_HEADS, MLA_ROPE).transpose(1, 0, 2, 3, 4)

    def attend(blk):
        qn, qr = blk
        s = (jnp.einsum('bqhd,bkhd->bhqk', qn, k_nope, preferred_element_type=jnp.float32)
             + jnp.einsum('bqhr,bkr->bhqk', qr, k_rope, preferred_element_type=jnp.float32))
        p = jax.nn.softmax(s * MLA_SCALE, axis=-1)
        return jnp.einsum('bhqk,bkhd->bqhd', p.astype(v.dtype), v)

    o = lax.map(attend, (qn_b, qr_b))
    return o.transpose(1, 0, 2, 3, 4).reshape(B, S, MLA_WIDTH).astype(c_q.dtype)

def pool_mixer(u, w_pool, pool_scale):
    B, S, C = u.shape
    uf = u.astype(jnp.float32)
    cs = jnp.concatenate([jnp.zeros((B, 1, C), jnp.float32), jnp.cumsum(uf, axis=1)], axis=1)
    t = jnp.arange(S)
    outs = []
    for gi, w in enumerate(POOL_WINDOWS):
        lo = jnp.clip(t - w // 2, 0, S)
        hi = jnp.clip(t + w // 2, 0, S)
        csg = cs[..., gi * POOL_GROUP_DIM:(gi + 1) * POOL_GROUP_DIM]
        win_sum = jnp.take(csg, hi, axis=1) - jnp.take(csg, lo, axis=1)
        cnt = (hi - lo).astype(jnp.float32)[None, :, None]
        outs.append(win_sum / cnt)
    pooled = jnp.concatenate(outs, axis=-1) - uf
    pooled = pooled.reshape(B, S, POOL_GROUPS, POOL_GROUP_DIM).astype(u.dtype)
    y = jnp.einsum('bsgc,gcd->bsgd', pooled, w_pool).reshape(B, S, C)
    return (y * pool_scale).astype(u.dtype)

def gla_direction(q, k, v, g):
    B, S, H, DK = q.shape
    DV = v.shape[-1]
    n = S // GLA_CHUNK

    def to_chunks(a):
        return a.reshape(B, n, GLA_CHUNK, H, a.shape[-1]).transpose(1, 0, 3, 2, 4)

    mask = jnp.tril(jnp.ones((GLA_CHUNK, GLA_CHUNK), dtype=bool))[None, None, :, :, None]

    def step(state, inp):
        qc, kc, vc, gc = inp
        b = jnp.cumsum(gc, axis=2)
        o_inter = jnp.einsum('bhcd,bhde->bhce', qc * jnp.exp(b), state)
        decay = jnp.exp(jnp.where(mask, b[:, :, :, None, :] - b[:, :, None, :, :], -jnp.inf))
        a = jnp.einsum('bhid,bhijd,bhjd->bhij', qc, decay, kc)
        o = o_inter + jnp.einsum('bhij,bhje->bhie', a, vc)
        b_last = b[:, :, -1, :]
        state = (jnp.exp(b_last)[..., None] * state
                 + jnp.einsum('bhcd,bhce->bhde', kc * jnp.exp(b_last[:, :, None, :] - b), vc))
        return state, o

    s0 = jnp.zeros((B, H, DK, DV), jnp.float32)
    _, o = lax.scan(step, s0, (to_chunks(q), to_chunks(k), to_chunks(v), to_chunks(g)))
    return o.transpose(1, 0, 3, 2, 4).reshape(B, S, H, DV)

def gla_mixer(q_in, k_in, v_in, lr_fwd, lr_bwd, gk_up_fwd, gk_bias_fwd, gk_up_bwd, gk_bias_bwd, gla_norm_g):
    B, S, _ = q_in.shape
    f32 = jnp.float32
    q = q_in.astype(f32).reshape(B, S, GLA_HEADS, GLA_DK) * (GLA_DK ** -0.5)
    k = k_in.astype(f32).reshape(B, S, GLA_HEADS, GLA_DK)
    v = v_in.astype(f32).reshape(B, S, GLA_HEADS, GLA_DV)

    def log_gate(lr, up, bias):
        z = jnp.einsum('bsr,rk->bsk', lr, up).astype(f32) + bias.astype(f32)
        return (jax.nn.log_sigmoid(z) / GLA_GATE_NORM).reshape(B, S, GLA_HEADS, GLA_DK)

    g_f = log_gate(lr_fwd, gk_up_fwd, gk_bias_fwd)
    g_b = log_gate(lr_bwd, gk_up_bwd, gk_bias_bwd)
    o_f = gla_direction(q, k, v, g_f)
    o_b = gla_direction(q[:, ::-1], k[:, ::-1], v[:, ::-1], g_b[:, ::-1])[:, ::-1]
    o = rmsnorm(o_f + o_b, gla_norm_g)
    return o.reshape(B, S, GLA_WIDTH).astype(q_in.dtype)

def hybrid_layer(x, norm_g, w_in, q_norm_g, w_uq, kv_norm_g, w_ukv, w_pool, pool_scale,
                 gk_up_fwd, gk_bias_fwd, gk_up_bwd, gk_bias_bwd, gla_norm_g, w_out):
    h = rmsnorm(x, norm_g)
    z = jnp.einsum('bsd,de->bse', h, w_in)
    (c_q, c_kv, k_rope, gate_mla, u_pool, gate_pool,
     q_gla, k_gla, v_gla, lr_fwd, lr_bwd, gate_gla) = jnp.split(z, IN_SPLITS, axis=-1)
    o_mla = mla_mixer(c_q, c_kv, k_rope, q_norm_g, w_uq, kv_norm_g, w_ukv)
    o_pool = pool_mixer(u_pool, w_pool, pool_scale)
    o_gla = gla_mixer(q_gla, k_gla, v_gla, lr_fwd, lr_bwd, gk_up_fwd, gk_bias_fwd,
                      gk_up_bwd, gk_bias_bwd, gla_norm_g)
    mixed = jnp.concatenate([o_mla * jax.nn.silu(gate_mla),
                             o_pool * jax.nn.silu(gate_pool),
                             o_gla * jax.nn.silu(gate_gla)], axis=-1).astype(x.dtype)
    return x + jnp.einsum('bse,ed->bsd', mixed, w_out)

def setup_inputs(seed: int = 0) -> dict:
    key = jax.random.key(seed)
    ks = jax.random.split(key, 20)
    f32 = jnp.float32

    def nrm(k, shape, fan_in):
        return jax.random.normal(k, shape, f32) * (fan_in ** -0.5)

    def gain(k, shape):
        return 1.0 + 0.02 * jax.random.normal(k, shape, f32)

    return {
        "x_prompt": jax.random.normal(ks[0], (BATCH, SEQ, D_MODEL), f32),
        "x_sample": jax.random.normal(ks[1], (DEC_BATCH, DEC_SEQ, D_MODEL), f32),
        "norm_g": gain(ks[2], (DEPTH, D_MODEL)),
        "w_in": nrm(ks[3], (DEPTH, D_MODEL, IN_COLS), D_MODEL),
        "q_norm_g": gain(ks[4], (DEPTH, MLA_Q_LORA)),
        "w_uq": nrm(ks[5], (DEPTH, MLA_Q_LORA, MLA_HEADS * (MLA_NOPE + MLA_ROPE)), MLA_Q_LORA),
        "kv_norm_g": gain(ks[6], (DEPTH, MLA_KV_LORA)),
        "w_ukv": nrm(ks[7], (DEPTH, MLA_KV_LORA, MLA_HEADS * (MLA_NOPE + MLA_VDIM)), MLA_KV_LORA),
        "w_pool": nrm(ks[8], (DEPTH, POOL_GROUPS, POOL_GROUP_DIM, POOL_GROUP_DIM), POOL_GROUP_DIM),
        "pool_scale": gain(ks[9], (DEPTH, POOL_WIDTH)),
        "gk_up_fwd": nrm(ks[10], (DEPTH, GLA_GATE_RANK, GLA_KEY), GLA_GATE_RANK),
        "gk_bias_fwd": 0.1 * jax.random.normal(ks[11], (DEPTH, GLA_KEY), f32),
        "gk_up_bwd": nrm(ks[12], (DEPTH, GLA_GATE_RANK, GLA_KEY), GLA_GATE_RANK),
        "gk_bias_bwd": 0.1 * jax.random.normal(ks[13], (DEPTH, GLA_KEY), f32),
        "gla_norm_g": gain(ks[14], (DEPTH, GLA_DV)),
        "w_out": nrm(ks[15], (DEPTH, MIX_WIDTH, D_MODEL), MIX_WIDTH),
        "final_norm_g": gain(ks[16], (D_MODEL,)),
    }

def reference(x_prompt, x_sample, norm_g, w_in, q_norm_g, w_uq, kv_norm_g, w_ukv, w_pool, pool_scale,
              gk_up_fwd, gk_bias_fwd, gk_up_bwd, gk_bias_bwd, gla_norm_g, w_out, final_norm_g):
    def trunk(x):
        for l in range(DEPTH):
            x = hybrid_layer(x, norm_g[l], w_in[l], q_norm_g[l], w_uq[l], kv_norm_g[l], w_ukv[l],
                             w_pool[l], pool_scale[l], gk_up_fwd[l], gk_bias_fwd[l], gk_up_bwd[l],
                             gk_bias_bwd[l], gla_norm_g[l], w_out[l])
        return rmsnorm(x, final_norm_g)

    y_prompt = trunk(x_prompt)
    y_sample = trunk(x_sample)
    return (y_prompt, y_sample)


_drawn_inputs = setup_inputs


def setup_inputs(seed=0):
    import zlib

    import numpy as np

    out = dict(_drawn_inputs(seed))
    spreads = {}
    factors = {'norm_g': 4.099,
     'q_norm_g': 34.569,
     'kv_norm_g': 31.957,
     'pool_scale': 85.51,
     'gk_up_fwd': 2.953,
     'gk_bias_fwd': 34.724,
     'gk_up_bwd': 2.968,
     'gk_bias_bwd': 35.704,
     'gla_norm_g': 200.0,
     'final_norm_g': 23.486}
    for name, (base, spread) in spreads.items():
        noise = np.random.default_rng([zlib.crc32(name.encode()), seed]).standard_normal(out[name].shape)
        drawn = base * np.exp(spread * noise) if base else spread * noise
        out[name] = __import__('jax').numpy.asarray(drawn.astype(out[name].dtype))
    for name, factor in factors.items():
        out[name] = (out[name] * factor).astype(out[name].dtype)
    return out
```

```python
from contextlib import ExitStack

import concourse.bass as bass
from concourse import mybir

F32 = mybir.dt.float32
F32R = mybir.dt.float32r
ALU = mybir.AluOpType
ACT = mybir.ActivationFunctionType
AX_X = mybir.AxisListType.X

P = 128
D_MODEL = 1024
SEQS = ((0, 1024), (1024, 512))
NT = 1536
TILES = NT // P
KT = D_MODEL // P
BLK = 512
TB = NT // BLK
EPS = 1e-6

Z_LR, Z_Q, Z_K, Z_V, Z_U, Z_CQ, Z_CKV = 0, 1, 2, 3, 5, 7, 9
Z_PLAIN = 10
Z_GATES = 8
Z_TILES = Z_PLAIN + Z_GATES


def rows_of(t):
    return bass.ds(t * P, P)


Z_AT = 0
AFTER_Z = Z_PLAIN * NT * 4
H_BYTES = KT * NT * 4
MLA_AT = AFTER_Z
MLA_BYTES = 4 * NT * 4
SBUF_BYTES = 212224


class Region:

    def __init__(self, nc, at, end=SBUF_BYTES):
        self.nc, self.at, self.end = nc, at, end
        self.base = -(-nc.sbuf_base // 64) * 64

    def __call__(self, name, shape, dtype=F32):
        size = 4
        for n in shape[1:]:
            size *= n
        at, self.at = self.at, self.at + -(-size // 32) * 32
        assert self.at <= self.end, (name, self.at, self.end)
        return self.nc.alloc_sbuf_tensor_at(name, shape, dtype, offset=self.base + at)


def phase_norm_transpose(nc, cx, x_dram, norm_g_dram, h_hi, h_lo, ident, psum, ident_dram):
    with ExitStack() as mem:
        sb = Region(nc, AFTER_Z + 2 * H_BYTES)
        sem = cx.semaphore
        x_in = sb("n_x_in", [P, 2, D_MODEL])
        x_norm = sb("n_x_norm", [P, 2, D_MODEL])
        g_row = sb("n_g_row", [P, D_MODEL])
        squares = sb("n_squares", [P, 2, D_MODEL])
        mean_sq = sb("n_mean_sq", [P, 2])
        rstd = sb("n_rstd", [P, 2])
        eps = sb("n_eps", [P, 1])
        minus_half = sb("n_minus_half", [P, 1])

        x_loaded = [sem(f"n_x_loaded{s}") for s in range(2)]
        consts_loaded = sem("n_consts_loaded")
        half_set = sem("n_half_set")
        squares_done = sem("n_squares_done")
        eps_added = sem("n_eps_added")
        rstd_ready = sem("n_rstd_ready")
        norm_ready = sem("n_norm_ready")
        turned = sem("n_turned")
        hi_ready = sem("n_hi_ready")
        lo_ready = sem("n_lo_ready")

        block = mem.enter_context(nc.Block())

        @block.sync
        def _(sp):
            def load(i, s, first):
                if not first:
                    sp.wait_ge(norm_ready, 2 * i + s - 1)
                sp.dma_start(x_in[:, s, :], x_dram[rows_of(2 * i + s), :]).then_inc(x_loaded[s], 16)

            for s in range(2):
                load(0, s, True)
            sp.dma_start(g_row[:, :], norm_g_dram.partition_broadcast(P)).then_inc(consts_loaded, 16)
            sp.dma_start(ident[:, :], ident_dram).then_inc(consts_loaded, 16)
            with sp.Fori(1, TILES // 2) as i:
                for s in range(2):
                    load(i, s, False)

        @block.scalar
        def _(act):
            def square(i, s, first=False):
                act.wait_ge(x_loaded[s], 16 * i + 16)
                if not first:
                    act.wait_ge(eps_added, 2 * i + s - 1)
                nc.scalar.activation(squares[:, s, :], x_in[:, s, :], ACT.Square, scale=D_MODEL ** -0.5,
                                     accum_out=mean_sq[:, s:s + 1]).then_inc(squares_done, 1)

            def take_hi(i, s):
                n = 2 * i + s
                for half in range(2):
                    act.wait_ge(turned, 2 * n + half + 1)
                    nc.scalar.activation(h_hi[:, 4 * half:4 * half + 4, rows_of(n)],
                                         psum[:, 2 * s + half, :].rearrange("p (k t) -> p k t", k=4),
                                         ACT.Copy).then_inc(hi_ready, 1)

            square(0, 0, True)
            square(0, 1, True)
            take_hi(0, 0)
            square(1, 0)
            take_hi(0, 1)
            with act.Fori(1, TILES // 2 - 1) as i:
                square(i, 1)
                take_hi(i, 0)
                square(i + 1, 0)
                take_hi(i, 1)
            last = TILES // 2 - 1
            square(last, 1)
            take_hi(last, 0)
            take_hi(last, 1)

        @block.gpsimd
        def _(pool):
            nc.gpsimd.memset(minus_half[:, :], -0.5).then_inc(half_set, 1)
            nc.gpsimd.memset(eps[:, :], EPS).then_inc(half_set, 1)
            pool.wait_ge(half_set, 2)
            with pool.Fori(0, TILES // 2) as i:
                for s in range(2):
                    n, slot = 2 * i + s, slice(s, s + 1)
                    pool.wait_ge(squares_done, n + 1)
                    nc.gpsimd.tensor_tensor(rstd[:, slot], mean_sq[:, slot], eps[:, :], ALU.add).then_inc(eps_added, 1)
                    pool.wait_ge(eps_added, n + 1)
                    nc.gpsimd.tensor_tensor(rstd[:, slot], rstd[:, slot], minus_half[:, :],
                                            ALU.pow).then_inc(rstd_ready, 1)

        @block.vector
        def _(dve):
            def normalise(i, s, first):
                n = 2 * i + s
                dve.wait_ge(rstd_ready, n + 1)
                if not first:
                    dve.wait_ge(turned, 2 * n - 2)
                nc.vector.scalar_tensor_tensor(out=x_norm[:, s, :], in0=x_in[:, s, :],
                                               scalar=rstd[:, s:s + 1], in1=g_row[:, :],
                                               op0=ALU.mult, op1=ALU.mult).then_inc(norm_ready, 1)

            def take_lo(i, s):
                n = 2 * i + s
                for half in range(2):
                    dve.wait_ge(hi_ready, 2 * n + half + 1)
                    ks = slice(4 * half, 4 * half + 4)
                    nc.vector.tensor_tensor(h_lo[:, ks, rows_of(n)],
                                            psum[:, 2 * s + half, :].rearrange("p (k t) -> p k t", k=4),
                                            h_hi[:, ks, rows_of(n)].bitcast(F32),
                                            ALU.subtract).then_inc(lo_ready, 1)

            dve.wait_ge(consts_loaded, 32)
            normalise(0, 0, True)
            normalise(0, 1, True)
            take_lo(0, 0)
            with dve.Fori(1, TILES // 2) as i:
                normalise(i, 0, False)
                take_lo(i - 1, 1)
                normalise(i, 1, False)
                take_lo(i, 0)
            take_lo(TILES // 2 - 1, 1)

        @block.tensor
        def _(pe):
            def turn(i, s, first):
                n = 2 * i + s
                pe.wait_ge(norm_ready, n + 1)
                for half in range(2):
                    if not first:
                        pe.wait_ge(lo_ready, 2 * n - 3 + half)
                    for k in range(4):
                        mm = nc.tensor.transpose(psum[:, 2 * s + half, k * P:(k + 1) * P],
                                                 x_norm[:, s, (4 * half + k) * P:(4 * half + k + 1) * P],
                                                 ident[:, :])
                    mm.then_inc(turned, 1)

            pe.wait_ge(consts_loaded, 32)
            turn(0, 0, True)
            turn(0, 1, True)
            with pe.Fori(1, TILES // 2) as i:
                for s in range(2):
                    turn(i, s, False)


POOL_PAD = 8
PADDED = NT + 2 * len(SEQS) * POOL_PAD
POOL_AT = (POOL_PAD, SEQS[0][1] + 3 * POOL_PAD)


def phase_project(nc, cx, w_z_dram, gates_dram, pool_edge_dram, pool_mean_dram, h_hi, h_lo, z, psum):
    with ExitStack() as mem:
        sb = Region(nc, AFTER_Z + 2 * H_BYTES)
        sem = cx.semaphore
        w_raw = sb("z_w_raw", [P, 2, D_MODEL])
        w_hi = sb("z_w_hi", [P, 2, D_MODEL], F32R)
        w_lo = sb("z_w_lo", [P, 2, D_MODEL], F32R)
        gate = sb("z_gate", [P, 2, NT])
        sums = [sb(f"z_sums{n}", [P, PADDED]) for n in range(2)]
        pool_edge = sb("z_pool_edge", [P, 2, 2, POOL_PAD])
        pool_mean = sb("z_pool_mean", [P, 2])

        w_loaded = [sem(f"z_w_loaded{s}") for s in range(2)]
        gate_stored = [sem(f"z_gate_stored{s}") for s in range(2)]
        w_hi_ready = sem("z_w_hi_ready")
        w_lo_ready = sem("z_w_lo_ready")
        z_done = sem("z_done")
        z_emptied = sem("z_emptied")
        pool_loaded = sem("z_pool_loaded")
        pool_step = sem("z_pool_step")
        pairs = Z_TILES // 2

        block = mem.enter_context(nc.Block())

        @block.sync
        def _(sp):
            def load(i, s, first):
                if not first:
                    sp.wait_ge(w_lo_ready, 2 * i + s - 1)
                sp.dma_start(w_raw[:, s, :], w_z_dram[bass.ds(2 * i + s, 1), :, :].rearrange("a p n -> (a p) n"))\
                  .then_inc(w_loaded[s], 16)

            for s in range(2):
                load(0, s, True)
            sp.dma_start(pool_edge[:, :, :, :], pool_edge_dram).then_inc(pool_loaded, 16)
            sp.dma_start(pool_mean[:, :], pool_mean_dram).then_inc(pool_loaded, 16)
            with sp.Fori(1, pairs) as i:
                for s in range(2):
                    load(i, s, False)

        @block.scalar
        def _(act):
            def split_hi(i, s, first):
                act.wait_ge(w_loaded[s], 16 * i + 16)
                if not first:
                    act.wait_ge(z_done, TB * (2 * i + s) - TB)
                nc.scalar.activation(w_hi[:, s, :], w_raw[:, s, :], ACT.Copy).then_inc(w_hi_ready, 1)

            def empty(i, s):
                n = 2 * i + s
                for tb in range(TB):
                    act.wait_ge(z_done, TB * n + tb + 1)
                    nc.scalar.activation(
                        z[:, bass.ds(n, 1), tb * BLK:(tb + 1) * BLK].rearrange("p a t -> p (a t)"),
                        psum[:, TB * s + tb, :], ACT.Copy).then_inc(z_emptied, 1)

            def empty_gate(i, s, first):
                n = 2 * i + s
                if not first:
                    act.wait_ge(gate_stored[s], 16 * i - 8 * Z_PLAIN)
                for tb in range(TB):
                    act.wait_ge(z_done, TB * n + tb + 1)
                    nc.scalar.activation(gate[:, s, tb * BLK:(tb + 1) * BLK], psum[:, TB * s + tb, :],
                                         ACT.Silu).then_inc(z_emptied, 1)
                act.wait_ge(z_emptied, TB * n + TB)
                act.dma_start(gates_dram[bass.ds(n - Z_PLAIN, 1), :, :].rearrange("a p t -> (a p) t"),
                              gate[:, s, :]).then_inc(gate_stored[s], 16)

            split_hi(0, 0, True)
            split_hi(0, 1, True)
            empty(0, 0)
            with act.Fori(1, Z_PLAIN // 2) as i:
                split_hi(i, 0, False)
                empty(i - 1, 1)
                split_hi(i, 1, False)
                empty(i, 0)
            i = Z_PLAIN // 2
            split_hi(i, 0, False)
            empty(i - 1, 1)
            split_hi(i, 1, False)
            empty_gate(i, 0, True)
            split_hi(i + 1, 0, False)
            empty_gate(i, 1, True)
            split_hi(i + 1, 1, False)
            empty_gate(i + 1, 0, False)
            with act.Fori(Z_PLAIN // 2 + 2, pairs) as i:
                split_hi(i, 0, False)
                empty_gate(i - 1, 1, False)
                split_hi(i, 1, False)
                empty_gate(i, 0, False)
            empty_gate(pairs - 1, 1, False)
            for s in range(2):
                act.wait_ge(gate_stored[s], 8 * Z_GATES)

        @block.gpsimd
        def _(pool):
            def split_lo(i, s, first):
                pool.wait_ge(w_hi_ready, 2 * i + s + 1)
                if not first:
                    pool.wait_ge(z_done, TB * (2 * i + s) - TB)
                nc.gpsimd.tensor_tensor(w_lo[:, s, :], w_raw[:, s, :], w_hi[:, s, :].bitcast(F32),
                                        ALU.subtract).then_inc(w_lo_ready, 1)

            for s in range(2):
                split_lo(0, s, True)
            with pool.Fori(1, pairs) as i:
                for s in range(2):
                    split_lo(i, s, False)

        @block.vector
        def _(dve):
            steps = [0]

            def step(instruction):
                steps[0] += 1
                instruction.then_inc(pool_step, 1)
                dve.wait_ge(pool_step, steps[0])

            even, odd = sums
            dve.wait_ge(pool_loaded, 32)
            dve.wait_ge(z_emptied, TB * (Z_U + 2))
            for u in range(2):
                step(nc.vector.memset(even[:, :], 0.0))
                step(nc.vector.memset(odd[:, :], 0.0))
                for (t0, n), at in zip(SEQS, POOL_AT):
                    step(nc.vector.tensor_copy(even[:, at:at + n], z[:, Z_U + u, t0:t0 + n]))
                upper = slice(64, P)
                step(nc.vector.tensor_tensor(odd[:, 1:], even[:, :-1], even[:, 1:], ALU.add))
                rows = upper if u == 0 else slice(0, P)
                step(nc.vector.tensor_tensor(even[rows, 1:-1], odd[rows, :-2], odd[rows, 2:], ALU.add))
                if u == 1:
                    step(nc.vector.tensor_tensor(odd[:, 2:-2], even[:, :-4], even[:, 4:], ALU.add))
                    step(nc.vector.tensor_tensor(even[upper, 4:-4], odd[upper, :-8], odd[upper, 8:], ALU.add))
                for rows, total in ((slice(0, 64), odd), (upper, even)):
                    for (t0, n), at in zip(SEQS, POOL_AT):
                        ends = total[rows, at:at + n].rearrange("p (a b) -> p a b", b=POOL_PAD)[:, ::n // POOL_PAD - 1, :]
                        step(nc.vector.tensor_tensor(ends, ends, pool_edge[rows, u, :, :], ALU.mult))
                        out = z[rows, Z_U + u, t0:t0 + n]
                        step(nc.vector.scalar_tensor_tensor(out=out, in0=total[rows, at:at + n],
                                                            scalar=pool_mean[rows, u:u + 1], in1=out,
                                                            op0=ALU.mult, op1=ALU.subtract))

        @block.tensor
        def _(pe):
            def project(i, s, first):
                n = 2 * i + s
                pe.wait_ge(w_lo_ready, n + 1)
                for tb in range(TB):
                    if not first:
                        pe.wait_ge(z_emptied, TB * n - 2 * TB + tb + 1)
                    t = slice(tb * BLK, (tb + 1) * BLK)
                    for k in range(KT):
                        c = slice(k * P, (k + 1) * P)
                        out = psum[:, TB * s + tb, :]
                        nc.tensor.matmul(out, w_hi[:, s, c], h_hi[:, k, t], start=(k == 0), stop=False)
                        nc.tensor.matmul(out, w_hi[:, s, c], h_lo[:, k, t], start=False, stop=False)
                        mm = nc.tensor.matmul(out, w_lo[:, s, c], h_hi[:, k, t], start=False, stop=(k == KT - 1))
                    mm.then_inc(z_done, 1)

            for s in range(2):
                project(0, s, True)
            with pe.Fori(1, pairs) as i:
                for s in range(2):
                    project(i, s, False)


CHUNK = 64
CHUNKS = NT // CHUNK
GROUP = BLK // CHUNK
SPLITS = (32, 16, 8, 4, 2, 1)
LEVELS = len(SPLITS) + 1
HEADS = 4
DK, DV = 32, 64
ENDS = tuple(t0 // CHUNK for t0, _ in SEQS), tuple((t0 + n) // CHUNK - 1 for t0, n in SEQS)
GLA_Q_SCALE = DK ** -0.5
GATE_SCALE = 1.0 / 16.0
FWD, BWD = 0, 1


def phase_gla(nc, cx, dram, gates_dram, z, psum, ident):
    with ExitStack() as mem:
        sb = Region(nc, AFTER_Z)
        sem = cx.semaphore
        gate_up = sb("g_gate_up", [P, 2, P])
        gate_bias = sb("g_gate_bias", [P, 2])
        scan_keep = sb("g_scan_keep", [P, CHUNKS * (CHUNK + 1)])
        level_mask = sb("g_level_mask", [P, LEVELS * CHUNK])
        pair_mask = sb("g_pair_mask", [P, P])
        head_ones = sb("g_head_ones", [P, 2])
        gla_gain = sb("g_gain", [P, 1])
        w_pool = sb("g_w_pool", [P, 2, P])
        pool_scale = sb("g_pool_scale", [P, 2])
        minus_half = sb("g_minus_half", [P, 1])
        sums = [sb(f"g_sums{d}", [P, CHUNKS, CHUNK + 1]) for d in range(2)]
        decay = sb("g_decay", [P, 2, CHUNKS])
        work = sb("g_work", [P, 4 * NT])
        q_in = [sb(f"g_q_in{d}", [P, NT]) for d in range(2)]
        k_turned = sb("g_k_turned", [P, 2, TILES, P])
        v_half = sb("g_v_half", [P, TILES, 2, HEADS * DV])
        state = sb("g_state", [P, 2, CHUNKS, P])
        expo = sb("g_expo", [P, 2, 2, BLK])
        weighted = sb("g_weighted", [P, 2, LEVELS * CHUNK])
        attn = sb("g_attn", [P, 2, HEADS, CHUNK])
        o_sq = sb("g_o_sq", [P, 2, BLK])
        stats = sb("g_stats", [P, 16])
        gate = sb("g_gate", [P, 2, BLK])

        temp = work[:, :].rearrange("p (a t) -> p a t", a=4)
        q_lv, k_lv = (work[:, n * 6 * BLK:(n + 1) * 6 * BLK].rearrange("p (l t) -> p l t", l=6) for n in range(2))
        o = expo[:, 0, :, :]

        consts_loaded = sem("g_consts_loaded")
        pool_set = sem("g_pool_set")
        gate_mm = sem("g_gate_mm")
        soft = sem("g_soft")
        dve_step = sem("g_dve_step")
        act_step = sem("g_act_step")
        pool_step = sem("g_pool_step")
        k_scaled = sem("g_k_scaled")
        v_mm = sem("g_v_mm")
        k_mm = sem("g_k_mm")
        turned_out = sem("g_turned_out")
        kv_mm = sem("g_kv_mm")
        kv_used = sem("g_kv_used")
        states_ready = sem("g_states_ready")
        expo_ready = sem("g_expo_ready")
        exp_done = sem("g_exp_done")
        q_lv_ready = sem("g_q_lv_ready")
        k_lv_ready = sem("g_k_lv_ready")
        attn_mm = sem("g_attn_mm")
        attn_read = sem("g_attn_read")
        attn_ready = sem("g_attn_ready")
        o_mm = sem("g_o_mm")
        o_taken = sem("g_o_taken")
        sq_taken = sem("g_sq_taken")
        stats_mm = sem("g_stats_mm")
        stats_taken = sem("g_stats_taken")
        rstd_ready = sem("g_rstd_ready")
        rstd_spread = sem("g_rstd_spread")
        spread_mm = sem("g_spread_mm")
        mixed = sem("g_mixed")
        gate_loaded = sem("g_gate_loaded")
        pool_mm = sem("g_pool_mm")
        pool_out = sem("g_pool_out")
        q, k = z[:, Z_Q, :], z[:, Z_K, :]
        chunked = lambda ap: ap.rearrange("p (c t) -> p c t", t=CHUNK)

        block = mem.enter_context(nc.Block())
        N_CONSTS = 8

        @block.sync
        def _(sp):
            sp.dma_start(gate_up[2 * DK:3 * DK, :, :], dram["gate_up"]).then_inc(consts_loaded, 16)
            sp.dma_start(gate_bias[:, :], dram["gate_bias"]).then_inc(consts_loaded, 16)
            sp.dma_start(level_mask[:, :], dram["level_mask"]).then_inc(consts_loaded, 16)
            sp.dma_start(pair_mask[:, :], dram["pair_mask"]).then_inc(consts_loaded, 16)
            sp.dma_start(head_ones[:, :], dram["head_ones"]).then_inc(consts_loaded, 16)
            sp.dma_start(gla_gain[:, :], dram["gla_gain"]).then_inc(consts_loaded, 16)
            sp.dma_start(w_pool[:, :, :], dram["w_pool"]).then_inc(consts_loaded, 16)
            sp.dma_start(pool_scale[:, :], dram["pool_scale"]).then_inc(consts_loaded, 16)
            for n in range(2 * TB):
                if n:
                    sp.wait_ge(pool_out if n <= TB else mixed, n if n <= TB else n - TB)
                row = 4 if n < TB else 6
                t = (n % TB) * BLK
                sp.dma_start(gate[:, :, :], gates_dram[row:row + 2, :, t:t + BLK].rearrange("a p t -> p a t"))\
                  .then_inc(gate_loaded, 16)

        @block.gpsimd
        def _(pool):
            steps = [0]

            def step(instruction):
                steps[0] += 1
                instruction.then_inc(pool_step, 1)
                pool.wait_ge(pool_step, steps[0])

            keep = scan_keep[:, :].rearrange("p (c t) -> p c t", t=CHUNK + 1)
            step(nc.gpsimd.memset(scan_keep[:, :], 1.0))
            nc.gpsimd.memset(keep[:, :, 0:1], 0.0).then_inc(pool_set, 1)
            nc.gpsimd.memset(minus_half[:, :], -0.5).then_inc(pool_set, 1)
            nc.gpsimd.memset(v_half[:, :, :, :], 0.0).then_inc(pool_set, 1)
            for d in range(2):
                for c in (ENDS[0] if d == FWD else ENDS[1]):
                    nc.gpsimd.memset(state[:, d, c, :], 0.0).then_inc(pool_set, 1)
            for d in range(2):
                pool.wait_ge(act_step, 8 + d)
                nc.gpsimd.tensor_tensor(temp[:, d, :], temp[:, d, :], k, ALU.mult).then_inc(k_scaled, 1)
            for d in range(2):
                pool.wait_ge(kv_used, 2 * CHUNKS)
                nc.gpsimd.tensor_tensor(state[:, d, :, :], state[:, d, :, :],
                                        pair_mask[:, :].unsqueeze(1).broadcast_to([P, CHUNKS, P]),
                                        ALU.mult).then_inc(states_ready, 1)
            for b in range(TB):
                for lv in range(len(SPLITS)):
                    n = b * len(SPLITS) + lv
                    pool.wait_ge(exp_done, n + 1)
                    if lv == 0:
                        pool.wait_ge(k_mm if b == 0 else attn_mm, 6 if b == 0 else 16 * b)
                    nc.gpsimd.tensor_tensor(k_lv[:, lv, :], expo[:, lv % 2, 1, :], k[:, b * BLK:(b + 1) * BLK],
                                            ALU.mult).then_inc(k_lv_ready, 1)
                pool.wait_ge(stats_taken, b + 1)
                step(nc.gpsimd.tensor_scalar(stats[:, :], stats[:, :], EPS, None, ALU.add))
                nc.gpsimd.tensor_tensor(stats[:, :], stats[:, :], minus_half[:, :].broadcast_to([P, 16]),
                                        ALU.pow).then_inc(rstd_ready, 1)

        @block.scalar
        def _(act):
            steps = [0]

            def step(instruction, wait=True):
                steps[0] += 1
                instruction.then_inc(act_step, 1)
                if wait:
                    act.wait_ge(act_step, steps[0])

            act.wait_ge(consts_loaded, 16 * N_CONSTS)
            for d in range(2):
                act.wait_ge(dve_step, 4 * d + 2)
                step(nc.scalar.activation(temp[:, d, :], temp[:, 2 + d, :], ACT.Abs))
                step(nc.scalar.activation(temp[:, d, :], temp[:, d, :], ACT.Exp, scale=-1.0))
                nc.scalar.activation(temp[:, d, :], temp[:, d, :], ACT.Ln, bias=1.0).then_inc(soft, 1)
            act.wait_ge(dve_step, 12)
            step(nc.scalar.activation(decay[:, 0, :], sums[0][:, :, CHUNK], ACT.Exp, scale=GATE_SCALE), False)
            step(nc.scalar.activation(decay[:, 1, :], sums[1][:, :, CHUNK], ACT.Exp, scale=GATE_SCALE), False)
            step(nc.scalar.activation(chunked(q_in[0][:, :]), sums[0][:, :, 1:], ACT.Exp, scale=GATE_SCALE), False)
            step(nc.scalar.activation(temp[:, 0, :], temp[:, 0, :], ACT.Exp, scale=GATE_SCALE), False)
            step(nc.scalar.activation(chunked(temp[:, 1, :]), sums[1][:, :, :CHUNK], ACT.Exp, scale=GATE_SCALE), False)
            step(nc.scalar.activation(q_in[1][:, :], temp[:, 3, :], ACT.Exp, scale=GATE_SCALE), False)
            for n in range(TILES // 2):
                act.wait_ge(v_mm, n + 1)
                if n == 0:
                    act.wait_ge(pool_set, 3)
                for half in range(2):
                    rows = slice(64 * half, 64 * half + 64)
                    nc.scalar.activation(v_half[rows, 2 * n:2 * n + 2, half, :],
                                         psum[rows, n % 2, :].rearrange("p (a e) -> p a e", a=2),
                                         ACT.Copy).then_inc(turned_out, 1)
            for n in range(6):
                act.wait_ge(k_mm, n + 1)
                nc.scalar.activation(k_turned[:, n // 3, 4 * (n % 3):4 * (n % 3) + 4, :],
                                     psum[:, 2 + n % 2, :].rearrange("p (a e) -> p a e", a=4),
                                     ACT.Copy).then_inc(turned_out, 1)
            for b in range(TB):
                for lv in range(len(SPLITS)):
                    n = b * len(SPLITS) + lv
                    act.wait_ge(expo_ready, 4 * n + 4)
                    nc.scalar.activation(expo[:, lv % 2, :, :], expo[:, lv % 2, :, :], ACT.Exp,
                                         scale=GATE_SCALE).then_inc(exp_done, 1)
                act.wait_ge(o_mm, 4 * b + 4)
                nc.scalar.activation(o_sq[:, :, :], psum[:, 4:6, :], ACT.Square, scale=DV ** -0.5).then_inc(sq_taken, 1)
                act.wait_ge(stats_mm, b + 1)
                nc.scalar.activation(stats[:, :], psum[:, 6, 0:16], ACT.Copy).then_inc(stats_taken, 1)
                act.wait_ge(rstd_ready, b + 1)
                nc.scalar.activation(o_sq[:, :, :].rearrange("p a (n e) -> p (a n) e", e=DV),
                                     stats[:, :].unsqueeze(2).broadcast_to([P, 16, DV]),
                                     ACT.Copy).then_inc(rstd_spread, 1)

        @block.vector
        def _(dve):
            steps = [0]

            def step(instruction, wait=True):
                steps[0] += 1
                instruction.then_inc(dve_step, 1)
                if wait:
                    dve.wait_ge(dve_step, steps[0])

            dve.wait_ge(consts_loaded, 16 * N_CONSTS)
            dve.wait_ge(pool_set, 1)
            step(nc.vector.tensor_scalar(q, q, GLA_Q_SCALE, None, ALU.mult), False)
            for d in range(2):
                dve.wait_ge(gate_mm, 3 * d + 3)
                step(nc.vector.tensor_scalar(temp[:, 2 + d, :].rearrange("p (a t) -> p a t", a=TB), psum[:, 3 * d:3 * d + 3, :],
                                             gate_bias[:, d:d + 1], None, ALU.add))
                dve.wait_ge(soft, d + 1)
                step(nc.vector.memset(sums[d][:, :, 0:1], 0.0))
                step(nc.vector.scalar_tensor_tensor(out=sums[d][:, :, 1:], in0=chunked(temp[:, 2 + d, :]), scalar=0.0,
                                                    in1=chunked(temp[:, d, :]), op0=ALU.min, op1=ALU.subtract))
                flat = sums[d][:, :, :].rearrange("p c t -> p (c t)")
                step(nc.vector.tensor_tensor_scan(flat, scan_keep[:, :], flat, 0.0, ALU.mult, ALU.add))
            end = lambda d: sums[d][:, :, CHUNK:].broadcast_to([P, CHUNKS, CHUNK])
            step(nc.vector.tensor_tensor(chunked(temp[:, 0, :]), end(FWD), sums[FWD][:, :, 1:], ALU.subtract))
            step(nc.vector.tensor_tensor(chunked(temp[:, 3, :]), end(BWD), sums[BWD][:, :, :CHUNK], ALU.subtract))
            assert steps[0] == 11
            step(nc.vector.memset(stats[:, 0:1], 0.0))
            dve.wait_ge(act_step, 10)
            for d in range(2):
                step(nc.vector.tensor_tensor(q_in[d][:, :], q_in[d][:, :], q, ALU.mult), False)
            for n in range(TILES):
                for d in range(2):
                    dve.wait_ge(kv_mm, 2 * n + d + 1)
                    tile = n if d == FWD else TILES - 1 - n
                    for part in range(2):
                        half = part if d == FWD else 1 - part
                        c = 2 * tile + half
                        to = c + 1 if d == FWD else c - 1
                        if c in ENDS[1 - d]:
                            nc.vector.engine_nop().then_inc(kv_used, 1)
                            continue
                        if n == 0 and part == 0:
                            dve.wait_ge(pool_set, 7)
                        else:
                            dve.wait_ge(kv_used, 4 * n + 2 * d + part if part else 4 * n + 2 * d - 2)
                        bank = 4 + (2 * n + d) % 4
                        nc.vector.scalar_tensor_tensor(
                            out=state[:, d, to, :], in0=state[:, d, c, :], scalar=decay[:, d, c:c + 1],
                            in1=psum[:, bank, half * P:half * P + P],
                            op0=ALU.mult, op1=ALU.add).then_inc(kv_used, 1)
            for b in range(TB):
                t = slice(b * BLK, (b + 1) * BLK)
                dve.wait_ge(gate_loaded, 16 * b + 16)
                dve.wait_ge(pool_mm, b + 1)
                for u in range(2):
                    ins = nc.vector.scalar_tensor_tensor(out=z[:, Z_U + u, t], in0=psum[:, u, :],
                                                         scalar=pool_scale[:, u:u + 1], in1=gate[:, u, :],
                                                         op0=ALU.mult, op1=ALU.mult)
                ins.then_inc(pool_out, 1)
            for b in range(TB):
                t = slice(b * BLK, (b + 1) * BLK)
                for lv, h in enumerate(SPLITS):
                    n = b * len(SPLITS) + lv
                    def part(ap, half, shift):
                        ap = ap[:, b * GROUP:(b + 1) * GROUP, shift:shift + CHUNK]
                        return ap.rearrange("p c (n a h) -> p c n a h", a=2, h=h)[:, :, :, half, :]

                    def bound(ap):
                        ap = ap[:, b * GROUP:(b + 1) * GROUP, 0:CHUNK]
                        ap = ap.rearrange("p c (n a h) -> p c n a h", a=2, h=h)[:, :, :, 1, 0:1]
                        return ap.broadcast_to([P, GROUP, CHUNK // (2 * h), h])

                    def to(qk, half):
                        ap = expo[:, lv % 2, qk, :].rearrange("p (c n a h) -> p c n a h", c=GROUP, a=2, h=h)
                        return ap[:, :, :, half, :]

                    if n >= 2:
                        dve.wait_ge(q_lv_ready, n - 1)
                        dve.wait_ge(k_lv_ready, n - 1)
                    if lv == 0 and b:
                        dve.wait_ge(mixed, b)
                    for out, a, c in ((to(0, 1), part(sums[FWD], 1, 1), bound(sums[FWD])),
                                      (to(0, 0), bound(sums[BWD]), part(sums[BWD], 0, 0)),
                                      (to(1, 0), bound(sums[FWD]), part(sums[FWD], 0, 1)),
                                      (to(1, 1), part(sums[BWD], 1, 0), bound(sums[BWD]))):
                        nc.vector.tensor_tensor(out, a, c, ALU.subtract).then_inc(expo_ready, 1)
                    dve.wait_ge(exp_done, n + 1)
                    if lv == 0:
                        dve.wait_ge(k_mm if b == 0 else attn_mm, 6 if b == 0 else 16 * b)
                    nc.vector.tensor_tensor(q_lv[:, lv, :], expo[:, lv % 2, 0, :], q[:, t], ALU.mult).then_inc(q_lv_ready, 1)
                for tt in range(4):
                    for head in range(HEADS):
                        n = 16 * b + 4 * tt + head
                        dve.wait_ge(attn_mm, n + 1)
                        if n >= 2:
                            dve.wait_ge(attn_ready, n - 1)
                        nc.vector.tensor_tensor(weighted[:, n % 2, :], psum[:, head, 0:LEVELS * CHUNK],
                                                level_mask[:, :], ALU.mult).then_inc(attn_read, 1)
                        dve.wait_ge(attn_read, n + 1)
                        if head == 0 and n >= 8:
                            dve.wait_ge(o_mm, n // 4 - 1)
                        nc.vector.tensor_reduce(attn[:, tt % 2, head, :],
                                                weighted[:, n % 2, :].rearrange("p (l i) -> p i l", l=LEVELS),
                                                AX_X, ALU.add).then_inc(attn_ready, 1)
                dve.wait_ge(sq_taken, b + 1)
                nc.vector.tensor_copy(o, psum[:, 4:6, :]).then_inc(o_taken, 1)
                dve.wait_ge(o_taken, 2 * b + 1)
                dve.wait_ge(gate_loaded, 16 * (TB + b) + 16)
                nc.vector.scalar_tensor_tensor(out=o, in0=o, scalar=gla_gain[:, 0:1], in1=gate[:, :, :],
                                               op0=ALU.mult, op1=ALU.mult).then_inc(o_taken, 1)
                dve.wait_ge(o_taken, 2 * b + 2)
                dve.wait_ge(spread_mm, b + 1)
                nc.vector.tensor_tensor(z[:, Z_V:Z_V + 2, t], o, psum[:, 4:6, :], ALU.mult).then_inc(mixed, 1)

        @block.tensor
        def _(pe):
            pe.wait_ge(consts_loaded, 16 * N_CONSTS)
            for d in range(2):
                for tb in range(TB):
                    rows = slice(2 * DK, 3 * DK)
                    nc.tensor.matmul(psum[:, 3 * d + tb, :], gate_up[rows, d, :], z[rows, Z_LR, tb * BLK:(tb + 1) * BLK],
                                     start=True, stop=True).then_inc(gate_mm, 1)
            pe.wait_ge(soft, 2)
            pe.wait_ge(dve_step, 9)
            for n in range(TILES // 2):
                if n >= 2:
                    pe.wait_ge(turned_out, 2 * n - 2)
                for a in range(4):
                    t = (2 * n + a // 2) * P
                    mm = nc.tensor.transpose(psum[:, n % 2, a * P:(a + 1) * P], z[:, Z_V + a % 2, t:t + P], ident[:, :])
                mm.then_inc(v_mm, 1)
            for n in range(6):
                if n % 3 == 0:
                    pe.wait_ge(k_scaled, n // 3 + 1)
                if n >= 2:
                    pe.wait_ge(turned_out, TILES + n - 1)
                for a in range(4):
                    t = (4 * (n % 3) + a) * P
                    mm = nc.tensor.transpose(psum[:, 2 + n % 2, a * P:(a + 1) * P], temp[:, n // 3, t:t + P], ident[:, :])
                mm.then_inc(k_mm, 1)
            pe.wait_ge(turned_out, TILES + 6)
            for n in range(TILES):
                for d in range(2):
                    i = 2 * n + d
                    if i >= 4:
                        pe.wait_ge(kv_used, 2 * (i - 4) + 2)
                    tile = n if d == FWD else TILES - 1 - n
                    for pair in range(2):
                        rows = slice(64 * pair, 64 * pair + 64)
                        mm = nc.tensor.matmul(psum[rows, 4 + i % 4, 0:2 * P],
                                              k_turned[:, d, tile, rows],
                                              v_half[:, tile, :, pair * P:(pair + 1) * P],
                                              start=True, stop=True)
                    mm.then_inc(kv_mm, 1)
            for b in range(TB):
                if b:
                    pe.wait_ge(pool_out, b)
                for u in range(2):
                    mm = nc.tensor.matmul(psum[:, u, :], w_pool[:, u, :], z[:, Z_U + u, b * BLK:(b + 1) * BLK],
                                          start=True, stop=True)
                mm.then_inc(pool_mm, 1)
            pe.wait_ge(states_ready, 2)
            pe.wait_ge(pool_out, TB)

            def out_tile(b, tt):
                tile = 4 * b + tt
                pe.wait_ge(attn_ready, 4 * tile + 4)
                if tt == 0 and b:
                    pe.wait_ge(mixed, b)
                for half in range(2):
                    c = 2 * tile + half
                    t = slice(c * CHUNK, (c + 1) * CHUNK)
                    cols = slice(tt * P + half * CHUNK, tt * P + half * CHUNK + CHUNK)
                    for pair in range(2):
                        group = []
                        for head in (2 * pair, 2 * pair + 1):
                            rows = slice(64 * (head % 2), 64 * (head % 2) + 64)
                            mm = nc.tensor.matmul(psum[rows, 4 + pair, cols], v_half[:, tile, half, head * DV:(head + 1) * DV],
                                                  attn[:, tt % 2, head, :], start=True, stop=False, skip_group_check=True)
                        rows = slice(64 * pair, 64 * pair + 64)
                        dirs = [d for d in range(2) if c not in ENDS[d]]
                        for d in dirs:
                            mm = nc.tensor.matmul(psum[:, 4 + pair, cols], state[rows, d, c, :], q_in[d][rows, t],
                                                  start=False, stop=(d == dirs[-1]), skip_group_check=True)
                mm.then_inc(o_mm, 1)

            for b in range(TB):
                for tt in range(4):
                    tile = 4 * b + tt
                    for head in range(HEADS):
                        n = 4 * tile + head
                        if n >= HEADS:
                            pe.wait_ge(attn_read, n - HEADS + 1)
                        rows = slice(DK * head, DK * head + DK)
                        for lv in range(LEVELS):
                            if head == 0 and tt == 0 and lv < len(SPLITS):
                                pe.wait_ge(k_lv_ready, b * len(SPLITS) + lv + 1)
                                pe.wait_ge(q_lv_ready, b * len(SPLITS) + lv + 1)
                            for half in range(2):
                                t = (tt * P + half * CHUNK) if lv < len(SPLITS) else tile * P + half * CHUNK
                                t = slice(t, t + CHUNK)
                                ks, qs = (k_lv[rows, lv, t], q_lv[rows, lv, t]) if lv < len(SPLITS) else (k[rows, t], q[rows, t])
                                mm = nc.tensor.matmul(psum[64 * half:64 * half + 64, head, lv * CHUNK:(lv + 1) * CHUNK],
                                                      ks, qs, start=True, stop=True)
                        mm.then_inc(attn_mm, 1)
                    if tt:
                        out_tile(b, tt - 1)
                out_tile(b, 3)
                pe.wait_ge(sq_taken, b + 1)
                for tt in range(4):
                    for pair in range(2):
                        n = pair * 4 + tt
                        mm = nc.tensor.matmul(psum[:, 6, 2 * n:2 * n + 2], o_sq[:, pair, tt * P:(tt + 1) * P],
                                              head_ones[:, :], start=True, stop=True)
                mm.then_inc(stats_mm, 1)
                pe.wait_ge(rstd_spread, b + 1)
                pe.wait_ge(o_taken, 2 * b + 1)
                for pair in range(2):
                    for tt in range(4):
                        mm = nc.tensor.matmul(psum[:, 4 + pair, tt * P:(tt + 1) * P],
                                              o_sq[:, pair, tt * P:(tt + 1) * P], ident[:, :], start=True, stop=True)
                mm.then_inc(spread_mm, 1)


class Semaphores:

    def __init__(self, nc, stack):
        self.nc, self.stack = nc, stack

    def semaphore(self, name):
        return self.stack.enter_context(self.nc.semaphore(name))


NOPE, ROPE = 128, 64
HALF_ROPE = ROPE // 2
MLA_SCALE = (NOPE + ROPE) ** -0.5
UQ_TILES = HEADS + 2


def product(nc, out, a_hi, a_lo, b_hi, b_lo, first=True, last=True):
    nc.tensor.matmul(out, a_hi, b_hi, start=first, stop=False)
    nc.tensor.matmul(out, a_hi, b_lo, start=False, stop=False)
    return nc.tensor.matmul(out, a_lo, b_hi, start=False, stop=last)


def phase_mla_prepare(nc, cx, dram, rope_dram, v_dram, z, psum, ident, keep):
    with ExitStack() as mem:
        sem = cx.semaphore
        sb = Region(nc, keep.next_at)
        w_v = sb("p_w_v", [P, HEADS * P])
        w_v_hi = sb("p_w_v_hi", [P, HEADS * P], F32R)
        w_v_lo = sb("p_w_v_lo", [P, HEADS * P], F32R)
        w_rope_hi = sb("p_w_rope_hi", [P, 2, 2, P], F32R)
        w_rope_lo = sb("p_w_rope_lo", [P, 2, 2, P], F32R)
        cos = sb("p_cos", [P, NT])
        sin = sb("p_sin", [P, NT])
        big = sb("p_big", [P, NT])
        k_swapped = sb("p_k_swapped", [ROPE, NT])
        turned = [sb(f"p_turned{n}", [P, BLK]) for n in range(4)]
        rope_half = {(n, part): sb(f"p_rope{n}{part}", [P, NT], F32R) for n in range(2) for part in ("hi", "lo")}
        v_stage = {part: sb(f"p_v_{part}", [P, 2, BLK], F32R) for part in ("hi", "lo")}
        ones = sb("p_ones", [P, 1])
        minus_half = sb("p_minus_half", [P, 1])
        mean_sq = sb("p_mean_sq", [P, 2 * TILES])
        q_gain = sb("p_q_gain", [P, 2])
        kv_gain = sb("p_kv_gain", [P, 1])

        consts_loaded = sem("p_consts_loaded")
        swapped = sem("p_swapped")
        ones_set = sem("p_ones_set")
        sq_ready = sem("p_sq_ready")
        sq_mm = sem("p_sq_mm")
        mean_ready = sem("p_mean_ready")
        pool_step = sem("p_pool_step")
        rstd_ready = sem("p_rstd_ready")
        spread_ready = sem("p_spread_ready")
        spread_mm = sem("p_spread_mm")
        ckv_ready = sem("p_ckv_ready")
        hi_ready = sem("p_hi_ready")
        lo_ready = sem("p_lo_ready")
        dve_step = sem("p_dve_step")
        k_rope_hi = sem("p_k_rope_hi")
        k_stacked = sem("p_k_stacked")
        rope_mm = sem("p_rope_mm")
        rope_read = sem("p_rope_read")
        rope_turned = sem("p_rope_turned")
        rope_lo = sem("p_rope_lo")
        rope_stored = sem("p_rope_stored")
        v_mm = sem("p_v_mm")
        v_hi_ready = sem("p_v_hi_ready")
        v_lo_ready = sem("p_v_lo_ready")
        v_stored = [sem(f"p_v_stored{n}") for n in range(2)]
        cq, ckv = z[:, Z_CQ:Z_CQ + 2, :], z[:, Z_CKV, :]

        block = mem.enter_context(nc.Block())

        @block.sync
        def _(sp):
            for to, of in ((keep.w_uq[:, :, :, :], dram["w_uq"]), (keep.w_uk[:, :, :], dram["w_uk"]),
                           (w_v[:, :], dram["w_uv"]), (cos[:, :], dram["rope_cos"]), (sin[:, :], dram["rope_sin"]),
                           (q_gain[:, :], dram["q_gain"]), (kv_gain[:, :], dram["kv_gain"])):
                sp.dma_start(to, of).then_inc(consts_loaded, 16)
            sp.dma_start(k_swapped[0:HALF_ROPE, :], z[HALF_ROPE:ROPE, Z_LR, :]).then_inc(swapped, 16)
            sp.dma_start(k_swapped[HALF_ROPE:ROPE, :], z[0:HALF_ROPE, Z_LR, :]).then_inc(swapped, 16)
            sp.wait_ge(k_rope_hi, 1)
            sp.dma_start(keep.k_rope[ROPE:P, :].bitcast(F32), keep.k_rope[0:ROPE, :].bitcast(F32)).then_inc(k_stacked, 16)
            for n in range(4):
                part, half = ("hi", "lo")[n // 2], n % 2
                sp.wait_ge(rope_read if part == "hi" else rope_lo, 2 * TB - 1 + half)
                sp.dma_start(rope_dram[:, n * HALF_ROPE:(n + 1) * HALF_ROPE, :],
                             rope_half[half, part][:, :].bitcast(F32)).then_inc(rope_stored, 16)
            for t in range(TILES):
                sp.wait_ge(v_lo_ready, t + 1)
                for n, part in enumerate(("hi", "lo")):
                    sp.dma_start(v_dram[n, :, :, t, :].rearrange("h p d -> p h d"),
                                 v_stage[part][:, t % 2, :].bitcast(F32).rearrange("p (h d) -> p h d", h=HEADS))\
                      .then_inc(v_stored[t % 2], 16)
            sp.wait_ge(rope_stored, 64)
            sp.wait_ge(k_stacked, 16)
            for n in range(2):
                sp.wait_ge(v_stored[n], 32 * TILES // 2)

        @block.gpsimd
        def _(pool):
            nc.gpsimd.memset(ones[:, :], 1.0).then_inc(ones_set, 1)
            nc.gpsimd.memset(minus_half[:, :], -0.5).then_inc(ones_set, 1)
            pool.wait_ge(ones_set, 2)
            pool.wait_ge(mean_ready, 1)
            nc.gpsimd.tensor_scalar(mean_sq[:, :], mean_sq[:, :], EPS, None, ALU.add).then_inc(pool_step, 1)
            pool.wait_ge(pool_step, 1)
            nc.gpsimd.tensor_tensor(mean_sq[:, :], mean_sq[:, :], minus_half[:, :].broadcast_to([P, 2 * TILES]),
                                    ALU.pow).then_inc(pool_step, 1)
            pool.wait_ge(pool_step, 2)
            nc.gpsimd.tensor_scalar(keep.q_scale[:, :], mean_sq[:, 0:TILES], MLA_SCALE, None, ALU.mult)\
              .then_inc(rstd_ready, 1)

        @block.scalar
        def _(act):
            act.wait_ge(consts_loaded, 16 * 7)
            for n, (source, width) in enumerate(((cq[:, 0, :], 256), (cq[:, 1, :], 256), (ckv, 128))):
                if n:
                    act.wait_ge(sq_mm, n)
                nc.scalar.activation(big[:, :], source, ACT.Square, scale=width ** -0.5).then_inc(sq_ready, 1)
            for n, (out, source) in enumerate(((w_v_hi[:, :], w_v[:, :]), (w_rope_hi[:, :, :, :], keep.w_uq[:, HEADS:, :, :]))):
                nc.scalar.activation(out, source, ACT.Copy).then_inc(hi_ready, 1)
            for n in range(2):
                nc.scalar.activation(keep.cq_hi[:, n, :], cq[:, n, :], ACT.Copy, scale=q_gain[:, n:n + 1]).then_inc(hi_ready, 1)
            act.wait_ge(dve_step, 4)
            nc.scalar.activation(keep.k_rope[0:ROPE, :], k_swapped[:, :], ACT.Copy).then_inc(k_rope_hi, 1)
            act.wait_ge(sq_mm, 3)
            nc.scalar.activation(mean_sq[:, :], psum[:, 7, 0:2 * TILES], ACT.Copy).then_inc(mean_ready, 1)
            act.wait_ge(rstd_ready, 1)
            nc.scalar.activation(big[:, :].rearrange("p (a b) -> p a b", b=P),
                                 mean_sq[:, TILES:].unsqueeze(2).broadcast_to([P, TILES, P]), ACT.Copy)\
              .then_inc(spread_ready, 1)
            for tb in range(TB):
                t = slice(tb * BLK, (tb + 1) * BLK)
                act.wait_ge(rope_turned, 2 * tb + 2)
                for n in range(2):
                    nc.scalar.activation(rope_half[n, "hi"][:, t], turned[2 * n][:, :], ACT.Copy).then_inc(rope_read, 1)
            act.wait_ge(ckv_ready, 1)
            nc.scalar.activation(keep.ckv_hi[:, :], big[:, :], ACT.Copy).then_inc(hi_ready, 1)
            for t in range(TILES):
                act.wait_ge(v_mm, t + 1)
                if t >= 2:
                    act.wait_ge(v_stored[t % 2], 32 * (t // 2))
                nc.scalar.activation(v_stage["hi"][:, t % 2, :], psum[:, 4 + t % 2, :], ACT.Copy).then_inc(v_hi_ready, 1)

        @block.vector
        def _(dve):
            steps = [0]

            def step(instruction):
                steps[0] += 1
                instruction.then_inc(dve_step, 1)
                dve.wait_ge(dve_step, steps[0])

            dve.wait_ge(consts_loaded, 16 * 7)
            dve.wait_ge(swapped, 32)
            k_raw = z[0:ROPE, Z_LR, :]
            step(nc.vector.tensor_tensor(k_swapped[:, :], k_swapped[:, :], sin[0:ROPE, :], ALU.mult))
            step(nc.vector.tensor_tensor(k_raw, k_raw, cos[0:ROPE, :], ALU.mult))
            for n, op in enumerate((ALU.subtract, ALU.add)):
                rows = slice(n * HALF_ROPE, (n + 1) * HALF_ROPE)
                step(nc.vector.tensor_tensor(k_swapped[rows, :], z[rows, Z_LR, :], k_swapped[rows, :], op))
            dve.wait_ge(k_rope_hi, 1)
            step(nc.vector.tensor_tensor(keep.k_rope_lo[:, :], k_swapped[:, :], keep.k_rope[0:ROPE, :].bitcast(F32),
                                         ALU.subtract))
            dve.wait_ge(hi_ready, 1)
            nc.vector.tensor_tensor(w_v_lo[:, :], w_v[:, :], w_v_hi[:, :].bitcast(F32), ALU.subtract).then_inc(lo_ready, 1)
            dve.wait_ge(hi_ready, 2)
            nc.vector.tensor_tensor(w_rope_lo[:, :, :, :], keep.w_uq[:, HEADS:, :, :], w_rope_hi[:, :, :, :].bitcast(F32),
                                    ALU.subtract).then_inc(lo_ready, 1)
            for n in range(2):
                dve.wait_ge(hi_ready, 3 + n)
                nc.vector.scalar_tensor_tensor(out=keep.cq_lo[:, n, :], in0=cq[:, n, :], scalar=q_gain[:, n:n + 1],
                                               in1=keep.cq_hi[:, n, :].bitcast(F32), op0=ALU.mult, op1=ALU.subtract)\
                  .then_inc(lo_ready, 1)
            for tb in range(TB):
                t = slice(tb * BLK, (tb + 1) * BLK)
                one, two = psum[:, 2 * (tb % 2), :], psum[:, 2 * (tb % 2) + 1, :]
                dve.wait_ge(rope_mm, tb + 1)
                if tb:
                    dve.wait_ge(rope_lo, tb * 2)
                    dve.wait_ge(rope_read, 2 * tb)
                step(nc.vector.tensor_tensor(turned[0][:, :], one, cos[:, t], ALU.mult))
                step(nc.vector.tensor_tensor(turned[1][:, :], two, sin[:, t], ALU.mult))
                step(nc.vector.tensor_tensor(turned[2][:, :], two, cos[:, t], ALU.mult))
                step(nc.vector.tensor_tensor(turned[3][:, :], one, sin[:, t], ALU.mult))
                for n, op in enumerate((ALU.subtract, ALU.add)):
                    nc.vector.tensor_tensor(turned[2 * n][:, :], turned[2 * n][:, :], turned[2 * n + 1][:, :], op)\
                      .then_inc(rope_turned, 1)
                for n in range(2):
                    dve.wait_ge(rope_read, 2 * tb + n + 1)
                    nc.vector.tensor_tensor(rope_half[n, "lo"][:, t], turned[2 * n][:, :],
                                            rope_half[n, "hi"][:, t].bitcast(F32), ALU.subtract).then_inc(rope_lo, 1)
            dve.wait_ge(spread_mm, 1)
            nc.vector.scalar_tensor_tensor(out=big[:, :].rearrange("p (a t) -> p a t", a=TB),
                                           in0=ckv.rearrange("p (a t) -> p a t", a=TB), scalar=kv_gain[:, 0:1],
                                           in1=psum[:, 4:7, :], op0=ALU.mult, op1=ALU.mult).then_inc(ckv_ready, 1)
            dve.wait_ge(hi_ready, 5)
            nc.vector.tensor_tensor(keep.ckv_lo[:, :], big[:, :], keep.ckv_hi[:, :].bitcast(F32), ALU.subtract)\
              .then_inc(lo_ready, 1)
            for t in range(TILES):
                dve.wait_ge(v_hi_ready, t + 1)
                nc.vector.tensor_tensor(v_stage["lo"][:, t % 2, :], psum[:, 4 + t % 2, :],
                                        v_stage["hi"][:, t % 2, :].bitcast(F32), ALU.subtract).then_inc(v_lo_ready, 1)

        @block.tensor
        def _(pe):
            pe.wait_ge(ones_set, 2)
            for n in range(3):
                pe.wait_ge(sq_ready, n + 1)
                for t in range(TILES):
                    col = t if n < 2 else TILES + t
                    mm = nc.tensor.matmul(psum[:, 7, col:col + 1], big[:, t * P:(t + 1) * P], ones[:, :],
                                          start=(n == 0 and t == 0), stop=(n == 2 and t == TILES - 1),
                                          skip_group_check=True)
                mm.then_inc(sq_mm, 1)
            pe.wait_ge(lo_ready, 4)
            for tb in range(TB):
                t = slice(tb * BLK, (tb + 1) * BLK)
                if tb == 2:
                    pe.wait_ge(rope_turned, 2)
                for n in range(2):
                    for k in range(2):
                        mm = product(nc, psum[:, 2 * (tb % 2) + n, :], w_rope_hi[:, n, k, :], w_rope_lo[:, n, k, :],
                                     keep.cq_hi[:, k, t], keep.cq_lo[:, k, t], k == 0, k == 1)
                mm.then_inc(rope_mm, 1)
            pe.wait_ge(spread_ready, 1)
            for t in range(TILES):
                mm = nc.tensor.matmul(psum[:, 4 + t // 4, (t % 4) * P:(t % 4 + 1) * P], big[:, t * P:(t + 1) * P],
                                      ident[:, :], start=True, stop=True)
            mm.then_inc(spread_mm, 1)
            pe.wait_ge(lo_ready, 5)
            for t in range(TILES):
                if t >= 2:
                    pe.wait_ge(v_lo_ready, t - 1)
                tok = slice(t * P, (t + 1) * P)
                product(nc, psum[:, 4 + t % 2, :], keep.ckv_hi[:, tok], keep.ckv_lo[:, tok],
                        w_v_hi[:, :], w_v_lo[:, :]).then_inc(v_mm, 1)


class MlaKeep:

    def __init__(self, nc):
        low = Region(nc, Z_AT, Z_Q * NT * 4 + 2 * NT * 4)
        high = Region(nc, MLA_AT)
        self.mixed = high("mla_mixed", [P, HEADS, NT])
        self.cq_hi = high("mla_cq_hi", [P, 2, NT], F32R)
        self.cq_lo = high("mla_cq_lo", [P, 2, NT], F32R)
        self.ckv_hi = high("mla_ckv_hi", [P, NT], F32R)
        self.ckv_lo = high("mla_ckv_lo", [P, NT], F32R)
        self.w_uq = high("mla_w_uq", [P, UQ_TILES, 2, P])
        self.w_uk = high("mla_w_uk", [P, HEADS, P])
        self.q_scale = high("mla_q_scale", [P, TILES])
        self.next_at = high.at
        low.at = Z_Q * NT * 4
        self.k_rope = low("mla_k_rope", [P, NT], F32R)
        self.k_rope_lo = low("mla_k_rope_lo", [ROPE, NT], F32R)
        self.low_free = Region(nc, Z_AT, Z_Q * NT * 4)


SEQ_TILES = tuple((t0 // P, n // P) for t0, n in SEQS)
QUERY_TILES = [(f + n, f, count) for f, count in SEQ_TILES for n in range(count)]
LAG = 2
SLOTS = 3
PROJ = 2 * TB


def phase_mla_attend(nc, cx, rope_dram, v_dram, gates_dram, psum, ident, keep):
    with ExitStack() as mem:
        sem = cx.semaphore
        sb = Region(nc, keep.next_at)
        q_rope = keep.low_free("a_q_rope", [P, NT], F32R)
        q_hi = sb("a_q_hi", [P, NT], F32R)
        q_lo = sb("a_q_lo", [P, NT], F32R)
        k_hi = sb("a_k_hi", [P, NT], F32R)
        k_lo = sb("a_k_lo", [P, NT], F32R)
        v_hi = sb("a_v_hi", [P, TILES, P], F32R)
        v_lo = sb("a_v_lo", [P, TILES, P], F32R)
        wq_hi = sb("a_wq_hi", [P, 2, P], F32R)
        wq_lo = sb("a_wq_lo", [P, 2, P], F32R)
        wk_hi = sb("a_wk_hi", [P, P], F32R)
        wk_lo = sb("a_wk_lo", [P, P], F32R)
        turned_hi = sb("a_turned_hi", [P, KT, BLK], F32R)
        turned_lo = sb("a_turned_lo", [P, KT, BLK], F32R)
        top = sb("a_top", [P, TILES])
        bias = sb("a_bias", [P, TILES])
        total = sb("a_total", [P, TILES])
        share = sb("a_share", [P, TILES])
        latents = Region(nc, Z_CQ * NT * 4, AFTER_Z)
        gate = latents("a_gate", [P, NT])
        weights = latents("a_weights", [P, SLOTS, 1024])

        rope_loaded = sem("a_rope_loaded")
        v_loaded = sem("a_v_loaded")
        gate_loaded = sem("a_gate_loaded")
        w_hi_ready = sem("a_w_hi_ready")
        w_lo_ready = sem("a_w_lo_ready")
        proj_done = sem("a_proj_done")
        proj_hi = sem("a_proj_hi")
        proj_lo = sem("a_proj_lo")
        scores_done = sem("a_scores_done")
        top_ready = sem("a_top_ready")
        bias_ready = sem("a_bias_ready")
        exp_done = sem("a_exp_done")
        share_ready = sem("a_share_ready")
        weights_ready = sem("a_weights_ready")
        turned = sem("a_turned")
        turned_hi_ready = sem("a_turned_hi_ready")
        turned_lo_ready = sem("a_turned_lo_ready")
        values_done = sem("a_values_done")
        values_out = sem("a_values_out")

        HALVES = sum(count // 4 for _, _, count in QUERY_TILES)
        half_at = [sum(count // 4 for _, _, count in QUERY_TILES[:g]) for g in range(TILES)]
        BLOCKS = TB

        block = mem.enter_context(nc.Block())

        @block.sync
        def _(sp):
            with sp.Fori(0, HEADS) as h:
                sp.wait_ge(scores_done, TILES * h + 1)
                sp.dma_start(q_rope[:, :].bitcast(F32), rope_dram[bass.ds(h, 1), :, :].rearrange("a p t -> (a p) t"))\
                  .then_inc(rope_loaded, 16)
                sp.wait_ge(values_done, BLOCKS * h + 1)
                for n, v in enumerate((v_hi, v_lo)):
                    sp.dma_start(v[:, :, :].bitcast(F32), v_dram[n, bass.ds(h, 1), :, :, :].rearrange("a p t d -> (a p) t d"))\
                      .then_inc(v_loaded, 16)
                sp.wait_ge(values_out, BLOCKS * h + 1)
                sp.dma_start(gate[:, :], gates_dram[bass.ds(h, 1), :, :].rearrange("a p t -> (a p) t"))\
                  .then_inc(gate_loaded, 16)

        @block.scalar
        def _(act):
            def take_hi(h, g):
                for n in range(QUERY_TILES[g][2] // 4):
                    i = HALVES * h + half_at[g] + n
                    act.wait_ge(turned, i + 1)
                    if g % 4 == 0 and n == 0:
                        act.wait_ge(values_done, BLOCKS * h + g // 4 + 1)
                    nc.scalar.activation(turned_hi[:, 4 * n:4 * n + 4, (g % 4) * P:(g % 4 + 1) * P],
                                         psum[:, 4 + (half_at[g] + n) % 2, :].rearrange("p (k q) -> p k q", k=4),
                                         ACT.Copy).then_inc(turned_hi_ready, 1)

            with act.Fori(0, HEADS) as h:
                act.wait_ge(proj_done, PROJ * h + 1)
                nc.scalar.activation(wq_hi[:, :, :], keep.w_uq[:, bass.ds(h, 1), :, :].rearrange("p a k d -> p (a k) d"),
                                     ACT.Copy).then_inc(w_hi_ready, 1)
                nc.scalar.activation(wk_hi[:, :], keep.w_uk[:, bass.ds(h, 1), :].rearrange("p a d -> p (a d)"),
                                     ACT.Copy).then_inc(w_hi_ready, 1)
                for n in range(PROJ):
                    out = (q_hi if n < TB else k_hi)[:, (n % TB) * BLK:(n % TB + 1) * BLK]
                    act.wait_ge(proj_done, PROJ * h + n + 2)
                    nc.scalar.activation(out, psum[:, n, :], ACT.Copy).then_inc(proj_hi, 1)
                for g in range(TILES + LAG):
                    if g < TILES:
                        _, _, count = QUERY_TILES[g]
                        banks = slice(2 * (g % 2), 2 * (g % 2) + count // 4)
                        w = weights[:, g % SLOTS, 0:count * P]
                        act.wait_ge(bias_ready, TILES * h + g + 1)
                        if g >= SLOTS:
                            act.wait_ge(turned, HALVES * h + half_at[g - SLOTS + 1])
                        nc.scalar.activation(w.rearrange("p (a k) -> p a k", k=BLK), psum[:, banks, :], ACT.Exp,
                                             bias=bias[:, g:g + 1], scale=keep.q_scale[:, g:g + 1],
                                             accum_out=total[:, g:g + 1]).then_inc(exp_done, 1)
                    if g >= LAG:
                        take_hi(h, g - LAG)
                    if g < TILES:
                        act.wait_ge(share_ready, TILES * h + g + 1)
                        nc.scalar.activation(w, w, ACT.Copy, scale=share[:, g:g + 1]).then_inc(weights_ready, 1)

        @block.vector
        def _(dve):
            def take_lo(h, g):
                for n in range(QUERY_TILES[g][2] // 4):
                    dve.wait_ge(turned_hi_ready, HALVES * h + half_at[g] + n + 1)
                    at = (slice(None), slice(4 * n, 4 * n + 4), slice((g % 4) * P, (g % 4 + 1) * P))
                    nc.vector.tensor_tensor(turned_lo[at], psum[:, 4 + (half_at[g] + n) % 2, :].rearrange("p (k q) -> p k q", k=4),
                                            turned_hi[at].bitcast(F32), ALU.subtract).then_inc(turned_lo_ready, 1)

            def gather(h, b):
                t = slice(b * BLK, (b + 1) * BLK)
                if b == 0:
                    dve.wait_ge(gate_loaded, 16 * h + 16)
                dve.wait_ge(values_done, BLOCKS * h + b + 2)
                nc.vector.tensor_tensor(keep.mixed[:, bass.ds(h, 1), t].rearrange("p a t -> p (a t)"), psum[:, 6, :],
                                        gate[:, t], ALU.mult).then_inc(values_out, 1)

            dve.engine_nop().then_inc(values_out, 1)
            with dve.Fori(0, HEADS) as h:
                dve.wait_ge(w_hi_ready, 2 * h + 1)
                nc.vector.tensor_tensor(wq_lo[:, :, :], keep.w_uq[:, bass.ds(h, 1), :, :].rearrange("p a k d -> p (a k) d"),
                                        wq_hi[:, :, :].bitcast(F32), ALU.subtract).then_inc(w_lo_ready, 1)
                dve.wait_ge(w_hi_ready, 2 * h + 2)
                nc.vector.tensor_tensor(wk_lo[:, :], keep.w_uk[:, bass.ds(h, 1), :].rearrange("p a d -> p (a d)"),
                                        wk_hi[:, :].bitcast(F32), ALU.subtract).then_inc(w_lo_ready, 1)
                for n in range(PROJ):
                    t = slice((n % TB) * BLK, (n % TB + 1) * BLK)
                    hi, lo = (q_hi, q_lo) if n < TB else (k_hi, k_lo)
                    dve.wait_ge(proj_hi, PROJ * h + n + 1)
                    nc.vector.tensor_tensor(lo[:, t], psum[:, n, :], hi[:, t].bitcast(F32), ALU.subtract).then_inc(proj_lo, 1)
                for g in range(TILES + LAG):
                    if g < TILES:
                        _, _, count = QUERY_TILES[g]
                        banks = slice(2 * (g % 2), 2 * (g % 2) + count // 4)
                        dve.wait_ge(scores_done, TILES * h + g + 2)
                        nc.vector.tensor_reduce(top[:, g:g + 1], psum[:, banks, :], mybir.AxisListType.XY, ALU.max)\
                          .then_inc(top_ready, 1)
                        dve.wait_ge(top_ready, TILES * h + g + 1)
                        nc.vector.tensor_scalar(bias[:, g:g + 1], top[:, g:g + 1], keep.q_scale[:, g:g + 1], -1.0,
                                                ALU.mult, ALU.mult).then_inc(bias_ready, 1)
                        dve.wait_ge(exp_done, TILES * h + g + 1)
                        nc.vector.reciprocal(share[:, g:g + 1], total[:, g:g + 1]).then_inc(share_ready, 1)
                    if g >= LAG:
                        take_lo(h, g - LAG)
                    if g >= LAG + 4 and (g - LAG) % 4 == 0:
                        gather(h, (g - LAG) // 4 - 1)
                gather(h, BLOCKS - 1)

        @block.tensor
        def _(pe):
            def scores(h, g):
                tile, first, count = QUERY_TILES[g]
                q = slice(tile * P, (tile + 1) * P)
                for n in range(count // 4):
                    if g >= 2 and n == 0:
                        pe.wait_ge(exp_done, TILES * h + g - 1)
                    k = slice(first * P + n * BLK, first * P + (n + 1) * BLK)
                    out = psum[:, 2 * (g % 2) + n, :]
                    product(nc, out, q_hi[:, q], q_lo[:, q], k_hi[:, k], k_lo[:, k], True, False)
                    nc.tensor.matmul(out, q_rope[:, q], keep.k_rope[:, k], start=False, stop=False)
                    mm = nc.tensor.matmul(out, q_rope[0:ROPE, q], keep.k_rope_lo[:, k], start=False, stop=True)
                mm.then_inc(scores_done, 1)

            def turn(h, g):
                pe.wait_ge(weights_ready, TILES * h + g + 1)
                for n in range(QUERY_TILES[g][2] // 4):
                    i = half_at[g] + n
                    if i >= 2:
                        pe.wait_ge(turned_lo_ready, HALVES * h + i - 1)
                    for k in range(4):
                        mm = nc.tensor.transpose(psum[:, 4 + i % 2, k * P:(k + 1) * P],
                                                 weights[:, g % SLOTS, (4 * n + k) * P:(4 * n + k + 1) * P], ident[:, :])
                    mm.then_inc(turned, 1)

            def values(h, b):
                _, first, count = QUERY_TILES[4 * b]
                g = 4 * b + 3
                if b == 0:
                    pe.wait_ge(v_loaded, 32 * h + 32)
                else:
                    pe.wait_ge(values_out, BLOCKS * h + b + 1)
                pe.wait_ge(turned_lo_ready, HALVES * h + half_at[g] + count // 4)
                for k in range(count):
                    mm = product(nc, psum[:, 6, :], v_hi[:, first + k, :], v_lo[:, first + k, :],
                                 turned_hi[:, k, :], turned_lo[:, k, :], k == 0, k == count - 1)
                mm.then_inc(values_done, 1)

            for done in (scores_done, values_done, proj_done):
                pe.nop().then_inc(done, 1)
            with pe.Fori(0, HEADS) as h:
                for n in range(PROJ):
                    t = slice((n % TB) * BLK, (n % TB + 1) * BLK)
                    if n == 0:
                        pe.wait_ge(w_lo_ready, 2 * h + 1)
                    if n == TB:
                        pe.wait_ge(w_lo_ready, 2 * h + 2)
                    if n < TB:
                        for k in range(2):
                            mm = product(nc, psum[:, n, :], wq_hi[:, k, :], wq_lo[:, k, :],
                                         keep.cq_hi[:, k, t], keep.cq_lo[:, k, t], k == 0, k == 1)
                    else:
                        mm = product(nc, psum[:, n, :], wk_hi[:, :], wk_lo[:, :], keep.ckv_hi[:, t], keep.ckv_lo[:, t])
                    mm.then_inc(proj_done, 1)
                pe.wait_ge(rope_loaded, 16 * h + 16)
                pe.wait_ge(proj_lo, PROJ * h + PROJ)
                for g in range(TILES + LAG):
                    if g < TILES:
                        scores(h, g)
                    if g >= LAG + 4 and (g - LAG) % 4 == 0:
                        values(h, (g - LAG) // 4 - 1)
                    if g >= LAG:
                        turn(h, g - LAG)
                values(h, BLOCKS - 1)


def phase_output(nc, cx, w_out_dram, final_g_dram, x_dram, y_dram, z, mla_mixed, psum):
    with ExitStack() as mem:
        sem = cx.semaphore
        sb = Region(nc, MLA_AT + MLA_BYTES)
        w_hi = sb("o_w_hi", [P, KT, D_MODEL], F32R)
        w_lo = sb("o_w_lo", [P, KT, D_MODEL], F32R)
        m_hi = sb("o_m_hi", [P, 2, KT, P], F32R)
        m_lo = sb("o_m_lo", [P, 2, KT, P], F32R)
        y = sb("o_y", [P, 2, D_MODEL])
        g_row = sb("o_g_row", [P, D_MODEL])
        low = Region(nc, Z_AT, Z_V * NT * 4)
        w_raw = low("o_w_raw", [P, 2, D_MODEL])
        x_in = low("o_x_in", [P, 2, D_MODEL])
        squares = Region(nc, Z_CQ * NT * 4, AFTER_Z)("o_squares", [P, 2, D_MODEL])
        mean_sq = sb("o_mean_sq", [P, 2])
        rstd = sb("o_rstd", [P, 2])
        eps = sb("o_eps", [P, 1])
        minus_half = sb("o_minus_half", [P, 1])

        g_loaded = sem("o_g_loaded")
        w_loaded = [sem(f"o_w_loaded{n}") for n in range(2)]
        x_loaded = [sem(f"o_x_loaded{n}") for n in range(2)]
        y_stored = [sem(f"o_y_stored{n}") for n in range(2)]
        w_hi_ready = sem("o_w_hi_ready")
        w_lo_ready = sem("o_w_lo_ready")
        half_set = sem("o_half_set")
        m_hi_ready = sem("o_m_hi_ready")
        m_lo_ready = sem("o_m_lo_ready")
        out_mm = sem("o_out_mm")
        summed = sem("o_summed")
        squares_done = sem("o_squares_done")
        eps_added = sem("o_eps_added")
        rstd_ready = sem("o_rstd_ready")
        y_ready = sem("o_y_ready")
        pairs = TILES // 2

        block = mem.enter_context(nc.Block())

        @block.sync
        def _(sp):
            sp.dma_start(g_row[:, :], final_g_dram.partition_broadcast(P)).then_inc(g_loaded, 16)
            for s in range(2):
                sp.dma_start(x_in[:, s, :], x_dram[rows_of(s), :]).then_inc(x_loaded[s], 16)
            for k in range(KT):
                if k >= 2:
                    sp.wait_ge(w_lo_ready, k - 1)
                sp.dma_start(w_raw[:, k % 2, :], w_out_dram[k * P:(k + 1) * P, :]).then_inc(w_loaded[k % 2], 16)
            with sp.Fori(1, pairs) as i:
                for s in range(2):
                    sp.wait_ge(summed, 4 * i + 2 * s - 2)
                    sp.dma_start(x_in[:, s, :], x_dram[rows_of(2 * i + s), :]).then_inc(x_loaded[s], 16)

        @block.gpsimd
        def _(pool):
            for k in range(KT):
                pool.wait_ge(w_hi_ready, k + 1)
                nc.gpsimd.tensor_tensor(w_lo[:, k, :], w_raw[:, k % 2, :], w_hi[:, k, :].bitcast(F32), ALU.subtract)\
                  .then_inc(w_lo_ready, 1)
            nc.gpsimd.memset(minus_half[:, :], -0.5).then_inc(half_set, 1)
            nc.gpsimd.memset(eps[:, :], EPS).then_inc(half_set, 1)
            pool.wait_ge(half_set, 2)
            with pool.Fori(0, pairs) as i:
                for s in range(2):
                    n, slot = 2 * i + s, slice(s, s + 1)
                    pool.wait_ge(squares_done, n + 1)
                    nc.gpsimd.tensor_tensor(rstd[:, slot], mean_sq[:, slot], eps[:, :], ALU.add).then_inc(eps_added, 1)
                    pool.wait_ge(eps_added, n + 1)
                    nc.gpsimd.tensor_tensor(rstd[:, slot], rstd[:, slot], minus_half[:, :],
                                            ALU.pow).then_inc(rstd_ready, 1)

        @block.scalar
        def _(act):
            def take_hi(i, s, first):
                n = 2 * i + s
                if not first:
                    act.wait_ge(out_mm, 2 * n - 2)
                nc.scalar.activation(m_hi[:, s, 0:4, :], mla_mixed[:, :, rows_of(n)], ACT.Copy).then_inc(m_hi_ready, 1)
                nc.scalar.activation(m_hi[:, s, 4:8, :], z[:, Z_V:Z_V + 4, rows_of(n)], ACT.Copy).then_inc(m_hi_ready, 1)

            def finish(i, s, first):
                n = 2 * i + s
                if not first:
                    act.wait_ge(eps_added, n - 1)
                act.wait_ge(summed, 2 * n + 2)
                nc.scalar.activation(squares[:, s, :], y[:, s, :], ACT.Square, scale=D_MODEL ** -0.5,
                                     accum_out=mean_sq[:, s:s + 1]).then_inc(squares_done, 1)

            def store(i, s):
                n = 2 * i + s
                act.wait_ge(y_ready, n + 1)
                act.dma_start(y_dram[rows_of(n), :], y[:, s, :]).then_inc(y_stored[s], 16)

            for k in range(KT):
                act.wait_ge(w_loaded[k % 2], 16 * (k // 2) + 16)
                nc.scalar.activation(w_hi[:, k, :], w_raw[:, k % 2, :], ACT.Copy).then_inc(w_hi_ready, 1)
                if k < 2:
                    take_hi(0, k, True)
            finish(0, 0, True)
            take_hi(1, 0, False)
            store(0, 0)
            finish(0, 1, True)
            take_hi(1, 1, False)
            store(0, 1)
            with act.Fori(1, pairs - 1) as i:
                for s in range(2):
                    finish(i, s, False)
                    take_hi(i + 1, s, False)
                    store(i, s)
            for s in range(2):
                finish(pairs - 1, s, False)
                store(pairs - 1, s)
            for s in range(2):
                act.wait_ge(y_stored[s], 16 * pairs)

        @block.vector
        def _(dve):
            def take_lo(i, s):
                n = 2 * i + s
                dve.wait_ge(m_hi_ready, 2 * n + 1)
                nc.vector.tensor_tensor(m_lo[:, s, 0:4, :], mla_mixed[:, :, rows_of(n)], m_hi[:, s, 0:4, :].bitcast(F32),
                                        ALU.subtract).then_inc(m_lo_ready, 1)
                dve.wait_ge(m_hi_ready, 2 * n + 2)
                nc.vector.tensor_tensor(m_lo[:, s, 4:8, :], z[:, Z_V:Z_V + 4, rows_of(n)], m_hi[:, s, 4:8, :].bitcast(F32),
                                        ALU.subtract).then_inc(m_lo_ready, 1)

            def add_input(i, s, first):
                n = 2 * i + s
                dve.wait_ge(x_loaded[s], 16 * i + 16)
                if not first:
                    dve.wait_ge(y_stored[s], 16 * i)
                for half in range(2):
                    dve.wait_ge(out_mm, 2 * n + half + 1)
                    cols = slice(half * BLK, (half + 1) * BLK)
                    nc.vector.tensor_tensor(y[:, s, cols], psum[:, 2 * s + half, :], x_in[:, s, cols], ALU.add)\
                      .then_inc(summed, 1)

            def normalise(i, s):
                n = 2 * i + s
                dve.wait_ge(rstd_ready, n + 1)
                nc.vector.scalar_tensor_tensor(out=y[:, s, :], in0=y[:, s, :], scalar=rstd[:, s:s + 1],
                                               in1=g_row[:, :], op0=ALU.mult, op1=ALU.mult).then_inc(y_ready, 1)

            dve.wait_ge(g_loaded, 16)
            take_lo(0, 0)
            take_lo(0, 1)
            for s in range(2):
                add_input(0, s, True)
                take_lo(1, s)
                normalise(0, s)
            with dve.Fori(1, pairs - 1) as i:
                for s in range(2):
                    add_input(i, s, False)
                    take_lo(i + 1, s)
                    normalise(i, s)
            for s in range(2):
                add_input(pairs - 1, s, False)
                normalise(pairs - 1, s)

        @block.tensor
        def _(pe):
            def multiply(i, s, first):
                n = 2 * i + s
                pe.wait_ge(m_lo_ready, 2 * n + 2)
                for half in range(2):
                    if not first:
                        pe.wait_ge(summed, 2 * n - 3 + half)
                    cols = slice(half * BLK, (half + 1) * BLK)
                    for k in range(KT):
                        if first and s == 0 and half == 0:
                            pe.wait_ge(w_lo_ready, k + 1)
                        mm = product(nc, psum[:, 2 * s + half, :], m_hi[:, s, k, :], m_lo[:, s, k, :],
                                     w_hi[:, k, cols], w_lo[:, k, cols], k == 0, k == KT - 1)
                    mm.then_inc(out_mm, 1)

            for s in range(2):
                multiply(0, s, True)
            with pe.Fori(1, pairs) as i:
                for s in range(2):
                    multiply(i, s, False)


class Semaphores:

    def __init__(self, nc, stack):
        self.nc, self.stack = nc, stack

    def semaphore(self, name):
        return self.stack.enter_context(self.nc.semaphore(name))


def hymba_encoder_kernel(nc, dram, y_dram):
    with ExitStack() as whole:
        cx = Semaphores(nc, whole)
        scratch = lambda name, shape, dt: nc.dram_tensor(name, shape, dt, kind="Internal").ap()
        psum = whole.enter_context(nc.psum_tensor("psum", [P, 8, BLK], F32))
        ident = Region(nc, SBUF_BYTES, SBUF_BYTES + P * 4)("ident", [P, P])
        gates_dram = scratch("gates_scratch", (Z_GATES, P, NT), F32)
        rope_dram = scratch("rope_scratch", (HEADS, P, NT), F32)
        v_dram = scratch("v_scratch", (2, HEADS, P, TILES, P), F32)
        z = Region(nc, Z_AT)("z", [P, Z_PLAIN, NT])
        h_mem = Region(nc, AFTER_Z)
        h_hi = h_mem("h_hi", [P, KT, NT], F32R)
        h_lo = h_mem("h_lo", [P, KT, NT], F32R)
        phase_norm_transpose(nc, cx, dram["x"], dram["norm_g"], h_hi, h_lo, ident, psum, dram["ident"])
        phase_project(nc, cx, dram["w_z"], gates_dram, dram["pool_edge"], dram["pool_mean"], h_hi, h_lo, z, psum)
        phase_gla(nc, cx, dram, gates_dram, z, psum, ident)
        keep = MlaKeep(nc)
        phase_mla_prepare(nc, cx, dram, rope_dram, v_dram, z, psum, ident, keep)
        phase_mla_attend(nc, cx, rope_dram, v_dram, gates_dram, psum, ident, keep)
        phase_output(nc, cx, dram["w_out"], dram["final_norm_g"], dram["x"], y_dram, z, keep.mixed, psum)


POOL_WINDOWS = (2, 4, 8, 16)
ROPE_BASE = 10000.0
IN_COLUMNS = ((Z_LR, 384, 448, 0), (Z_LR, 1984, 2016, 64),
              (Z_Q, 1472, 1600, 0), (Z_K, 1600, 1728, 0), (Z_V, 1728, 1984, 0),
              (Z_U, 960, 1216, 0), (Z_CQ, 0, 256, 0), (Z_CKV, 256, 384, 0),
              (Z_PLAIN, 448, 960, 0), (Z_PLAIN + 4, 1216, 1472, 0), (Z_PLAIN + 6, 2016, 2272, 0))


def shape_tables(np):
    lane = np.arange(P)
    edge = np.ones((P, 2, 2, POOL_PAD), np.float32)
    mean = np.zeros((P, 2), np.float32)
    for g, w in enumerate(POOL_WINDOWS):
        u, rows = g // 2, slice(64 * (g % 2), 64 * (g % 2) + 64)
        mean[rows, u] = 1.0 / w
        for t in range(POOL_PAD):
            edge[rows, u, 0, t] = w / (w // 2 + min(t, w // 2))
            edge[rows, u, 1, t] = w / (w // 2 + min(POOL_PAD - t, w // 2))
    level_mask = np.zeros((P, LEVELS, CHUNK), np.float32)
    for key in range(P):
        for query in range(CHUNK):
            apart = (key % CHUNK) ^ query
            level_mask[key, LEVELS - 1 - apart.bit_length(), query] = 1.0 if apart else 2.0
    inverse = (1.0 / ROPE_BASE ** (np.arange(0, ROPE, 2, dtype=np.float32) / np.float32(ROPE))).astype(np.float32)
    position = np.concatenate([np.arange(n) for _, n in SEQS]).astype(np.float32)
    angle = inverse[:, None] * position[None]
    return {
        "ident": np.eye(P, dtype=np.float32),
        "pool_edge": edge,
        "pool_mean": mean,
        "level_mask": level_mask.reshape(P, LEVELS * CHUNK),
        "pair_mask": ((lane[:, None] // DK) % 2 == lane[None, :] // DV).astype(np.float32),
        "head_ones": (lane[:, None] // DV == np.arange(2)).astype(np.float32),
        "rope_cos": np.tile(np.cos(angle), (HEADS, 1)),
        "rope_sin": np.tile(np.sin(angle), (HEADS, 1)),
    }


def lay_out(np, inp):
    w_in = inp["w_in"][0]
    columns = np.zeros((D_MODEL, Z_TILES * P), np.float32)
    for tile, start, end, at in IN_COLUMNS:
        columns[:, tile * P + at:tile * P + at + end - start] = w_in[:, start:end]
    gate_up = np.zeros((32, 2, P), np.float32)
    gate_up[:16, FWD], gate_up[16:, BWD] = inp["gk_up_fwd"][0], inp["gk_up_bwd"][0]
    w_pool = np.zeros((P, 2, P), np.float32)
    for g in range(len(POOL_WINDOWS)):
        at = 64 * (g % 2)
        w_pool[at:at + 64, g // 2, at:at + 64] = inp["w_pool"][0, g]
    w_uq = inp["w_uq"][0].reshape(2 * P, HEADS, NOPE + ROPE)
    parts = (w_uq[:, :, :NOPE], w_uq[:, :, NOPE:NOPE + HALF_ROPE], w_uq[:, :, NOPE + HALF_ROPE:])
    w_uq = np.concatenate([part.reshape(2 * P, -1) for part in parts], 1)
    w_ukv = inp["w_ukv"][0].reshape(P, HEADS, 2 * P)
    w_out = inp["w_out"][0]
    return {
        "x": np.concatenate([inp["x_prompt"][0], inp["x_sample"][0]], 0),
        "w_z": columns.reshape(KT, P, Z_TILES, P).transpose(2, 1, 0, 3).reshape(Z_TILES, P, D_MODEL),
        "norm_g": inp["norm_g"][0],
        "gate_up": gate_up,
        "gate_bias": np.stack([inp["gk_bias_fwd"][0], inp["gk_bias_bwd"][0]], 1),
        "gla_gain": np.tile(inp["gla_norm_g"][0], 2)[:, None],
        "w_pool": w_pool,
        "pool_scale": inp["pool_scale"][0].reshape(2, P).T,
        "w_uq": w_uq.reshape(2, P, UQ_TILES, P).transpose(1, 2, 0, 3),
        "w_uk": w_ukv[:, :, :NOPE],
        "w_uv": w_ukv[:, :, NOPE:].reshape(P, HEADS * P),
        "q_gain": inp["q_norm_g"][0].reshape(2, P).T,
        "kv_gain": inp["kv_norm_g"][0][:, None],
        "w_out": np.concatenate([w_out[:512], w_out[768:], w_out[512:768]], 0),
        "final_norm_g": inp["final_norm_g"],
    }


def kernel(**inputs):
    import numpy as np
    import concourse.bacc as bacc
    from concourse.bass_utils import run_bass_kernel_spmd

    inputs = {name: np.asarray(a) for name, a in inputs.items()}
    nc = bacc.Bacc("TRN2", target_bir_lowering=False, num_devices=1)
    arrays, dram = {}, {}
    for name, a in {**lay_out(np, inputs), **shape_tables(np)}.items():
        a = np.ascontiguousarray(a)
        arrays[f"in_{name}_dram"] = a
        dram[name] = nc.dram_tensor(f"in_{name}_dram", a.shape, mybir.dt.from_np(a.dtype), kind="ExternalInput").ap()
    y = nc.dram_tensor("out_dram", (NT, D_MODEL), F32, kind="ExternalOutput").ap()
    hymba_encoder_kernel(nc, dram, y)
    got = run_bass_kernel_spmd(nc, [arrays], core_ids=[0]).results[0]["out_dram"]
    return tuple(got[start:start + n][None] for start, n in SEQS)
```

```python
from contextlib import ExitStack

import concourse.bass as bass
from concourse import mybir

F32 = mybir.dt.float32
F32R = mybir.dt.float32r
ALU = mybir.AluOpType
ACT = mybir.ActivationFunctionType
AX_X = mybir.AxisListType.X

P = 128
D_MODEL = 1024
SEQS = ((0, 1024), (1024, 512))
NT = 1536
TILES = NT // P
KT = D_MODEL // P
BLK = 512
TB = NT // BLK
EPS = 1e-6

Z_LR, Z_Q, Z_K, Z_V, Z_U, Z_CQ, Z_CKV = 0, 1, 2, 3, 5, 7, 9
Z_PLAIN = 10
Z_GATES = 8
Z_TILES = Z_PLAIN + Z_GATES


def rows_of(t):
    return bass.ds(t * P, P)


Z_AT = 0
AFTER_Z = Z_PLAIN * NT * 4
H_BYTES = KT * NT * 4
MLA_AT = AFTER_Z
MLA_BYTES = 4 * NT * 4
SBUF_BYTES = 212224


class Region:

    def __init__(self, nc, at, end=SBUF_BYTES):
        self.nc, self.at, self.end = nc, at, end
        self.base = -(-nc.sbuf_base // 64) * 64

    def __call__(self, name, shape, dtype=F32):
        size = 4
        for n in shape[1:]:
            size *= n
        at, self.at = self.at, self.at + -(-size // 32) * 32
        assert self.at <= self.end, (name, self.at, self.end)
        return self.nc.alloc_sbuf_tensor_at(name, shape, dtype, offset=self.base + at)


def product(nc, out, a_hi, a_lo, b_hi, b_lo, first=True, last=True):
    nc.tensor.matmul(out, a_hi, b_hi, start=first, stop=False)
    nc.tensor.matmul(out, a_hi, b_lo, start=False, stop=False)
    return nc.tensor.matmul(out, a_lo, b_hi, start=False, stop=last)


X_SLOTS = 4
EARLY_BLOCKS = ((0, 0), (1, 0), (0, 1), (1, 1), (0, 2), (1, 2))


POOL_PAD = 8
PADDED = NT + 2 * len(SEQS) * POOL_PAD
POOL_AT = (POOL_PAD, SEQS[0][1] + 3 * POOL_PAD)


def phase_project(nc, cx, dram, gates_dram, h_hi, h_lo, z, psum, ident):
    with ExitStack() as mem:
        sb = Region(nc, AFTER_Z + 2 * H_BYTES)
        sem = cx.semaphore
        w_raw = sb("z_w_raw", [P, 2, D_MODEL])
        w_hi = sb("z_w_hi", [P, 2, D_MODEL], F32R)
        w_lo = sb("z_w_lo", [P, 2, D_MODEL], F32R)
        gate = sb("z_gate", [P, 2, NT])
        sums = [sb(f"z_sums{n}", [P, PADDED]) for n in range(2)]
        pool_edge = sb("z_pool_edge", [P, 2, 2, POOL_PAD])
        pool_mean = sb("z_pool_mean", [P, 2])
        mean_sq = sb("n_mean_sq", [P, TILES])
        rstd = sb("n_rstd", [P, TILES])
        minus_half = sb("n_minus_half", [P, 1])
        eps = sb("n_eps", [P, 1])
        late_z = Region(nc, Z_U * NT * 4, AFTER_Z)
        x_in = late_z("n_x_in", [P, X_SLOTS, D_MODEL])
        x_norm = late_z("n_x_norm", [P, 2, D_MODEL])
        g_row = late_z("n_g_row", [P, D_MODEL])

        x_loaded = [sem(f"n_x_loaded{s}") for s in range(X_SLOTS)]
        g_loaded = sem("n_g_loaded")
        ident_loaded = sem("n_ident_loaded")
        half_set = sem("n_half_set")
        squares_done = sem("n_squares_done")
        eps_added = sem("n_eps_added")
        rstd_ready = sem("n_rstd_ready")
        norm_ready = sem("n_norm_ready")
        turned = sem("n_turned")
        hi_ready = sem("n_hi_ready")
        lo_ready = sem("n_lo_ready")
        w_loaded = [sem(f"z_w_loaded{s}") for s in range(2)]
        gate_stored = [sem(f"z_gate_stored{s}") for s in range(2)]
        w_hi_ready = sem("z_w_hi_ready")
        w_lo_ready = sem("z_w_lo_ready")
        z_done = sem("z_done")
        z_emptied = sem("z_emptied")
        pool_loaded = sem("z_pool_loaded")
        pool_step = sem("z_pool_step")
        pairs = Z_TILES // 2

        block = mem.enter_context(nc.Block())

        @block.sync
        def _(sp):
            def load_x(n):
                if n >= X_SLOTS:
                    sp.wait_ge(norm_ready, n - X_SLOTS + 1)
                sp.dma_start(x_in[:, n % X_SLOTS, :], dram["x"][n * P:(n + 1) * P, :]).then_inc(x_loaded[n % X_SLOTS], 16)

            def load_w(i, s, first):
                if not first:
                    sp.wait_ge(w_lo_ready, 2 * i + s - 1)
                sp.dma_start(w_raw[:, s, :], dram["w_z"][bass.ds(2 * i + s, 1), :, :].rearrange("a p n -> (a p) n"))\
                  .then_inc(w_loaded[s], 16)

            load_x(0)
            sp.dma_start(g_row[:, :], dram["norm_g"].partition_broadcast(P)).then_inc(g_loaded, 16)
            load_x(1)
            sp.dma_start(ident[:, :], dram["ident"]).then_inc(ident_loaded, 16)
            load_x(2)
            load_x(3)
            for s in range(2):
                load_w(0, s, True)
            for n in range(X_SLOTS, TILES):
                load_x(n)
            sp.dma_start(pool_edge[:, :, :, :], dram["pool_edge"]).then_inc(pool_loaded, 16)
            sp.dma_start(pool_mean[:, :], dram["pool_mean"]).then_inc(pool_loaded, 16)
            with sp.Fori(1, pairs) as i:
                for s in range(2):
                    load_w(i, s, False)

        @block.scalar
        def _(act):
            def square(n):
                act.wait_ge(x_loaded[n % X_SLOTS], 16 * (n // X_SLOTS) + 16)
                if n >= 2:
                    act.wait_ge(turned, 2 * n - 2)
                nc.scalar.activation(x_norm[:, n % 2, :], x_in[:, n % X_SLOTS, :], ACT.Square, scale=D_MODEL ** -0.5,
                                     accum_out=mean_sq[:, n:n + 1]).then_inc(squares_done, 1)

            def take_hi(n):
                for half in range(2):
                    act.wait_ge(turned, 2 * n + half + 1)
                    nc.scalar.activation(h_hi[:, 4 * half:4 * half + 4, n * P:(n + 1) * P],
                                         psum[:, 6 + half, :].rearrange("p (k t) -> p k t", k=4),
                                         ACT.Copy).then_inc(hi_ready, 1)

            def split_hi(i, s, first):
                act.wait_ge(w_loaded[s], 16 * i + 16)
                if not first:
                    act.wait_ge(z_done, TB * (2 * i + s) - TB)
                nc.scalar.activation(w_hi[:, s, :], w_raw[:, s, :], ACT.Copy).then_inc(w_hi_ready, 1)

            def empty(i, s, first=False):
                n = 2 * i + s
                for tb in range(TB):
                    act.wait_ge(z_done, 2 * tb + 1 if first else TB * n + tb + 1)
                    nc.scalar.activation(
                        z[:, bass.ds(n, 1), tb * BLK:(tb + 1) * BLK].rearrange("p a t -> p (a t)"),
                        psum[:, TB * s + tb, :], ACT.Copy).then_inc(z_emptied, 1)

            def empty_gate(i, s, first):
                n = 2 * i + s
                if not first:
                    act.wait_ge(gate_stored[s], 16 * i - 8 * Z_PLAIN)
                for tb in range(TB):
                    act.wait_ge(z_done, TB * n + tb + 1)
                    nc.scalar.activation(gate[:, s, tb * BLK:(tb + 1) * BLK], psum[:, TB * s + tb, :],
                                         ACT.Silu).then_inc(z_emptied, 1)
                act.wait_ge(z_emptied, TB * n + TB)
                act.dma_start(gates_dram[bass.ds(n - Z_PLAIN, 1), :, :].rearrange("a p t -> (a p) t"),
                              gate[:, s, :]).then_inc(gate_stored[s], 16)

            square(0)
            square(1)
            for n in range(TILES):
                take_hi(n)
                if n + 2 < TILES:
                    square(n + 2)
                if n in (1, 2):
                    split_hi(0, n - 1, True)
            empty(0, 0, True)
            with act.Fori(1, Z_PLAIN // 2) as i:
                split_hi(i, 0, False)
                empty(i - 1, 1)
                split_hi(i, 1, False)
                empty(i, 0)
            i = Z_PLAIN // 2
            split_hi(i, 0, False)
            empty(i - 1, 1)
            split_hi(i, 1, False)
            empty_gate(i, 0, True)
            split_hi(i + 1, 0, False)
            empty_gate(i, 1, True)
            split_hi(i + 1, 1, False)
            empty_gate(i + 1, 0, False)
            with act.Fori(Z_PLAIN // 2 + 2, pairs) as i:
                split_hi(i, 0, False)
                empty_gate(i - 1, 1, False)
                split_hi(i, 1, False)
                empty_gate(i, 0, False)
            empty_gate(pairs - 1, 1, False)
            for s in range(2):
                act.wait_ge(gate_stored[s], 8 * Z_GATES)

        @block.gpsimd
        def _(pool):
            def invert_root(n):
                pool.wait_ge(squares_done, n + 1)
                nc.gpsimd.tensor_tensor(rstd[:, n:n + 1], mean_sq[:, n:n + 1], eps[:, :], ALU.add).then_inc(eps_added, 1)
                pool.wait_ge(eps_added, n + 1)
                nc.gpsimd.tensor_tensor(rstd[:, n:n + 1], rstd[:, n:n + 1], minus_half[:, :], ALU.pow)\
                  .then_inc(rstd_ready, 1)

            def split_lo(i, s, first):
                pool.wait_ge(w_hi_ready, 2 * i + s + 1)
                if not first:
                    pool.wait_ge(z_done, TB * (2 * i + s) - TB)
                nc.gpsimd.tensor_tensor(w_lo[:, s, :], w_raw[:, s, :], w_hi[:, s, :].bitcast(F32),
                                        ALU.subtract).then_inc(w_lo_ready, 1)

            nc.gpsimd.memset(minus_half[:, :], -0.5).then_inc(half_set, 1)
            nc.gpsimd.memset(eps[:, :], EPS).then_inc(half_set, 1)
            pool.wait_ge(half_set, 2)
            for n in range(TILES):
                invert_root(n)
                if n in (4, 5):
                    split_lo(0, n - 4, True)
            with pool.Fori(1, pairs) as i:
                for s in range(2):
                    split_lo(i, s, False)

        @block.vector
        def _(dve):
            def normalise(n):
                dve.wait_ge(rstd_ready, n + 1)
                nc.vector.scalar_tensor_tensor(out=x_norm[:, n % 2, :], in0=x_in[:, n % X_SLOTS, :],
                                               scalar=rstd[:, n:n + 1], in1=g_row[:, :],
                                               op0=ALU.mult, op1=ALU.mult).then_inc(norm_ready, 1)

            def take_lo(n):
                for half in range(2):
                    dve.wait_ge(hi_ready, 2 * n + half + 1)
                    at = (slice(None), slice(4 * half, 4 * half + 4), slice(n * P, (n + 1) * P))
                    nc.vector.tensor_tensor(h_lo[at], psum[:, 6 + half, :].rearrange("p (k t) -> p k t", k=4),
                                            h_hi[at].bitcast(F32), ALU.subtract).then_inc(lo_ready, 1)

            dve.wait_ge(g_loaded, 16)
            normalise(0)
            for n in range(TILES):
                if n + 1 < TILES:
                    normalise(n + 1)
                take_lo(n)

            steps = [0]

            def step(instruction):
                steps[0] += 1
                instruction.then_inc(pool_step, 1)
                dve.wait_ge(pool_step, steps[0])

            even, odd = sums
            dve.wait_ge(pool_loaded, 32)
            dve.wait_ge(z_emptied, TB * (Z_U + 2))
            for u in range(2):
                step(nc.vector.memset(even[:, :], 0.0))
                step(nc.vector.memset(odd[:, :], 0.0))
                for (t0, n), at in zip(SEQS, POOL_AT):
                    step(nc.vector.tensor_copy(even[:, at:at + n], z[:, Z_U + u, t0:t0 + n]))
                upper = slice(64, P)
                step(nc.vector.tensor_tensor(odd[:, 1:], even[:, :-1], even[:, 1:], ALU.add))
                rows = upper if u == 0 else slice(0, P)
                step(nc.vector.tensor_tensor(even[rows, 1:-1], odd[rows, :-2], odd[rows, 2:], ALU.add))
                if u == 1:
                    step(nc.vector.tensor_tensor(odd[:, 2:-2], even[:, :-4], even[:, 4:], ALU.add))
                    step(nc.vector.tensor_tensor(even[upper, 4:-4], odd[upper, :-8], odd[upper, 8:], ALU.add))
                for rows, total in ((slice(0, 64), odd), (upper, even)):
                    for (t0, n), at in zip(SEQS, POOL_AT):
                        ends = total[rows, at:at + n].rearrange("p (a b) -> p a b", b=POOL_PAD)[:, ::n // POOL_PAD - 1, :]
                        step(nc.vector.tensor_tensor(ends, ends, pool_edge[rows, u, :, :], ALU.mult))
                        out = z[rows, Z_U + u, t0:t0 + n]
                        step(nc.vector.scalar_tensor_tensor(out=out, in0=total[rows, at:at + n],
                                                            scalar=pool_mean[rows, u:u + 1], in1=out,
                                                            op0=ALU.mult, op1=ALU.subtract))

        @block.tensor
        def _(pe):
            def turn(n):
                pe.wait_ge(norm_ready, n + 1)
                for half in range(2):
                    if n:
                        pe.wait_ge(lo_ready, 2 * n - 1 + half)
                    for k in range(4):
                        mm = nc.tensor.transpose(psum[:, 6 + half, k * P:(k + 1) * P],
                                                 x_norm[:, n % 2, (4 * half + k) * P:(4 * half + k + 1) * P],
                                                 ident[:, :])
                    mm.then_inc(turned, 1)

            def project_block(s, tb, tiles=()):
                t = slice(tb * BLK, (tb + 1) * BLK)
                for k in range(KT):
                    if k in (2, 5) and tiles:
                        turn(tiles[k == 5])
                    c = slice(k * P, (k + 1) * P)
                    mm = product(nc, psum[:, TB * s + tb, :], w_hi[:, s, c], w_lo[:, s, c],
                                 h_hi[:, k, t], h_lo[:, k, t], k == 0, k == KT - 1)
                mm.then_inc(z_done, 1)

            pe.wait_ge(ident_loaded, 16)
            for n in range(4):
                turn(n)
            for n, (s, tb) in enumerate(EARLY_BLOCKS):
                pe.wait_ge(w_lo_ready, s + 1)
                pe.wait_ge(lo_ready, 8 * tb + 8)
                project_block(s, tb, (2 * n + 4, 2 * n + 5) if 2 * n + 5 < TILES else ())
            with pe.Fori(1, pairs) as i:
                for s in range(2):
                    n = 2 * i + s
                    pe.wait_ge(w_lo_ready, n + 1)
                    for tb in range(TB):
                        pe.wait_ge(z_emptied, TB * n - 2 * TB + tb + 1)
                        project_block(s, tb)


CHUNK = 64
CHUNKS = NT // CHUNK
GROUP = BLK // CHUNK
SPLITS = (32, 16, 8, 4, 2, 1)
LEVELS = len(SPLITS) + 1
HEADS = 4
DK, DV = 32, 64
ENDS = tuple(t0 // CHUNK for t0, _ in SEQS), tuple((t0 + n) // CHUNK - 1 for t0, n in SEQS)
GLA_Q_SCALE = DK ** -0.5
GATE_SCALE = 1.0 / 16.0
FWD, BWD = 0, 1


def phase_gla(nc, cx, dram, gates_dram, z, psum, ident):
    with ExitStack() as mem:
        sb = Region(nc, AFTER_Z)
        sem = cx.semaphore
        gate_up = sb("g_gate_up", [P, 2, P])
        gate_bias = sb("g_gate_bias", [P, 2])
        scan_keep = sb("g_scan_keep", [P, CHUNKS * (CHUNK + 1)])
        level_mask = sb("g_level_mask", [P, LEVELS * CHUNK])
        pair_mask = sb("g_pair_mask", [P, P])
        head_ones = sb("g_head_ones", [P, 2])
        gla_gain = sb("g_gain", [P, 1])
        w_pool = sb("g_w_pool", [P, 2, P])
        pool_scale = sb("g_pool_scale", [P, 2])
        minus_half = sb("g_minus_half", [P, 1])
        sums = [sb(f"g_sums{d}", [P, CHUNKS, CHUNK + 1]) for d in range(2)]
        decay = sb("g_decay", [P, 2, CHUNKS])
        work = sb("g_work", [P, 4 * NT])
        q_in = [sb(f"g_q_in{d}", [P, NT]) for d in range(2)]
        k_turned = sb("g_k_turned", [P, 2, TILES, P])
        v_half = sb("g_v_half", [P, TILES, 2, HEADS * DV])
        state = sb("g_state", [P, 2, CHUNKS, P])
        expo = sb("g_expo", [P, 2, 2, BLK])
        weighted = sb("g_weighted", [P, 2, LEVELS * CHUNK])
        attn = sb("g_attn", [P, 2, HEADS, CHUNK])
        o_sq = sb("g_o_sq", [P, 2, BLK])
        stats = sb("g_stats", [P, 16])
        gate = sb("g_gate", [P, 2, BLK])

        temp = work[:, :].rearrange("p (a t) -> p a t", a=4)
        q_lv, k_lv = (work[:, n * 6 * BLK:(n + 1) * 6 * BLK].rearrange("p (l t) -> p l t", l=6) for n in range(2))
        o = expo[:, 0, :, :]

        consts_loaded = sem("g_consts_loaded")
        pool_set = sem("g_pool_set")
        gate_mm = sem("g_gate_mm")
        soft = sem("g_soft")
        dve_step = sem("g_dve_step")
        act_step = sem("g_act_step")
        pool_step = sem("g_pool_step")
        k_scaled = sem("g_k_scaled")
        v_mm = sem("g_v_mm")
        k_mm = sem("g_k_mm")
        turned_out = sem("g_turned_out")
        kv_mm = sem("g_kv_mm")
        kv_used = sem("g_kv_used")
        states_ready = sem("g_states_ready")
        expo_ready = sem("g_expo_ready")
        exp_done = sem("g_exp_done")
        q_lv_ready = sem("g_q_lv_ready")
        k_lv_ready = sem("g_k_lv_ready")
        attn_mm = sem("g_attn_mm")
        attn_read = sem("g_attn_read")
        attn_ready = sem("g_attn_ready")
        o_mm = sem("g_o_mm")
        o_taken = sem("g_o_taken")
        sq_taken = sem("g_sq_taken")
        stats_mm = sem("g_stats_mm")
        stats_taken = sem("g_stats_taken")
        rstd_ready = sem("g_rstd_ready")
        rstd_spread = sem("g_rstd_spread")
        spread_mm = sem("g_spread_mm")
        mixed = sem("g_mixed")
        gate_loaded = sem("g_gate_loaded")
        pool_mm = sem("g_pool_mm")
        pool_out = sem("g_pool_out")
        q, k = z[:, Z_Q, :], z[:, Z_K, :]
        chunked = lambda ap: ap.rearrange("p (c t) -> p c t", t=CHUNK)

        block = mem.enter_context(nc.Block())
        N_CONSTS = 8

        @block.sync
        def _(sp):
            sp.dma_start(gate_up[2 * DK:3 * DK, :, :], dram["gate_up"]).then_inc(consts_loaded, 16)
            sp.dma_start(gate_bias[:, :], dram["gate_bias"]).then_inc(consts_loaded, 16)
            sp.dma_start(level_mask[:, :], dram["level_mask"]).then_inc(consts_loaded, 16)
            sp.dma_start(pair_mask[:, :], dram["pair_mask"]).then_inc(consts_loaded, 16)
            sp.dma_start(head_ones[:, :], dram["head_ones"]).then_inc(consts_loaded, 16)
            sp.dma_start(gla_gain[:, :], dram["gla_gain"]).then_inc(consts_loaded, 16)
            sp.dma_start(w_pool[:, :, :], dram["w_pool"]).then_inc(consts_loaded, 16)
            sp.dma_start(pool_scale[:, :], dram["pool_scale"]).then_inc(consts_loaded, 16)
            for n in range(2 * TB):
                if n:
                    sp.wait_ge(pool_out if n <= TB else mixed, n if n <= TB else n - TB)
                row = 4 if n < TB else 6
                t = (n % TB) * BLK
                sp.dma_start(gate[:, :, :], gates_dram[row:row + 2, :, t:t + BLK].rearrange("a p t -> p a t"))\
                  .then_inc(gate_loaded, 16)

        @block.gpsimd
        def _(pool):
            steps = [0]

            def step(instruction):
                steps[0] += 1
                instruction.then_inc(pool_step, 1)
                pool.wait_ge(pool_step, steps[0])

            keep = scan_keep[:, :].rearrange("p (c t) -> p c t", t=CHUNK + 1)
            step(nc.gpsimd.memset(scan_keep[:, :], 1.0))
            nc.gpsimd.memset(keep[:, :, 0:1], 0.0).then_inc(pool_set, 1)
            nc.gpsimd.memset(minus_half[:, :], -0.5).then_inc(pool_set, 1)
            nc.gpsimd.memset(v_half[:, :, :, :], 0.0).then_inc(pool_set, 1)
            for d in range(2):
                for c in (ENDS[0] if d == FWD else ENDS[1]):
                    nc.gpsimd.memset(state[:, d, c, :], 0.0).then_inc(pool_set, 1)
            for d in range(2):
                pool.wait_ge(act_step, 8 + d)
                nc.gpsimd.tensor_tensor(temp[:, d, :], temp[:, d, :], k, ALU.mult).then_inc(k_scaled, 1)
            for d in range(2):
                pool.wait_ge(kv_used, 2 * CHUNKS)
                nc.gpsimd.tensor_tensor(state[:, d, :, :], state[:, d, :, :],
                                        pair_mask[:, :].unsqueeze(1).broadcast_to([P, CHUNKS, P]),
                                        ALU.mult).then_inc(states_ready, 1)
            for b in range(TB):
                for lv in range(len(SPLITS)):
                    n = b * len(SPLITS) + lv
                    pool.wait_ge(exp_done, n + 1)
                    if lv == 0:
                        pool.wait_ge(k_mm if b == 0 else attn_mm, 6 if b == 0 else 16 * b)
                    nc.gpsimd.tensor_tensor(k_lv[:, lv, :], expo[:, lv % 2, 1, :], k[:, b * BLK:(b + 1) * BLK],
                                            ALU.mult).then_inc(k_lv_ready, 1)
                pool.wait_ge(stats_taken, b + 1)
                step(nc.gpsimd.tensor_scalar(stats[:, :], stats[:, :], EPS, None, ALU.add))
                nc.gpsimd.tensor_tensor(stats[:, :], stats[:, :], minus_half[:, :].broadcast_to([P, 16]),
                                        ALU.pow).then_inc(rstd_ready, 1)

        @block.scalar
        def _(act):
            steps = [0]

            def step(instruction, wait=True):
                steps[0] += 1
                instruction.then_inc(act_step, 1)
                if wait:
                    act.wait_ge(act_step, steps[0])

            act.wait_ge(consts_loaded, 16 * N_CONSTS)
            for d in range(2):
                act.wait_ge(dve_step, 4 * d + 2)
                step(nc.scalar.activation(temp[:, d, :], temp[:, 2 + d, :], ACT.Abs))
                step(nc.scalar.activation(temp[:, d, :], temp[:, d, :], ACT.Exp, scale=-1.0))
                nc.scalar.activation(temp[:, d, :], temp[:, d, :], ACT.Ln, bias=1.0).then_inc(soft, 1)
            act.wait_ge(dve_step, 12)
            step(nc.scalar.activation(decay[:, 0, :], sums[0][:, :, CHUNK], ACT.Exp, scale=GATE_SCALE), False)
            step(nc.scalar.activation(decay[:, 1, :], sums[1][:, :, CHUNK], ACT.Exp, scale=GATE_SCALE), False)
            step(nc.scalar.activation(chunked(q_in[0][:, :]), sums[0][:, :, 1:], ACT.Exp, scale=GATE_SCALE), False)
            step(nc.scalar.activation(temp[:, 0, :], temp[:, 0, :], ACT.Exp, scale=GATE_SCALE), False)
            step(nc.scalar.activation(chunked(temp[:, 1, :]), sums[1][:, :, :CHUNK], ACT.Exp, scale=GATE_SCALE), False)
            step(nc.scalar.activation(q_in[1][:, :], temp[:, 3, :], ACT.Exp, scale=GATE_SCALE), False)
            for n in range(TILES // 2):
                act.wait_ge(v_mm, n + 1)
                if n == 0:
                    act.wait_ge(pool_set, 3)
                for half in range(2):
                    rows = slice(64 * half, 64 * half + 64)
                    nc.scalar.activation(v_half[rows, 2 * n:2 * n + 2, half, :],
                                         psum[rows, n % 2, :].rearrange("p (a e) -> p a e", a=2),
                                         ACT.Copy).then_inc(turned_out, 1)
            for n in range(6):
                act.wait_ge(k_mm, n + 1)
                nc.scalar.activation(k_turned[:, n // 3, 4 * (n % 3):4 * (n % 3) + 4, :],
                                     psum[:, 2 + n % 2, :].rearrange("p (a e) -> p a e", a=4),
                                     ACT.Copy).then_inc(turned_out, 1)
            for b in range(TB):
                for lv in range(len(SPLITS)):
                    n = b * len(SPLITS) + lv
                    act.wait_ge(expo_ready, 4 * n + 4)
                    nc.scalar.activation(expo[:, lv % 2, :, :], expo[:, lv % 2, :, :], ACT.Exp,
                                         scale=GATE_SCALE).then_inc(exp_done, 1)
                act.wait_ge(o_mm, 4 * b + 4)
                nc.scalar.activation(o_sq[:, :, :], psum[:, 4:6, :], ACT.Square, scale=DV ** -0.5).then_inc(sq_taken, 1)
                act.wait_ge(stats_mm, b + 1)
                nc.scalar.activation(stats[:, :], psum[:, 6, 0:16], ACT.Copy).then_inc(stats_taken, 1)
                act.wait_ge(rstd_ready, b + 1)
                nc.scalar.activation(o_sq[:, :, :].rearrange("p a (n e) -> p (a n) e", e=DV),
                                     stats[:, :].unsqueeze(2).broadcast_to([P, 16, DV]),
                                     ACT.Copy).then_inc(rstd_spread, 1)

        @block.vector
        def _(dve):
            steps = [0]

            def step(instruction, wait=True):
                steps[0] += 1
                instruction.then_inc(dve_step, 1)
                if wait:
                    dve.wait_ge(dve_step, steps[0])

            dve.wait_ge(consts_loaded, 16 * N_CONSTS)
            dve.wait_ge(pool_set, 1)
            step(nc.vector.tensor_scalar(q, q, GLA_Q_SCALE, None, ALU.mult), False)
            for d in range(2):
                dve.wait_ge(gate_mm, 3 * d + 3)
                step(nc.vector.tensor_scalar(temp[:, 2 + d, :].rearrange("p (a t) -> p a t", a=TB), psum[:, 3 * d:3 * d + 3, :],
                                             gate_bias[:, d:d + 1], None, ALU.add))
                dve.wait_ge(soft, d + 1)
                step(nc.vector.memset(sums[d][:, :, 0:1], 0.0))
                step(nc.vector.scalar_tensor_tensor(out=sums[d][:, :, 1:], in0=chunked(temp[:, 2 + d, :]), scalar=0.0,
                                                    in1=chunked(temp[:, d, :]), op0=ALU.min, op1=ALU.subtract))
                flat = sums[d][:, :, :].rearrange("p c t -> p (c t)")
                step(nc.vector.tensor_tensor_scan(flat, scan_keep[:, :], flat, 0.0, ALU.mult, ALU.add))
            end = lambda d: sums[d][:, :, CHUNK:].broadcast_to([P, CHUNKS, CHUNK])
            step(nc.vector.tensor_tensor(chunked(temp[:, 0, :]), end(FWD), sums[FWD][:, :, 1:], ALU.subtract))
            step(nc.vector.tensor_tensor(chunked(temp[:, 3, :]), end(BWD), sums[BWD][:, :, :CHUNK], ALU.subtract))
            assert steps[0] == 11
            step(nc.vector.memset(stats[:, 0:1], 0.0))
            dve.wait_ge(act_step, 10)
            for d in range(2):
                step(nc.vector.tensor_tensor(q_in[d][:, :], q_in[d][:, :], q, ALU.mult), False)
            for n in range(TILES):
                for d in range(2):
                    dve.wait_ge(kv_mm, 2 * n + d + 1)
                    tile = n if d == FWD else TILES - 1 - n
                    for part in range(2):
                        half = part if d == FWD else 1 - part
                        c = 2 * tile + half
                        to = c + 1 if d == FWD else c - 1
                        if c in ENDS[1 - d]:
                            nc.vector.engine_nop().then_inc(kv_used, 1)
                            continue
                        if n == 0 and part == 0:
                            dve.wait_ge(pool_set, 7)
                        else:
                            dve.wait_ge(kv_used, 4 * n + 2 * d + part if part else 4 * n + 2 * d - 2)
                        bank = 4 + (2 * n + d) % 4
                        nc.vector.scalar_tensor_tensor(
                            out=state[:, d, to, :], in0=state[:, d, c, :], scalar=decay[:, d, c:c + 1],
                            in1=psum[:, bank, half * P:half * P + P],
                            op0=ALU.mult, op1=ALU.add).then_inc(kv_used, 1)
            for b in range(TB):
                t = slice(b * BLK, (b + 1) * BLK)
                dve.wait_ge(gate_loaded, 16 * b + 16)
                dve.wait_ge(pool_mm, b + 1)
                for u in range(2):
                    ins = nc.vector.scalar_tensor_tensor(out=z[:, Z_U + u, t], in0=psum[:, u, :],
                                                         scalar=pool_scale[:, u:u + 1], in1=gate[:, u, :],
                                                         op0=ALU.mult, op1=ALU.mult)
                ins.then_inc(pool_out, 1)
            for b in range(TB):
                t = slice(b * BLK, (b + 1) * BLK)
                for lv, h in enumerate(SPLITS):
                    n = b * len(SPLITS) + lv
                    def part(ap, half, shift):
                        ap = ap[:, b * GROUP:(b + 1) * GROUP, shift:shift + CHUNK]
                        return ap.rearrange("p c (n a h) -> p c n a h", a=2, h=h)[:, :, :, half, :]

                    def bound(ap):
                        ap = ap[:, b * GROUP:(b + 1) * GROUP, 0:CHUNK]
                        ap = ap.rearrange("p c (n a h) -> p c n a h", a=2, h=h)[:, :, :, 1, 0:1]
                        return ap.broadcast_to([P, GROUP, CHUNK // (2 * h), h])

                    def to(qk, half):
                        ap = expo[:, lv % 2, qk, :].rearrange("p (c n a h) -> p c n a h", c=GROUP, a=2, h=h)
                        return ap[:, :, :, half, :]

                    if n >= 2:
                        dve.wait_ge(q_lv_ready, n - 1)
                        dve.wait_ge(k_lv_ready, n - 1)
                    if lv == 0 and b:
                        dve.wait_ge(mixed, b)
                    for out, a, c in ((to(0, 1), part(sums[FWD], 1, 1), bound(sums[FWD])),
                                      (to(0, 0), bound(sums[BWD]), part(sums[BWD], 0, 0)),
                                      (to(1, 0), bound(sums[FWD]), part(sums[FWD], 0, 1)),
                                      (to(1, 1), part(sums[BWD], 1, 0), bound(sums[BWD]))):
                        nc.vector.tensor_tensor(out, a, c, ALU.subtract).then_inc(expo_ready, 1)
                    dve.wait_ge(exp_done, n + 1)
                    if lv == 0:
                        dve.wait_ge(k_mm if b == 0 else attn_mm, 6 if b == 0 else 16 * b)
                    nc.vector.tensor_tensor(q_lv[:, lv, :], expo[:, lv % 2, 0, :], q[:, t], ALU.mult).then_inc(q_lv_ready, 1)
                for tt in range(4):
                    for head in range(HEADS):
                        n = 16 * b + 4 * tt + head
                        dve.wait_ge(attn_mm, n + 1)
                        if n >= 2:
                            dve.wait_ge(attn_ready, n - 1)
                        nc.vector.tensor_tensor(weighted[:, n % 2, :], psum[:, head, 0:LEVELS * CHUNK],
                                                level_mask[:, :], ALU.mult).then_inc(attn_read, 1)
                        dve.wait_ge(attn_read, n + 1)
                        if head == 0 and n >= 8:
                            dve.wait_ge(o_mm, n // 4 - 1)
                        nc.vector.tensor_reduce(attn[:, tt % 2, head, :],
                                                weighted[:, n % 2, :].rearrange("p (l i) -> p i l", l=LEVELS),
                                                AX_X, ALU.add).then_inc(attn_ready, 1)
                dve.wait_ge(sq_taken, b + 1)
                nc.vector.tensor_copy(o, psum[:, 4:6, :]).then_inc(o_taken, 1)
                dve.wait_ge(o_taken, 2 * b + 1)
                dve.wait_ge(gate_loaded, 16 * (TB + b) + 16)
                nc.vector.scalar_tensor_tensor(out=o, in0=o, scalar=gla_gain[:, 0:1], in1=gate[:, :, :],
                                               op0=ALU.mult, op1=ALU.mult).then_inc(o_taken, 1)
                dve.wait_ge(o_taken, 2 * b + 2)
                dve.wait_ge(spread_mm, b + 1)
                nc.vector.tensor_tensor(z[:, Z_V:Z_V + 2, t], o, psum[:, 4:6, :], ALU.mult).then_inc(mixed, 1)

        @block.tensor
        def _(pe):
            pe.wait_ge(consts_loaded, 16 * N_CONSTS)
            for d in range(2):
                for tb in range(TB):
                    rows = slice(2 * DK, 3 * DK)
                    nc.tensor.matmul(psum[:, 3 * d + tb, :], gate_up[rows, d, :], z[rows, Z_LR, tb * BLK:(tb + 1) * BLK],
                                     start=True, stop=True).then_inc(gate_mm, 1)
            pe.wait_ge(soft, 2)
            pe.wait_ge(dve_step, 9)
            for n in range(TILES // 2):
                if n >= 2:
                    pe.wait_ge(turned_out, 2 * n - 2)
                for a in range(4):
                    t = (2 * n + a // 2) * P
                    mm = nc.tensor.transpose(psum[:, n % 2, a * P:(a + 1) * P], z[:, Z_V + a % 2, t:t + P], ident[:, :])
                mm.then_inc(v_mm, 1)
            for n in range(6):
                if n % 3 == 0:
                    pe.wait_ge(k_scaled, n // 3 + 1)
                if n >= 2:
                    pe.wait_ge(turned_out, TILES + n - 1)
                for a in range(4):
                    t = (4 * (n % 3) + a) * P
                    mm = nc.tensor.transpose(psum[:, 2 + n % 2, a * P:(a + 1) * P], temp[:, n // 3, t:t + P], ident[:, :])
                mm.then_inc(k_mm, 1)
            pe.wait_ge(turned_out, TILES + 6)
            for n in range(TILES):
                for d in range(2):
                    i = 2 * n + d
                    if i >= 4:
                        pe.wait_ge(kv_used, 2 * (i - 4) + 2)
                    tile = n if d == FWD else TILES - 1 - n
                    for pair in range(2):
                        rows = slice(64 * pair, 64 * pair + 64)
                        mm = nc.tensor.matmul(psum[rows, 4 + i % 4, 0:2 * P],
                                              k_turned[:, d, tile, rows],
                                              v_half[:, tile, :, pair * P:(pair + 1) * P],
                                              start=True, stop=True)
                    mm.then_inc(kv_mm, 1)
            for b in range(TB):
                if b:
                    pe.wait_ge(pool_out, b)
                for u in range(2):
                    mm = nc.tensor.matmul(psum[:, u, :], w_pool[:, u, :], z[:, Z_U + u, b * BLK:(b + 1) * BLK],
                                          start=True, stop=True)
                mm.then_inc(pool_mm, 1)
            pe.wait_ge(states_ready, 2)
            pe.wait_ge(pool_out, TB)

            def out_tile(b, tt):
                tile = 4 * b + tt
                pe.wait_ge(attn_ready, 4 * tile + 4)
                if tt == 0 and b:
                    pe.wait_ge(mixed, b)
                for half in range(2):
                    c = 2 * tile + half
                    t = slice(c * CHUNK, (c + 1) * CHUNK)
                    cols = slice(tt * P + half * CHUNK, tt * P + half * CHUNK + CHUNK)
                    for pair in range(2):
                        group = []
                        for head in (2 * pair, 2 * pair + 1):
                            rows = slice(64 * (head % 2), 64 * (head % 2) + 64)
                            mm = nc.tensor.matmul(psum[rows, 4 + pair, cols], v_half[:, tile, half, head * DV:(head + 1) * DV],
                                                  attn[:, tt % 2, head, :], start=True, stop=False, skip_group_check=True)
                        rows = slice(64 * pair, 64 * pair + 64)
                        dirs = [d for d in range(2) if c not in ENDS[d]]
                        for d in dirs:
                            mm = nc.tensor.matmul(psum[:, 4 + pair, cols], state[rows, d, c, :], q_in[d][rows, t],
                                                  start=False, stop=(d == dirs[-1]), skip_group_check=True)
                mm.then_inc(o_mm, 1)

            for b in range(TB):
                for tt in range(4):
                    tile = 4 * b + tt
                    for head in range(HEADS):
                        n = 4 * tile + head
                        if n >= HEADS:
                            pe.wait_ge(attn_read, n - HEADS + 1)
                        rows = slice(DK * head, DK * head + DK)
                        for lv in range(LEVELS):
                            if head == 0 and tt == 0 and lv < len(SPLITS):
                                pe.wait_ge(k_lv_ready, b * len(SPLITS) + lv + 1)
                                pe.wait_ge(q_lv_ready, b * len(SPLITS) + lv + 1)
                            for half in range(2):
                                t = (tt * P + half * CHUNK) if lv < len(SPLITS) else tile * P + half * CHUNK
                                t = slice(t, t + CHUNK)
                                ks, qs = (k_lv[rows, lv, t], q_lv[rows, lv, t]) if lv < len(SPLITS) else (k[rows, t], q[rows, t])
                                mm = nc.tensor.matmul(psum[64 * half:64 * half + 64, head, lv * CHUNK:(lv + 1) * CHUNK],
                                                      ks, qs, start=True, stop=True)
                        mm.then_inc(attn_mm, 1)
                    if tt:
                        out_tile(b, tt - 1)
                out_tile(b, 3)
                pe.wait_ge(sq_taken, b + 1)
                for tt in range(4):
                    for pair in range(2):
                        n = pair * 4 + tt
                        mm = nc.tensor.matmul(psum[:, 6, 2 * n:2 * n + 2], o_sq[:, pair, tt * P:(tt + 1) * P],
                                              head_ones[:, :], start=True, stop=True)
                mm.then_inc(stats_mm, 1)
                pe.wait_ge(rstd_spread, b + 1)
                pe.wait_ge(o_taken, 2 * b + 1)
                for pair in range(2):
                    for tt in range(4):
                        mm = nc.tensor.matmul(psum[:, 4 + pair, tt * P:(tt + 1) * P],
                                              o_sq[:, pair, tt * P:(tt + 1) * P], ident[:, :], start=True, stop=True)
                mm.then_inc(spread_mm, 1)


class Semaphores:

    def __init__(self, nc, stack):
        self.nc, self.stack = nc, stack

    def semaphore(self, name):
        return self.stack.enter_context(self.nc.semaphore(name))


NOPE, ROPE = 128, 64
HALF_ROPE = ROPE // 2
MLA_SCALE = (NOPE + ROPE) ** -0.5


def phase_mla_prepare(nc, cx, dram, rope_dram, z, psum, ident, keep):
    with ExitStack() as mem:
        sem = cx.semaphore
        sb = Region(nc, keep.next_at)
        w_uq_t = sb("p_w_uq_t", [P, HEADS, 2, P])
        w_uk_t = sb("p_w_uk_t", [P, HEADS, P])
        w_v = sb("p_w_v", [P, HEADS * P])
        w_rope = sb("p_w_rope", [P, 2, 2, P])
        w_rope_hi = sb("p_w_rope_hi", [P, 2, 2, P], F32R)
        w_rope_lo = sb("p_w_rope_lo", [P, 2, 2, P], F32R)
        cos = sb("p_cos", [P, NT])
        sin = sb("p_sin", [P, NT])
        big = sb("p_big", [P, NT])
        k_swapped = sb("p_k_swapped", [ROPE, NT])
        over_mixed = Region(nc, MLA_AT, MLA_AT + MLA_BYTES)
        rope_half = {(n, part): over_mixed(f"p_rope{n}{part}", [P, NT], F32R) for n in range(2) for part in ("hi", "lo")}
        squares = Region(nc, MLA_AT, MLA_AT + MLA_BYTES)("p_squares", [P, 3, NT])
        turned = [sb(f"p_turned{n}", [P, BLK]) for n in range(4)]
        ones = sb("p_ones", [P, 1])
        minus_half = sb("p_minus_half", [P, 1])
        mean_sq = sb("p_mean_sq", [P, 2 * TILES])
        q_gain = sb("p_q_gain", [P, 2])
        kv_gain = sb("p_kv_gain", [P, 1])

        weights_loaded = sem("p_weights_loaded")
        consts_loaded = sem("p_consts_loaded")
        swapped = sem("p_swapped")
        ones_set = sem("p_ones_set")
        sq_ready = sem("p_sq_ready")
        sq_mm = sem("p_sq_mm")
        mean_ready = sem("p_mean_ready")
        pool_step = sem("p_pool_step")
        rstd_ready = sem("p_rstd_ready")
        spread_ready = sem("p_spread_ready")
        spread_mm = sem("p_spread_mm")
        ckv_ready = sem("p_ckv_ready")
        hi_ready = sem("p_hi_ready")
        lo_ready = sem("p_lo_ready")
        dve_step = sem("p_dve_step")
        k_rope_hi = sem("p_k_rope_hi")
        k_stacked = sem("p_k_stacked")
        w_q_mm = sem("p_w_q_mm")
        rope_mm = sem("p_rope_mm")
        rope_read = sem("p_rope_read")
        rope_turned = sem("p_rope_turned")
        rope_lo = sem("p_rope_lo")
        rope_stored = sem("p_rope_stored")
        tokens_mm = sem("p_tokens_mm")
        tokens_hi_ready = sem("p_tokens_hi_ready")
        tokens_lo_ready = sem("p_tokens_lo_ready")
        cq, ckv = z[:, Z_CQ:Z_CQ + 2, :], z[:, Z_CKV, :]

        block = mem.enter_context(nc.Block())

        @block.sync
        def _(sp):
            for to, of in ((w_uq_t[:, :, :, :], dram["w_uq_t"]), (w_uk_t[:, :, :], dram["w_uk_t"]),
                           (w_v[:, :], dram["w_uv"]), (w_rope[:, :, :, :], dram["w_rope"]),
                           (q_gain[:, :], dram["q_gain"]), (kv_gain[:, :], dram["kv_gain"])):
                sp.dma_start(to, of).then_inc(weights_loaded, 16)
            for to, of in ((cos[:, :], dram["rope_cos"]), (sin[:, :], dram["rope_sin"])):
                sp.dma_start(to, of).then_inc(consts_loaded, 16)
            sp.dma_start(k_swapped[0:HALF_ROPE, :], z[HALF_ROPE:ROPE, Z_LR, :]).then_inc(swapped, 16)
            sp.dma_start(k_swapped[HALF_ROPE:ROPE, :], z[0:HALF_ROPE, Z_LR, :]).then_inc(swapped, 16)
            sp.wait_ge(k_rope_hi, 1)
            sp.dma_start(keep.k_rope[ROPE:P, :].bitcast(F32), keep.k_rope[0:ROPE, :].bitcast(F32)).then_inc(k_stacked, 16)
            for n in range(4):
                part, half = ("hi", "lo")[n // 2], n % 2
                sp.wait_ge(rope_read if part == "hi" else rope_lo, 2 * TB - 1 + half)
                sp.dma_start(rope_dram[:, n * HALF_ROPE:(n + 1) * HALF_ROPE, :],
                             rope_half[half, part][:, :].bitcast(F32)).then_inc(rope_stored, 16)
            sp.wait_ge(rope_stored, 64)
            sp.wait_ge(k_stacked, 16)

        @block.gpsimd
        def _(pool):
            nc.gpsimd.memset(ones[:, :], 1.0).then_inc(ones_set, 1)
            nc.gpsimd.memset(minus_half[:, :], -0.5).then_inc(ones_set, 1)
            pool.wait_ge(ones_set, 2)
            pool.wait_ge(mean_ready, 1)
            nc.gpsimd.tensor_scalar(mean_sq[:, :], mean_sq[:, :], EPS, None, ALU.add).then_inc(pool_step, 1)
            pool.wait_ge(pool_step, 1)
            nc.gpsimd.tensor_tensor(mean_sq[:, :], mean_sq[:, :], minus_half[:, :].broadcast_to([P, 2 * TILES]),
                                    ALU.pow).then_inc(pool_step, 1)
            pool.wait_ge(pool_step, 2)
            nc.gpsimd.tensor_scalar(keep.q_scale[:, :], mean_sq[:, 0:TILES], MLA_SCALE, None, ALU.mult)\
              .then_inc(rstd_ready, 1)

        @block.scalar
        def _(act):
            for n, (source, width) in enumerate(((ckv, P), (cq[:, 0, :], 2 * P), (cq[:, 1, :], 2 * P))):
                nc.scalar.activation(squares[:, n, :], source, ACT.Square, scale=width ** -0.5).then_inc(sq_ready, 1)
            act.wait_ge(weights_loaded, 16 * 6)
            nc.scalar.activation(w_rope_hi[:, :, :, :], w_rope[:, :, :, :], ACT.Copy).then_inc(hi_ready, 1)
            for n in range(2):
                nc.scalar.activation(keep.cq_hi[:, n, :], cq[:, n, :], ACT.Copy, scale=q_gain[:, n:n + 1]).then_inc(hi_ready, 1)
            act.wait_ge(sq_mm, 3)
            nc.scalar.activation(mean_sq[:, :], psum[:, 7, 0:2 * TILES], ACT.Copy).then_inc(mean_ready, 1)
            act.wait_ge(w_q_mm, 1)
            nc.scalar.activation(keep.w_q_hi[:, :, :, :], psum[:, 0:2, :].rearrange("p a (h k c) -> p (a h) k c", k=2, c=P),
                                 ACT.Copy).then_inc(hi_ready, 1)
            act.wait_ge(rstd_ready, 1)
            nc.scalar.activation(big[:, :].rearrange("p (a b) -> p a b", b=P),
                                 mean_sq[:, TILES:].unsqueeze(2).broadcast_to([P, TILES, P]), ACT.Copy)\
              .then_inc(spread_ready, 1)
            nc.scalar.activation(keep.w_v_hi[:, :], w_v[:, :], ACT.Copy).then_inc(hi_ready, 1)
            act.wait_ge(dve_step, 4)
            nc.scalar.activation(keep.k_rope[0:ROPE, :], k_swapped[:, :], ACT.Copy).then_inc(k_rope_hi, 1)
            act.wait_ge(ckv_ready, 1)
            nc.scalar.activation(keep.ckv_hi[:, :], big[:, :], ACT.Copy).then_inc(hi_ready, 1)
            act.wait_ge(tokens_mm, 1)
            nc.scalar.activation(keep.tokens_hi[:, :, :].rearrange("p (a t) d -> p a (t d)", a=TB), psum[:, 4:7, :],
                                 ACT.Copy).then_inc(tokens_hi_ready, 1)
            for tb in range(TB):
                t = slice(tb * BLK, (tb + 1) * BLK)
                act.wait_ge(rope_turned, 2 * tb + 2)
                for n in range(2):
                    nc.scalar.activation(rope_half[n, "hi"][:, t], turned[2 * n][:, :], ACT.Copy).then_inc(rope_read, 1)

        @block.vector
        def _(dve):
            steps = [0]

            def step(instruction):
                steps[0] += 1
                instruction.then_inc(dve_step, 1)
                dve.wait_ge(dve_step, steps[0])

            dve.wait_ge(consts_loaded, 16 * 2)
            dve.wait_ge(swapped, 32)
            k_raw = z[0:ROPE, Z_LR, :]
            step(nc.vector.tensor_tensor(k_swapped[:, :], k_swapped[:, :], sin[0:ROPE, :], ALU.mult))
            step(nc.vector.tensor_tensor(k_raw, k_raw, cos[0:ROPE, :], ALU.mult))
            for n, op in enumerate((ALU.subtract, ALU.add)):
                rows = slice(n * HALF_ROPE, (n + 1) * HALF_ROPE)
                step(nc.vector.tensor_tensor(k_swapped[rows, :], z[rows, Z_LR, :], k_swapped[rows, :], op))
            dve.wait_ge(hi_ready, 1)
            nc.vector.tensor_tensor(w_rope_lo[:, :, :, :], w_rope[:, :, :, :], w_rope_hi[:, :, :, :].bitcast(F32),
                                    ALU.subtract).then_inc(lo_ready, 1)
            for n in range(2):
                dve.wait_ge(hi_ready, 2 + n)
                nc.vector.scalar_tensor_tensor(out=keep.cq_lo[:, n, :], in0=cq[:, n, :], scalar=q_gain[:, n:n + 1],
                                               in1=keep.cq_hi[:, n, :].bitcast(F32), op0=ALU.mult, op1=ALU.subtract)\
                  .then_inc(lo_ready, 1)
            dve.wait_ge(hi_ready, 4)
            nc.vector.tensor_tensor(keep.w_q_lo[:, :, :, :], psum[:, 0:2, :].rearrange("p a (h k c) -> p (a h) k c", k=2, c=P),
                                    keep.w_q_hi[:, :, :, :].bitcast(F32), ALU.subtract).then_inc(lo_ready, 1)
            dve.wait_ge(spread_mm, 1)
            nc.vector.scalar_tensor_tensor(out=big[:, :].rearrange("p (a t) -> p a t", a=TB),
                                           in0=ckv.rearrange("p (a t) -> p a t", a=TB), scalar=kv_gain[:, 0:1],
                                           in1=psum[:, 4:7, :], op0=ALU.mult, op1=ALU.mult).then_inc(ckv_ready, 1)
            dve.wait_ge(hi_ready, 5)
            nc.vector.tensor_tensor(keep.w_v_lo[:, :], w_v[:, :], keep.w_v_hi[:, :].bitcast(F32), ALU.subtract)\
              .then_inc(lo_ready, 1)
            dve.wait_ge(k_rope_hi, 1)
            nc.vector.tensor_tensor(keep.k_rope_lo[:, :], k_swapped[:, :], keep.k_rope[0:ROPE, :].bitcast(F32),
                                    ALU.subtract).then_inc(lo_ready, 1)
            dve.wait_ge(hi_ready, 6)
            nc.vector.tensor_tensor(keep.ckv_lo[:, :], big[:, :], keep.ckv_hi[:, :].bitcast(F32), ALU.subtract)\
              .then_inc(lo_ready, 1)
            dve.wait_ge(tokens_hi_ready, 1)
            nc.vector.tensor_tensor(keep.tokens_lo[:, :, :].rearrange("p (a t) d -> p a (t d)", a=TB), psum[:, 4:7, :],
                                    keep.tokens_hi[:, :, :].rearrange("p (a t) d -> p a (t d)", a=TB).bitcast(F32),
                                    ALU.subtract).then_inc(tokens_lo_ready, 1)
            for tb in range(TB):
                t = slice(tb * BLK, (tb + 1) * BLK)
                one, two = psum[:, 2 * (tb % 2), :], psum[:, 2 * (tb % 2) + 1, :]
                dve.wait_ge(rope_mm, tb + 1)
                if tb:
                    dve.wait_ge(rope_lo, tb * 2)
                    dve.wait_ge(rope_read, 2 * tb)
                step(nc.vector.tensor_tensor(turned[0][:, :], one, cos[:, t], ALU.mult))
                step(nc.vector.tensor_tensor(turned[1][:, :], two, sin[:, t], ALU.mult))
                step(nc.vector.tensor_tensor(turned[2][:, :], two, cos[:, t], ALU.mult))
                step(nc.vector.tensor_tensor(turned[3][:, :], one, sin[:, t], ALU.mult))
                for n, op in enumerate((ALU.subtract, ALU.add)):
                    nc.vector.tensor_tensor(turned[2 * n][:, :], turned[2 * n][:, :], turned[2 * n + 1][:, :], op)\
                      .then_inc(rope_turned, 1)
                for n in range(2):
                    dve.wait_ge(rope_read, 2 * tb + n + 1)
                    nc.vector.tensor_tensor(rope_half[n, "lo"][:, t], turned[2 * n][:, :],
                                            rope_half[n, "hi"][:, t].bitcast(F32), ALU.subtract).then_inc(rope_lo, 1)

        @block.tensor
        def _(pe):
            pe.wait_ge(ones_set, 2)
            for n in range(3):
                pe.wait_ge(sq_ready, n + 1)
                for t in range(TILES):
                    col = TILES + t if n == 0 else t
                    mm = nc.tensor.matmul(psum[:, 7, col:col + 1], squares[:, n, t * P:(t + 1) * P], ones[:, :],
                                          start=(n == 0 and t == 0), stop=(n == 2 and t == TILES - 1),
                                          skip_group_check=True)
                mm.then_inc(sq_mm, 1)
            pe.wait_ge(weights_loaded, 16 * 6)
            for h in range(HEADS):
                for k in range(2):
                    n = 2 * h + k
                    mm = nc.tensor.matmul(psum[:, n // 4, (n % 4) * P:(n % 4 + 1) * P], w_uq_t[:, h, k, :], w_uk_t[:, h, :],
                                          start=True, stop=True)
            mm.then_inc(w_q_mm, 1)
            pe.wait_ge(spread_ready, 1)
            for t in range(TILES):
                mm = nc.tensor.matmul(psum[:, 4 + t // 4, (t % 4) * P:(t % 4 + 1) * P], big[:, t * P:(t + 1) * P],
                                      ident[:, :], start=True, stop=True)
            mm.then_inc(spread_mm, 1)
            pe.wait_ge(ckv_ready, 1)
            for t in range(TILES):
                mm = nc.tensor.transpose(psum[:, 4 + t // 4, (t % 4) * P:(t % 4 + 1) * P], big[:, t * P:(t + 1) * P],
                                         ident[:, :])
            mm.then_inc(tokens_mm, 1)
            pe.wait_ge(lo_ready, 4)
            for tb in range(TB):
                t = slice(tb * BLK, (tb + 1) * BLK)
                if tb == 2:
                    pe.wait_ge(rope_turned, 2)
                for n in range(2):
                    for k in range(2):
                        mm = product(nc, psum[:, 2 * (tb % 2) + n, :], w_rope_hi[:, n, k, :], w_rope_lo[:, n, k, :],
                                     keep.cq_hi[:, k, t], keep.cq_lo[:, k, t], k == 0, k == 1)
                mm.then_inc(rope_mm, 1)


class MlaKeep:

    def __init__(self, nc):
        low = Region(nc, Z_Q * NT * 4, Z_Q * NT * 4 + 2 * NT * 4)
        high = Region(nc, MLA_AT)
        self.mixed = high("mla_mixed", [P, HEADS, NT])
        self.cq_hi = high("mla_cq_hi", [P, 2, NT], F32R)
        self.cq_lo = high("mla_cq_lo", [P, 2, NT], F32R)
        self.w_q_hi = high("mla_w_q_hi", [P, HEADS, 2, P], F32R)
        self.w_q_lo = high("mla_w_q_lo", [P, HEADS, 2, P], F32R)
        self.ckv_hi = high("mla_ckv_hi", [P, NT], F32R)
        self.ckv_lo = high("mla_ckv_lo", [P, NT], F32R)
        self.tokens_hi = high("mla_tokens_hi", [P, TILES, P], F32R)
        self.tokens_lo = high("mla_tokens_lo", [P, TILES, P], F32R)
        self.w_v_hi = high("mla_w_v_hi", [P, HEADS * P], F32R)
        self.w_v_lo = high("mla_w_v_lo", [P, HEADS * P], F32R)
        self.q_scale = high("mla_q_scale", [P, TILES])
        self.next_at = high.at
        self.k_rope = low("mla_k_rope", [P, NT], F32R)
        self.k_rope_lo = low("mla_k_rope_lo", [ROPE, NT], F32R)
        self.low_free = Region(nc, Z_AT, Z_Q * NT * 4)
        self.w_out = Region(nc, MLA_AT + MLA_BYTES)("o_w_raw", [P, KT, D_MODEL])


SEQ_TILES = tuple((t0 // P, n // P) for t0, n in SEQS)
QUERY_TILES = [(f + n, f, count) for f, count in SEQ_TILES for n in range(count)]
STEPS = HEADS * TILES
SLOTS = 3
PAIR = 2 * P
PAIRS = STEPS // 2
TURN_LAG, VALUES_LAG, OUTPUT_LAG, GATHER_LAG = 2, 4, 5, 6
PROJECT_AT = {5: 0, 7: 1, 9: 2}


def turn_order():
    count, tile_end, query_end = 0, {}, {}
    for b in range(TB):
        count += 1
        query_end[0, b] = count
    for m in range(TURN_LAG, STEPS + TURN_LAG):
        if m // TILES + 1 < HEADS and m % TILES in PROJECT_AT:
            count += 1
            query_end[m // TILES + 1, PROJECT_AT[m % TILES]] = count
        count += QUERY_TILES[(m - TURN_LAG) % TILES][2] // 4
        tile_end[m - TURN_LAG] = count
    return tile_end, query_end


TILE_END, QUERY_END = turn_order()


def turned_banks(m):
    count = QUERY_TILES[m % TILES][2] // 4
    return [(n, TILE_END[m] - count + n + 1) for n in range(count)]


def projected_at(m):
    if m // TILES + 1 < HEADS and m % TILES in PROJECT_AT:
        return [(m // TILES + 1, PROJECT_AT[m % TILES])]
    return []


def pair_at(m, lag):
    return [(m - lag) // 2] if (m - lag) % 2 and 0 < m - lag < STEPS else []


def phase_mla_attend(nc, cx, rope_dram, gates_dram, w_out_dram, w_out_loaded, psum, ident, keep):
    with ExitStack() as mem:
        sem = cx.semaphore
        sb = Region(nc, keep.next_at)
        q_rope = keep.low_free("a_q_rope", [P, NT], F32R)
        q_hi = sb("a_q_hi", [P, 2, NT], F32R)
        q_lo = sb("a_q_lo", [P, 2, NT], F32R)
        turned_hi = sb("a_turned_hi", [P, 2, KT, PAIR], F32R)
        turned_lo = sb("a_turned_lo", [P, 2, KT, PAIR], F32R)
        latent_hi = sb("a_latent_hi", [P, 2, PAIR], F32R)
        latent_lo = sb("a_latent_lo", [P, 2, PAIR], F32R)
        top = sb("a_top", [P, STEPS])
        bias = sb("a_bias", [P, STEPS])
        total = sb("a_total", [P, STEPS])
        share = sb("a_share", [P, STEPS])
        latents = Region(nc, Z_CQ * NT * 4, AFTER_Z)
        gate = latents("a_gate", [P, 2, PAIR])
        weights = latents("a_weights", [P, SLOTS, 1024])

        rope_loaded = [sem(f"a_rope_loaded{n}") for n in range(TB)]
        gate_loaded = [sem(f"a_gate_loaded{n}") for n in range(2)]
        scores_done = sem("a_scores_done")
        top_ready = sem("a_top_ready")
        bias_ready = sem("a_bias_ready")
        exp_done = sem("a_exp_done")
        share_ready = sem("a_share_ready")
        turned = sem("a_turned")
        turned_hi_ready = sem("a_turned_hi_ready")
        turned_lo_ready = sem("a_turned_lo_ready")
        values_done = sem("a_values_done")
        latent_hi_ready = sem("a_latent_hi_ready")
        latent_lo_ready = sem("a_latent_lo_ready")
        output_done = sem("a_output_done")
        gate_shared = sem("a_gate_shared")
        gathered = sem("a_gathered")

        block = mem.enter_context(nc.Block())

        @block.sync
        def _(sp):
            def load_rope(h, b):
                t = slice(b * BLK, (b + 1) * BLK)
                sp.dma_start(q_rope[:, t].bitcast(F32), rope_dram[h, :, t]).then_inc(rope_loaded[b], 16)

            for b in range(TB):
                load_rope(0, b)
            for h in range(HEADS):
                for b in range(TB):
                    for p in range(2 * TB * h + 2 * b, 2 * TB * h + 2 * b + 2):
                        if p >= 2:
                            sp.wait_ge(gathered, p - 1)
                        t = (p % (2 * TB)) * PAIR
                        sp.dma_start(gate[:, p % 2, :], gates_dram[h, :, t:t + PAIR]).then_inc(gate_loaded[p % 2], 16)
                    if (h, b) == (HEADS - 1, 1):
                        sp.wait_ge(turned, QUERY_END[HEADS - 1, TB - 1])
                        for k in range(KT):
                            sp.dma_start(keep.w_out[:, k, :], w_out_dram[k * P:(k + 1) * P, :]).then_inc(w_out_loaded[k], 16)
                    if h + 1 < HEADS:
                        sp.wait_ge(scores_done, TILES * h + 4 * b + 4)
                        load_rope(h + 1, b)

        @block.scalar
        def _(act):
            def project(h, b):
                act.wait_ge(turned, QUERY_END[h, b])
                if h >= 2:
                    act.wait_ge(scores_done, TILES * (h - 2) + 4 * b + 4)
                nc.scalar.activation(q_hi[:, h % 2, b * BLK:(b + 1) * BLK], psum[:, 4 + QUERY_END[h, b] % 2, :],
                                     ACT.Copy).then_inc(turned_hi_ready, 1)

            for b in range(TB):
                project(0, b)
            for m in range(STEPS + GATHER_LAG):
                if m < STEPS:
                    tile, _, count = QUERY_TILES[m % TILES]
                    banks = slice(2 * (m % 2), 2 * (m % 2) + count // 4)
                    act.wait_ge(bias_ready, m + 1)
                    if m >= SLOTS:
                        act.wait_ge(turned, TILE_END[m - SLOTS])
                    nc.scalar.activation(weights[:, m % SLOTS, 0:count * P].rearrange("p (a k) -> p a k", k=BLK),
                                         psum[:, banks, :], ACT.Exp, bias=bias[:, m:m + 1],
                                         scale=keep.q_scale[:, tile:tile + 1], accum_out=total[:, m:m + 1])\
                      .then_inc(exp_done, 1)
                for h, b in projected_at(m):
                    project(h, b)
                for p in pair_at(m, VALUES_LAG):
                    act.wait_ge(values_done, p + 1)
                    nc.scalar.activation(latent_hi[:, p % 2, :], psum[:, 6 + p % 2, :PAIR], ACT.Copy)\
                      .then_inc(latent_hi_ready, 1)
                if 0 <= m - TURN_LAG < STEPS:
                    tile = m - TURN_LAG
                    p = tile // 2
                    if tile % 2 == 0 and p >= 2:
                        act.wait_ge(values_done, p - 1)
                    for n, item in turned_banks(tile):
                        act.wait_ge(turned, item)
                        nc.scalar.activation(turned_hi[:, p % 2, 4 * n:4 * n + 4, (tile % 2) * P:(tile % 2 + 1) * P],
                                             psum[:, 4 + item % 2, :].rearrange("p (k q) -> p k q", k=4),
                                             ACT.Copy).then_inc(turned_hi_ready, 1)

        @block.vector
        def _(dve):
            def project(h, b):
                t = slice(b * BLK, (b + 1) * BLK)
                dve.wait_ge(turned_hi_ready, QUERY_END[h, b])
                nc.vector.tensor_tensor(q_lo[:, h % 2, t], psum[:, 4 + QUERY_END[h, b] % 2, :],
                                        q_hi[:, h % 2, t].bitcast(F32), ALU.subtract).then_inc(turned_lo_ready, 1)

            for b in range(TB):
                project(0, b)
            for m in range(STEPS + GATHER_LAG):
                if m < STEPS:
                    tile, _, count = QUERY_TILES[m % TILES]
                    banks = slice(2 * (m % 2), 2 * (m % 2) + count // 4)
                    dve.wait_ge(scores_done, m + 1)
                    nc.vector.tensor_reduce(top[:, m:m + 1], psum[:, banks, :], mybir.AxisListType.XY, ALU.max)\
                      .then_inc(top_ready, 1)
                    dve.wait_ge(top_ready, m + 1)
                    nc.vector.tensor_scalar(bias[:, m:m + 1], top[:, m:m + 1], keep.q_scale[:, tile:tile + 1], -1.0,
                                            ALU.mult, ALU.mult).then_inc(bias_ready, 1)
                for p in pair_at(m, GATHER_LAG):
                    h, t = p // (2 * TB), (p % (2 * TB)) * PAIR
                    dve.wait_ge(gate_loaded[p % 2], 16 * (p // 2) + 16)
                    dve.wait_ge(output_done, p + 1)
                    nc.vector.tensor_tensor(gate[:, p % 2, :], gate[:, p % 2, :], psum[:, 6 + p % 2, PAIR:], ALU.mult)\
                      .then_inc(gate_shared, 1)
                    dve.wait_ge(gate_shared, p + 1)
                    nc.vector.tensor_tensor(keep.mixed[:, h, t:t + PAIR], psum[:, 6 + p % 2, :PAIR],
                                            gate[:, p % 2, :], ALU.mult).then_inc(gathered, 1)
                for h, b in projected_at(m):
                    project(h, b)
                for p in pair_at(m, VALUES_LAG):
                    dve.wait_ge(latent_hi_ready, p + 1)
                    nc.vector.tensor_tensor(latent_lo[:, p % 2, :], psum[:, 6 + p % 2, :PAIR],
                                            latent_hi[:, p % 2, :].bitcast(F32), ALU.subtract)\
                      .then_inc(latent_lo_ready, 1)
                if 0 <= m - TURN_LAG < STEPS:
                    tile = m - TURN_LAG
                    dve.wait_ge(exp_done, tile + 1)
                    nc.vector.reciprocal(share[:, tile:tile + 1], total[:, tile:tile + 1]).then_inc(share_ready, 1)
                    for n, item in turned_banks(tile):
                        dve.wait_ge(turned_hi_ready, item)
                        at = (slice(None), (tile // 2) % 2, slice(4 * n, 4 * n + 4),
                              slice((tile % 2) * P, (tile % 2 + 1) * P))
                        nc.vector.tensor_tensor(turned_lo[at], psum[:, 4 + item % 2, :].rearrange("p (k q) -> p k q", k=4),
                                                turned_hi[at].bitcast(F32), ALU.subtract).then_inc(turned_lo_ready, 1)

        @block.tensor
        def _(pe):
            def project(h, b):
                item = QUERY_END[h, b]
                if item > 2:
                    pe.wait_ge(turned_lo_ready, item - 2)
                t = slice(b * BLK, (b + 1) * BLK)
                for k in range(2):
                    mm = product(nc, psum[:, 4 + item % 2, :], keep.w_q_hi[:, h, k, :], keep.w_q_lo[:, h, k, :],
                                 keep.cq_hi[:, k, t], keep.cq_lo[:, k, t], k == 0, k == 1)
                mm.then_inc(turned, 1)

            def scores(m):
                h, g = m // TILES, m % TILES
                tile, first, count = QUERY_TILES[g]
                q = slice(tile * P, (tile + 1) * P)
                if g % 4 == 0:
                    pe.wait_ge(rope_loaded[g // 4], 16 * (h + 1))
                    pe.wait_ge(turned_lo_ready, QUERY_END[h, g // 4])
                if m >= 2:
                    pe.wait_ge(exp_done, m - 1)
                for n in range(count // 4):
                    k = slice(first * P + n * BLK, first * P + (n + 1) * BLK)
                    out = psum[:, 2 * (m % 2) + n, :]
                    product(nc, out, q_hi[:, h % 2, q], q_lo[:, h % 2, q], keep.ckv_hi[:, k], keep.ckv_lo[:, k], True, False)
                    nc.tensor.matmul(out, q_rope[:, q], keep.k_rope[:, k], start=False, stop=False)
                    mm = nc.tensor.matmul(out, q_rope[0:ROPE, q], keep.k_rope_lo[:, k], start=False, stop=True)
                mm.then_inc(scores_done, 1)

            def turn(m):
                pe.wait_ge(exp_done, m + 1)
                for n, item in turned_banks(m):
                    pe.wait_ge(turned_lo_ready, item - 2)
                    for k in range(4):
                        mm = nc.tensor.transpose(psum[:, 4 + item % 2, k * P:(k + 1) * P],
                                                 weights[:, m % SLOTS, (4 * n + k) * P:(4 * n + k + 1) * P], ident[:, :])
                    mm.then_inc(turned, 1)

            def values(p):
                _, first, count = QUERY_TILES[(2 * p) % TILES]
                if p >= 2:
                    pe.wait_ge(gathered, p - 1)
                pe.wait_ge(turned_lo_ready, TILE_END[2 * p + 1])
                for k in range(count):
                    mm = product(nc, psum[:, 6 + p % 2, :PAIR], keep.tokens_hi[:, first + k, :],
                                 keep.tokens_lo[:, first + k, :], turned_hi[:, p % 2, k, :], turned_lo[:, p % 2, k, :],
                                 k == 0, k == count - 1)
                mm.then_inc(values_done, 1)

            def output(p):
                h = p // (2 * TB)
                pe.wait_ge(share_ready, 2 * p + 2)
                pe.wait_ge(latent_lo_ready, p + 1)
                for n in range(2):
                    nc.tensor.matmul(psum[:, 6 + p % 2, PAIR + n * P:PAIR + (n + 1) * P],
                                     share[:, 2 * p + n:2 * p + n + 1].broadcast_to([P, P]), ident[:, :],
                                     start=True, stop=True)
                product(nc, psum[:, 6 + p % 2, :PAIR], keep.w_v_hi[:, h * P:(h + 1) * P], keep.w_v_lo[:, h * P:(h + 1) * P],
                        latent_hi[:, p % 2, :], latent_lo[:, p % 2, :]).then_inc(output_done, 1)

            for b in range(TB):
                project(0, b)
            for m in range(STEPS + GATHER_LAG):
                if m < STEPS:
                    scores(m)
                for h, b in projected_at(m):
                    project(h, b)
                for p in pair_at(m, VALUES_LAG):
                    values(p)
                if 0 <= m - TURN_LAG < STEPS:
                    turn(m - TURN_LAG)
                for p in pair_at(m, OUTPUT_LAG):
                    output(p)


def phase_output(nc, cx, w_loaded, final_g_dram, x_dram, y_dram, z, keep, psum):
    with ExitStack() as mem:
        sem = cx.semaphore
        mla_mixed, w_raw = keep.mixed, keep.w_out
        sb = Region(nc, MLA_AT + MLA_BYTES + KT * D_MODEL * 4)
        w_hi = sb("o_w_hi", [P, KT, D_MODEL], F32R)
        w_lo = sb("o_w_lo", [P, KT, D_MODEL], F32R)
        m_hi = sb("o_m_hi", [P, 2, KT, P], F32R)
        m_lo = sb("o_m_lo", [P, 2, KT, P], F32R)
        y = sb("o_y", [P, 2, D_MODEL])
        low = Region(nc, Z_AT, Z_V * NT * 4)
        g_row = low("o_g_row", [P, D_MODEL])
        x_in = low("o_x_in", [P, 2, D_MODEL])
        squares = Region(nc, Z_CQ * NT * 4, AFTER_Z)("o_squares", [P, 2, D_MODEL])
        mean_sq = sb("o_mean_sq", [P, 2])
        rstd = sb("o_rstd", [P, 2])
        eps = sb("o_eps", [P, 1])
        minus_half = sb("o_minus_half", [P, 1])

        g_loaded = sem("o_g_loaded")
        x_loaded = [sem(f"o_x_loaded{n}") for n in range(2)]
        y_stored = [sem(f"o_y_stored{n}") for n in range(2)]
        w_hi_ready = sem("o_w_hi_ready")
        w_lo_ready = sem("o_w_lo_ready")
        w_lo_pool = sem("o_w_lo_pool")
        half_set = sem("o_half_set")
        m_hi_ready = sem("o_m_hi_ready")
        m_lo_ready = sem("o_m_lo_ready")
        out_mm = sem("o_out_mm")
        summed = sem("o_summed")
        squares_done = sem("o_squares_done")
        eps_added = sem("o_eps_added")
        rstd_ready = sem("o_rstd_ready")
        y_ready = sem("o_y_ready")
        pairs = TILES // 2

        block = mem.enter_context(nc.Block())

        @block.sync
        def _(sp):
            sp.dma_start(g_row[:, :], final_g_dram.partition_broadcast(P)).then_inc(g_loaded, 16)
            for s in range(2):
                sp.dma_start(x_in[:, s, :], x_dram[rows_of(s), :]).then_inc(x_loaded[s], 16)
            with sp.Fori(1, pairs) as i:
                for s in range(2):
                    sp.wait_ge(summed, 4 * i + 2 * s - 2)
                    sp.dma_start(x_in[:, s, :], x_dram[rows_of(2 * i + s), :]).then_inc(x_loaded[s], 16)

        @block.gpsimd
        def _(pool):
            for k in range(1, KT, 3):
                pool.wait_ge(w_hi_ready, k + 1)
                nc.gpsimd.tensor_tensor(w_lo[:, k, :], w_raw[:, k, :], w_hi[:, k, :].bitcast(F32), ALU.subtract)\
                  .then_inc(w_lo_pool, 1)
            nc.gpsimd.memset(minus_half[:, :], -0.5).then_inc(half_set, 1)
            nc.gpsimd.memset(eps[:, :], EPS).then_inc(half_set, 1)
            pool.wait_ge(half_set, 2)
            with pool.Fori(0, pairs) as i:
                for s in range(2):
                    n, slot = 2 * i + s, slice(s, s + 1)
                    pool.wait_ge(squares_done, n + 1)
                    nc.gpsimd.tensor_tensor(rstd[:, slot], mean_sq[:, slot], eps[:, :], ALU.add).then_inc(eps_added, 1)
                    pool.wait_ge(eps_added, n + 1)
                    nc.gpsimd.tensor_tensor(rstd[:, slot], rstd[:, slot], minus_half[:, :],
                                            ALU.pow).then_inc(rstd_ready, 1)

        @block.scalar
        def _(act):
            def take_hi(i, s, first):
                n = 2 * i + s
                if not first:
                    act.wait_ge(out_mm, 2 * n - 2)
                nc.scalar.activation(m_hi[:, s, 0:4, :], mla_mixed[:, :, rows_of(n)], ACT.Copy).then_inc(m_hi_ready, 1)
                nc.scalar.activation(m_hi[:, s, 4:8, :], z[:, Z_V:Z_V + 4, rows_of(n)], ACT.Copy).then_inc(m_hi_ready, 1)

            def finish(i, s, first):
                n = 2 * i + s
                if not first:
                    act.wait_ge(eps_added, n - 1)
                act.wait_ge(summed, 2 * n + 2)
                nc.scalar.activation(squares[:, s, :], y[:, s, :], ACT.Square, scale=D_MODEL ** -0.5,
                                     accum_out=mean_sq[:, s:s + 1]).then_inc(squares_done, 1)

            def store(i, s):
                n = 2 * i + s
                act.wait_ge(y_ready, n + 1)
                act.dma_start(y_dram[rows_of(n), :], y[:, s, :]).then_inc(y_stored[s], 16)

            for k in range(KT):
                act.wait_ge(w_loaded[k], 16)
                if k < 2:
                    take_hi(0, k, True)
                nc.scalar.activation(w_hi[:, k, :], w_raw[:, k, :], ACT.Copy).then_inc(w_hi_ready, 1)
            finish(0, 0, True)
            take_hi(1, 0, False)
            store(0, 0)
            finish(0, 1, True)
            take_hi(1, 1, False)
            store(0, 1)
            with act.Fori(1, pairs - 1) as i:
                for s in range(2):
                    finish(i, s, False)
                    take_hi(i + 1, s, False)
                    store(i, s)
            for s in range(2):
                finish(pairs - 1, s, False)
                store(pairs - 1, s)
            for s in range(2):
                act.wait_ge(y_stored[s], 16 * pairs)

        @block.vector
        def _(dve):
            def take_lo(i, s):
                n = 2 * i + s
                dve.wait_ge(m_hi_ready, 2 * n + 1)
                nc.vector.tensor_tensor(m_lo[:, s, 0:4, :], mla_mixed[:, :, rows_of(n)], m_hi[:, s, 0:4, :].bitcast(F32),
                                        ALU.subtract).then_inc(m_lo_ready, 1)
                dve.wait_ge(m_hi_ready, 2 * n + 2)
                nc.vector.tensor_tensor(m_lo[:, s, 4:8, :], z[:, Z_V:Z_V + 4, rows_of(n)], m_hi[:, s, 4:8, :].bitcast(F32),
                                        ALU.subtract).then_inc(m_lo_ready, 1)

            def add_input(i, s, first):
                n = 2 * i + s
                dve.wait_ge(x_loaded[s], 16 * i + 16)
                if not first:
                    dve.wait_ge(y_stored[s], 16 * i)
                for half in range(2):
                    dve.wait_ge(out_mm, 2 * n + half + 1)
                    cols = slice(half * BLK, (half + 1) * BLK)
                    nc.vector.tensor_tensor(y[:, s, cols], psum[:, 2 * s + half, :], x_in[:, s, cols], ALU.add)\
                      .then_inc(summed, 1)

            def normalise(i, s):
                n = 2 * i + s
                dve.wait_ge(rstd_ready, n + 1)
                nc.vector.scalar_tensor_tensor(out=y[:, s, :], in0=y[:, s, :], scalar=rstd[:, s:s + 1],
                                               in1=g_row[:, :], op0=ALU.mult, op1=ALU.mult).then_inc(y_ready, 1)

            take_lo(0, 0)
            for k in range(KT):
                if k % 3 != 1:
                    dve.wait_ge(w_hi_ready, k + 1)
                    nc.vector.tensor_tensor(w_lo[:, k, :], w_raw[:, k, :], w_hi[:, k, :].bitcast(F32), ALU.subtract)\
                      .then_inc(w_lo_ready, 1)
            take_lo(0, 1)
            dve.wait_ge(g_loaded, 16)
            for s in range(2):
                add_input(0, s, True)
                take_lo(1, s)
                normalise(0, s)
            with dve.Fori(1, pairs - 1) as i:
                for s in range(2):
                    add_input(i, s, False)
                    take_lo(i + 1, s)
                    normalise(i, s)
            for s in range(2):
                add_input(pairs - 1, s, False)
                normalise(pairs - 1, s)

        @block.tensor
        def _(pe):
            def multiply(i, s, first):
                n = 2 * i + s
                pe.wait_ge(m_lo_ready, 2 * n + 2)
                for half in range(2):
                    if not first:
                        pe.wait_ge(summed, 2 * n - 3 + half)
                    cols = slice(half * BLK, (half + 1) * BLK)
                    for k in range(KT):
                        if first and s == 0 and half == 0:
                            if k % 3 == 1:
                                pe.wait_ge(w_lo_pool, k // 3 + 1)
                            else:
                                pe.wait_ge(w_lo_ready, k + 1 - (k + 1) // 3)
                        mm = product(nc, psum[:, 2 * s + half, :], m_hi[:, s, k, :], m_lo[:, s, k, :],
                                     w_hi[:, k, cols], w_lo[:, k, cols], k == 0, k == KT - 1)
                    mm.then_inc(out_mm, 1)

            for s in range(2):
                multiply(0, s, True)
            with pe.Fori(1, pairs) as i:
                for s in range(2):
                    multiply(i, s, False)


class Semaphores:

    def __init__(self, nc, stack):
        self.nc, self.stack = nc, stack

    def semaphore(self, name):
        return self.stack.enter_context(self.nc.semaphore(name))


def hymba_encoder_kernel(nc, dram, y_dram):
    with ExitStack() as whole:
        cx = Semaphores(nc, whole)
        scratch = lambda name, shape, dt: nc.dram_tensor(name, shape, dt, kind="Internal").ap()
        psum = whole.enter_context(nc.psum_tensor("psum", [P, 8, BLK], F32))
        ident = Region(nc, SBUF_BYTES, SBUF_BYTES + P * 4)("ident", [P, P])
        gates_dram = scratch("gates_scratch", (Z_GATES, P, NT), F32)
        rope_dram = scratch("rope_scratch", (HEADS, P, NT), F32)
        z = Region(nc, Z_AT)("z", [P, Z_PLAIN, NT])
        h_mem = Region(nc, AFTER_Z)
        h_hi = h_mem("h_hi", [P, KT, NT], F32R)
        h_lo = h_mem("h_lo", [P, KT, NT], F32R)
        phase_project(nc, cx, dram, gates_dram, h_hi, h_lo, z, psum, ident)
        phase_gla(nc, cx, dram, gates_dram, z, psum, ident)
        keep = MlaKeep(nc)
        phase_mla_prepare(nc, cx, dram, rope_dram, z, psum, ident, keep)
        w_out_loaded = [cx.semaphore(f"w_out_loaded{k}") for k in range(KT)]
        phase_mla_attend(nc, cx, rope_dram, gates_dram, dram["w_out"], w_out_loaded, psum, ident, keep)
        phase_output(nc, cx, w_out_loaded, dram["final_norm_g"], dram["x"], y_dram, z, keep, psum)


POOL_WINDOWS = (2, 4, 8, 16)
ROPE_BASE = 10000.0
IN_COLUMNS = ((Z_LR, 384, 448, 0), (Z_LR, 1984, 2016, 64),
              (Z_Q, 1472, 1600, 0), (Z_K, 1600, 1728, 0), (Z_V, 1728, 1984, 0),
              (Z_U, 960, 1216, 0), (Z_CQ, 0, 256, 0), (Z_CKV, 256, 384, 0),
              (Z_PLAIN, 448, 960, 0), (Z_PLAIN + 4, 1216, 1472, 0), (Z_PLAIN + 6, 2016, 2272, 0))


def shape_tables(np):
    lane = np.arange(P)
    edge = np.ones((P, 2, 2, POOL_PAD), np.float32)
    mean = np.zeros((P, 2), np.float32)
    for g, w in enumerate(POOL_WINDOWS):
        u, rows = g // 2, slice(64 * (g % 2), 64 * (g % 2) + 64)
        mean[rows, u] = 1.0 / w
        for t in range(POOL_PAD):
            edge[rows, u, 0, t] = w / (w // 2 + min(t, w // 2))
            edge[rows, u, 1, t] = w / (w // 2 + min(POOL_PAD - t, w // 2))
    level_mask = np.zeros((P, LEVELS, CHUNK), np.float32)
    for key in range(P):
        for query in range(CHUNK):
            apart = (key % CHUNK) ^ query
            level_mask[key, LEVELS - 1 - apart.bit_length(), query] = 1.0 if apart else 2.0
    inverse = (1.0 / ROPE_BASE ** (np.arange(0, ROPE, 2, dtype=np.float32) / np.float32(ROPE))).astype(np.float32)
    position = np.concatenate([np.arange(n) for _, n in SEQS]).astype(np.float32)
    angle = inverse[:, None] * position[None]
    return {
        "ident": np.eye(P, dtype=np.float32),
        "pool_edge": edge,
        "pool_mean": mean,
        "level_mask": level_mask.reshape(P, LEVELS * CHUNK),
        "pair_mask": ((lane[:, None] // DK) % 2 == lane[None, :] // DV).astype(np.float32),
        "head_ones": (lane[:, None] // DV == np.arange(2)).astype(np.float32),
        "rope_cos": np.tile(np.cos(angle), (HEADS, 1)),
        "rope_sin": np.tile(np.sin(angle), (HEADS, 1)),
    }


def lay_out(np, inp):
    w_in = inp["w_in"][0]
    columns = np.zeros((D_MODEL, Z_TILES * P), np.float32)
    for tile, start, end, at in IN_COLUMNS:
        columns[:, tile * P + at:tile * P + at + end - start] = w_in[:, start:end]
    gate_up = np.zeros((32, 2, P), np.float32)
    gate_up[:16, FWD], gate_up[16:, BWD] = inp["gk_up_fwd"][0], inp["gk_up_bwd"][0]
    w_pool = np.zeros((P, 2, P), np.float32)
    for g in range(len(POOL_WINDOWS)):
        at = 64 * (g % 2)
        w_pool[at:at + 64, g // 2, at:at + 64] = inp["w_pool"][0, g]
    w_uq = inp["w_uq"][0].reshape(2 * P, HEADS, NOPE + ROPE)
    w_rope = w_uq[:, :, NOPE:].reshape(2, P, HEADS, 2, HALF_ROPE)
    w_ukv = inp["w_ukv"][0].reshape(P, HEADS, 2 * P)
    w_out = inp["w_out"][0]
    return {
        "x": np.concatenate([inp["x_prompt"][0], inp["x_sample"][0]], 0),
        "w_z": columns.reshape(KT, P, Z_TILES, P).transpose(2, 1, 0, 3).reshape(Z_TILES, P, D_MODEL),
        "norm_g": inp["norm_g"][0],
        "gate_up": gate_up,
        "gate_bias": np.stack([inp["gk_bias_fwd"][0], inp["gk_bias_bwd"][0]], 1),
        "gla_gain": np.tile(inp["gla_norm_g"][0], 2)[:, None],
        "w_pool": w_pool,
        "pool_scale": inp["pool_scale"][0].reshape(2, P).T,
        "w_uq_t": w_uq[:, :, :NOPE].transpose(2, 1, 0).reshape(P, HEADS, 2, P),
        "w_uk_t": w_ukv[:, :, :NOPE].transpose(2, 1, 0),
        "w_rope": w_rope.transpose(1, 3, 0, 2, 4).reshape(P, 2, 2, P),
        "w_uv": w_ukv[:, :, NOPE:].reshape(P, HEADS * P),
        "q_gain": inp["q_norm_g"][0].reshape(2, P).T,
        "kv_gain": inp["kv_norm_g"][0][:, None],
        "w_out": np.concatenate([w_out[:512], w_out[768:], w_out[512:768]], 0),
        "final_norm_g": inp["final_norm_g"],
    }


def kernel(**inputs):
    import numpy as np
    import concourse.bacc as bacc
    from concourse.bass_utils import run_bass_kernel_spmd

    inputs = {name: np.asarray(a) for name, a in inputs.items()}
    nc = bacc.Bacc("TRN2", target_bir_lowering=False, num_devices=1)
    arrays, dram = {}, {}
    for name, a in {**lay_out(np, inputs), **shape_tables(np)}.items():
        a = np.ascontiguousarray(a)
        arrays[f"in_{name}_dram"] = a
        dram[name] = nc.dram_tensor(f"in_{name}_dram", a.shape, mybir.dt.from_np(a.dtype), kind="ExternalInput").ap()
    y = nc.dram_tensor("out_dram", (NT, D_MODEL), F32, kind="ExternalOutput").ap()
    hymba_encoder_kernel(nc, dram, y)
    got = run_bass_kernel_spmd(nc, [arrays], core_ids=[0]).results[0]["out_dram"]
    return tuple(got[start:start + n][None] for start, n in SEQS)
```

```python
from contextlib import ExitStack

import concourse.bass as bass
from concourse import mybir

F32 = mybir.dt.float32
F32R = mybir.dt.float32r
ALU = mybir.AluOpType
ACT = mybir.ActivationFunctionType
AX_X = mybir.AxisListType.X

P = 128
D_MODEL = 1024
SEQS = ((0, 1024), (1024, 512))
NT = 1536
TILES = NT // P
KT = D_MODEL // P
BLK = 512
TB = NT // BLK
EPS = 1e-6

Z_LR, Z_Q, Z_K, Z_V, Z_U, Z_CQ, Z_CKV = 0, 1, 2, 3, 5, 7, 9
Z_PLAIN = 10
Z_GATES = 8
Z_FIRST_GATE = Z_CQ
Z_TILES = Z_PLAIN + Z_GATES
CHUNK = 64
CHUNKS = NT // CHUNK
FWD, BWD = 0, 1
HEADS = 4
GATE_RANK = 16


def rows_of(t):
    return bass.ds(t * P, P)


Z_AT = 0
AFTER_Z = Z_PLAIN * NT * 4
H_BYTES = KT * NT * 4
MLA_AT = AFTER_Z
MLA_BYTES = 4 * NT * 4
SBUF_BYTES = 212224
SUMS_AT = SBUF_BYTES - 2 * CHUNKS * (CHUNK + 1) * 4


class Region:

    def __init__(self, nc, at, end=SBUF_BYTES):
        self.nc, self.at, self.end = nc, at, end
        self.base = -(-nc.sbuf_base // 64) * 64

    def __call__(self, name, shape, dtype=F32):
        size = 4
        for n in shape[1:]:
            size *= n
        at, self.at = self.at, self.at + -(-size // 32) * 32
        assert self.at <= self.end, (name, self.at, self.end)
        return self.nc.alloc_sbuf_tensor_at(name, shape, dtype, offset=self.base + at)


def product(nc, out, a_hi, a_lo, b_hi, b_lo, first=True, last=True):
    nc.tensor.matmul(out, a_hi, b_hi, start=first, stop=False)
    nc.tensor.matmul(out, a_hi, b_lo, start=False, stop=False)
    return nc.tensor.matmul(out, a_lo, b_hi, start=False, stop=last)


X_SLOTS = 4
EARLY_BLOCKS = ((0, 0), (1, 0), (0, 1), (1, 1), (0, 2), (1, 2))


POOL_PAD = 8
PADDED = NT + 2 * len(SEQS) * POOL_PAD
POOL_STEPS = 30
POOL_AT = (POOL_PAD, SEQS[0][1] + 3 * POOL_PAD)


def phase_project(nc, cx, dram, gates_dram, h_hi, h_lo, z, psum, ident, sums):
    with ExitStack() as mem:
        sb = Region(nc, AFTER_Z + 2 * H_BYTES, SUMS_AT)
        sem = cx.semaphore
        w_raw = sb("z_w_raw", [P, 2, D_MODEL])
        w_hi = sb("z_w_hi", [P, 2, D_MODEL], F32R)
        w_lo = sb("z_w_lo", [P, 2, D_MODEL], F32R)
        gate = sb("z_gate", [P, 2, BLK])
        scan_keep = sb("z_scan_keep", [P, CHUNKS * (CHUNK + 1)])
        gate_up = sb("z_gate_up", [P, 2, P])
        gate_bias = sb("z_gate_bias", [P, 2])
        last_z = Region(nc, Z_CQ * NT * 4, AFTER_Z)
        log_gate = last_z("z_log_gate", [P, 2, NT])
        soft = last_z("z_soft", [P, NT])
        last_z = Region(nc, Z_CQ * NT * 4, AFTER_Z)
        window_sums = [last_z(f"z_window_sums{n}", [P, PADDED]) for n in range(2)]
        pool_edge = sb("z_pool_edge", [P, 2, 2, POOL_PAD])
        pool_mean = sb("z_pool_mean", [P, 2])
        mean_sq = sb("n_mean_sq", [P, TILES])
        rstd = sb("n_rstd", [P, TILES])
        minus_half = sb("n_minus_half", [P, 1])
        eps = sb("n_eps", [P, 1])
        late_z = Region(nc, Z_U * NT * 4, AFTER_Z)
        x_in = late_z("n_x_in", [P, X_SLOTS, D_MODEL])
        x_norm = late_z("n_x_norm", [P, 2, D_MODEL])
        g_row = late_z("n_g_row", [P, D_MODEL])

        x_loaded = [sem(f"n_x_loaded{s}") for s in range(X_SLOTS)]
        g_loaded = sem("n_g_loaded")
        ident_loaded = sem("n_ident_loaded")
        half_set = sem("n_half_set")
        squares_done = sem("n_squares_done")
        eps_added = sem("n_eps_added")
        rstd_ready = sem("n_rstd_ready")
        norm_ready = sem("n_norm_ready")
        turned = sem("n_turned")
        hi_ready = sem("n_hi_ready")
        lo_ready = sem("n_lo_ready")
        w_loaded = [sem(f"z_w_loaded{s}") for s in range(2)]
        gate_stored = [sem(f"z_gate_stored{s}") for s in range(2)]
        w_hi_ready = sem("z_w_hi_ready")
        w_lo_ready = sem("z_w_lo_ready")
        z_done = sem("z_done")
        z_emptied = sem("z_emptied")
        pool_loaded = sem("z_pool_loaded")
        pool_step = sem("z_pool_step")
        gate_consts = sem("z_gate_consts")
        keep_set = sem("z_keep_set")
        gate_mm = sem("z_gate_mm")
        biased = sem("z_biased")
        soft_step = sem("z_soft_step")
        log_step = sem("z_log_step")
        pairs = Z_TILES // 2

        block = mem.enter_context(nc.Block())

        @block.sync
        def _(sp):
            def load_x(n):
                if n >= X_SLOTS:
                    sp.wait_ge(norm_ready, n - X_SLOTS + 1)
                sp.dma_start(x_in[:, n % X_SLOTS, :], dram["x"][n * P:(n + 1) * P, :]).then_inc(x_loaded[n % X_SLOTS], 16)

            def load_w(i, s, first):
                if not first:
                    sp.wait_ge(w_lo_ready, 2 * i + s - 1)
                sp.dma_start(w_raw[:, s, :], dram["w_z"][bass.ds(2 * i + s, 1), :, :].rearrange("a p n -> (a p) n"))\
                  .then_inc(w_loaded[s], 16)

            load_x(0)
            sp.dma_start(g_row[:, :], dram["norm_g"].partition_broadcast(P)).then_inc(g_loaded, 16)
            load_x(1)
            sp.dma_start(ident[:, :], dram["ident"]).then_inc(ident_loaded, 16)
            load_x(2)
            load_x(3)
            for s in range(2):
                load_w(0, s, True)
            for n in range(X_SLOTS, TILES):
                load_x(n)
            sp.dma_start(gate_up[4 * GATE_RANK:6 * GATE_RANK, :, :], dram["gate_up"]).then_inc(gate_consts, 16)
            sp.dma_start(gate_bias[:, :], dram["gate_bias"]).then_inc(gate_consts, 16)
            sp.dma_start(pool_edge[:, :, :, :], dram["pool_edge"]).then_inc(pool_loaded, 16)
            sp.dma_start(pool_mean[:, :], dram["pool_mean"]).then_inc(pool_loaded, 16)
            with sp.Fori(1, pairs) as i:
                for s in range(2):
                    load_w(i, s, False)

        @block.scalar
        def _(act):
            def square(n):
                act.wait_ge(x_loaded[n % X_SLOTS], 16 * (n // X_SLOTS) + 16)
                if n >= 2:
                    act.wait_ge(turned, 2 * n - 2)
                nc.scalar.activation(x_norm[:, n % 2, :], x_in[:, n % X_SLOTS, :], ACT.Square, scale=D_MODEL ** -0.5,
                                     accum_out=mean_sq[:, n:n + 1]).then_inc(squares_done, 1)

            def take_hi(n):
                for half in range(2):
                    act.wait_ge(turned, 2 * n + half + 1)
                    nc.scalar.activation(h_hi[:, 4 * half:4 * half + 4, n * P:(n + 1) * P],
                                         psum[:, 6 + half, :].rearrange("p (k t) -> p k t", k=4),
                                         ACT.Copy).then_inc(hi_ready, 1)

            def split_hi(i, s, first):
                act.wait_ge(w_loaded[s], 16 * i + 16)
                if not first:
                    act.wait_ge(z_done, TB * (2 * i + s) - TB)
                nc.scalar.activation(w_hi[:, s, :], w_raw[:, s, :], ACT.Copy).then_inc(w_hi_ready, 1)

            def empty(i, s, first=False, place=None):
                n = 2 * i + s
                place = n if place is None else place
                for tb in range(TB):
                    act.wait_ge(z_done, 2 * tb + 1 if first else TB * n + tb + 1)
                    nc.scalar.activation(
                        z[:, bass.ds(place, 1), tb * BLK:(tb + 1) * BLK].rearrange("p a t -> p (a t)"),
                        psum[:, TB * s + tb, :], ACT.Copy).then_inc(z_emptied, 1)

            def empty_gate(i, s):
                for tb in range(TB):
                    r = TB * s + tb - TB * Z_FIRST_GATE
                    slot = r % 2
                    if not (isinstance(i, int) and 2 * TB * i + r < 2):
                        act.wait_ge(gate_stored[slot], 16 * (TB * i + r // 2))
                    act.wait_ge(z_done, TB * (2 * i + s) + tb + 1)
                    nc.scalar.activation(gate[:, slot, :], psum[:, TB * s + tb, :], ACT.Silu).then_inc(z_emptied, 1)
                    act.wait_ge(z_emptied, TB * (2 * i + s) + tb + 1)
                    act.dma_start(gates_dram[bass.ds(2 * i + s - Z_FIRST_GATE, 1), :, tb * BLK:(tb + 1) * BLK]
                                  .rearrange("a p t -> (a p) t"), gate[:, slot, :]).then_inc(gate_stored[slot], 16)

            def soften(d):
                act.wait_ge(biased, TB * (d + 1))
                if d:
                    act.wait_ge(log_step, 3)
                nc.scalar.activation(soft[:, :], log_gate[:, d, :], ACT.Abs).then_inc(soft_step, 1)
                act.wait_ge(soft_step, 3 * d + 1)
                nc.scalar.activation(soft[:, :], soft[:, :], ACT.Exp, scale=-1.0).then_inc(soft_step, 1)
                act.wait_ge(soft_step, 3 * d + 2)
                nc.scalar.activation(soft[:, :], soft[:, :], ACT.Ln, bias=1.0).then_inc(soft_step, 1)

            square(0)
            square(1)
            for n in range(TILES):
                take_hi(n)
                if n + 2 < TILES:
                    square(n + 2)
                if n in (1, 2):
                    split_hi(0, n - 1, True)
            empty(0, 0, True)
            for i in (1, 2):
                split_hi(i, 0, False)
                empty(i - 1, 1)
                split_hi(i, 1, False)
                empty(i, 0)
                soften(i - 1)
            i = Z_FIRST_GATE // 2
            split_hi(i, 0, False)
            empty(i - 1, 1)
            split_hi(i, 1, False)
            empty(i, 0)
            i += 1
            split_hi(i, 0, False)
            empty_gate(i - 1, 1)
            split_hi(i, 1, False)
            empty_gate(i, 0)
            with act.Fori(i + 1, pairs - 2) as n:
                split_hi(n, 0, False)
                empty_gate(n - 1, 1)
                split_hi(n, 1, False)
                empty_gate(n, 0)
            i = pairs - 2
            split_hi(i, 0, False)
            empty_gate(i - 1, 1)
            split_hi(i, 1, False)
            empty_gate(i, 0)
            split_hi(i + 1, 0, False)
            act.wait_ge(pool_step, POOL_STEPS)
            empty(i, 1, place=Z_CQ)
            split_hi(i + 1, 1, False)
            empty(i + 1, 0, place=Z_CQ + 1)
            empty(i + 1, 1, place=Z_CKV)
            for s in range(2):
                act.wait_ge(gate_stored[s], 8 * Z_GATES * TB)

        @block.gpsimd
        def _(pool):
            def invert_root(n):
                pool.wait_ge(squares_done, n + 1)
                nc.gpsimd.tensor_tensor(rstd[:, n:n + 1], mean_sq[:, n:n + 1], eps[:, :], ALU.add).then_inc(eps_added, 1)
                pool.wait_ge(eps_added, n + 1)
                nc.gpsimd.tensor_tensor(rstd[:, n:n + 1], rstd[:, n:n + 1], minus_half[:, :], ALU.pow)\
                  .then_inc(rstd_ready, 1)

            def split_lo(i, s, first):
                pool.wait_ge(w_hi_ready, 2 * i + s + 1)
                if not first:
                    pool.wait_ge(z_done, TB * (2 * i + s) - TB)
                nc.gpsimd.tensor_tensor(w_lo[:, s, :], w_raw[:, s, :], w_hi[:, s, :].bitcast(F32),
                                        ALU.subtract).then_inc(w_lo_ready, 1)

            nc.gpsimd.memset(minus_half[:, :], -0.5).then_inc(half_set, 1)
            nc.gpsimd.memset(eps[:, :], EPS).then_inc(half_set, 1)
            pool.wait_ge(half_set, 2)
            for n in range(TILES):
                invert_root(n)
                if n in (4, 5):
                    split_lo(0, n - 4, True)
            nc.gpsimd.memset(scan_keep[:, :], 1.0).then_inc(keep_set, 1)
            pool.wait_ge(keep_set, 1)
            nc.gpsimd.memset(scan_keep[:, :].rearrange("p (c t) -> p c t", t=CHUNK + 1)[:, :, 0:1], 0.0).then_inc(keep_set, 1)
            with pool.Fori(1, pairs) as i:
                for s in range(2):
                    split_lo(i, s, False)

        @block.vector
        def _(dve):
            def normalise(n):
                dve.wait_ge(rstd_ready, n + 1)
                nc.vector.scalar_tensor_tensor(out=x_norm[:, n % 2, :], in0=x_in[:, n % X_SLOTS, :],
                                               scalar=rstd[:, n:n + 1], in1=g_row[:, :],
                                               op0=ALU.mult, op1=ALU.mult).then_inc(norm_ready, 1)

            def take_lo(n):
                for half in range(2):
                    dve.wait_ge(hi_ready, 2 * n + half + 1)
                    at = (slice(None), slice(4 * half, 4 * half + 4), slice(n * P, (n + 1) * P))
                    nc.vector.tensor_tensor(h_lo[at], psum[:, 6 + half, :].rearrange("p (k t) -> p k t", k=4),
                                            h_hi[at].bitcast(F32), ALU.subtract).then_inc(lo_ready, 1)

            dve.wait_ge(g_loaded, 16)
            normalise(0)
            for n in range(TILES):
                if n + 1 < TILES:
                    normalise(n + 1)
                take_lo(n)

            dve.wait_ge(gate_consts, 32)
            for d in range(2):
                for tb in range(TB):
                    dve.wait_ge(gate_mm, TB * d + tb + 1)
                    nc.vector.tensor_scalar(log_gate[:, d, tb * BLK:(tb + 1) * BLK], psum[:, 6 + (TB * d + tb) % 2, :],
                                            gate_bias[:, d:d + 1], None, ALU.add).then_inc(biased, 1)
            dve.wait_ge(biased, 2 * TB)
            for d in range(2):
                dve.wait_ge(soft_step, 3 * d + 3)
                flat = sums[d][:, :, :].rearrange("p c t -> p (c t)")
                nc.vector.memset(sums[d][:, :, 0:1], 0.0).then_inc(log_step, 1)
                nc.vector.scalar_tensor_tensor(out=sums[d][:, :, 1:],
                                               in0=log_gate[:, d, :].rearrange("p (c t) -> p c t", t=CHUNK), scalar=0.0,
                                               in1=soft[:, :].rearrange("p (c t) -> p c t", t=CHUNK),
                                               op0=ALU.min, op1=ALU.subtract).then_inc(log_step, 1)
                dve.wait_ge(log_step, 3 * d + 2)
                dve.wait_ge(keep_set, 2)
                nc.vector.tensor_tensor_scan(flat, scan_keep[:, :], flat, 0.0, ALU.mult, ALU.add).then_inc(log_step, 1)

            steps = [0]

            def step(instruction):
                steps[0] += 1
                instruction.then_inc(pool_step, 1)
                dve.wait_ge(pool_step, steps[0])

            even, odd = window_sums
            dve.wait_ge(pool_loaded, 32)
            dve.wait_ge(z_emptied, TB * (Z_U + 2))
            for u in range(2):
                step(nc.vector.memset(even[:, :], 0.0))
                step(nc.vector.memset(odd[:, :], 0.0))
                for (t0, n), at in zip(SEQS, POOL_AT):
                    step(nc.vector.tensor_copy(even[:, at:at + n], z[:, Z_U + u, t0:t0 + n]))
                upper = slice(64, P)
                step(nc.vector.tensor_tensor(odd[:, 1:], even[:, :-1], even[:, 1:], ALU.add))
                rows = upper if u == 0 else slice(0, P)
                step(nc.vector.tensor_tensor(even[rows, 1:-1], odd[rows, :-2], odd[rows, 2:], ALU.add))
                if u == 1:
                    step(nc.vector.tensor_tensor(odd[:, 2:-2], even[:, :-4], even[:, 4:], ALU.add))
                    step(nc.vector.tensor_tensor(even[upper, 4:-4], odd[upper, :-8], odd[upper, 8:], ALU.add))
                for rows, total in ((slice(0, 64), odd), (upper, even)):
                    for (t0, n), at in zip(SEQS, POOL_AT):
                        ends = total[rows, at:at + n].rearrange("p (a b) -> p a b", b=POOL_PAD)[:, ::n // POOL_PAD - 1, :]
                        step(nc.vector.tensor_tensor(ends, ends, pool_edge[rows, u, :, :], ALU.mult))
                        out = z[rows, Z_U + u, t0:t0 + n]
                        step(nc.vector.scalar_tensor_tensor(out=out, in0=total[rows, at:at + n],
                                                            scalar=pool_mean[rows, u:u + 1], in1=out,
                                                            op0=ALU.mult, op1=ALU.subtract))
            assert steps[0] == POOL_STEPS

        @block.tensor
        def _(pe):
            def turn(n):
                pe.wait_ge(norm_ready, n + 1)
                for half in range(2):
                    if n:
                        pe.wait_ge(lo_ready, 2 * n - 1 + half)
                    for k in range(4):
                        mm = nc.tensor.transpose(psum[:, 6 + half, k * P:(k + 1) * P],
                                                 x_norm[:, n % 2, (4 * half + k) * P:(4 * half + k + 1) * P],
                                                 ident[:, :])
                    mm.then_inc(turned, 1)

            def project_block(s, tb, tiles=()):
                t = slice(tb * BLK, (tb + 1) * BLK)
                for k in range(KT):
                    if k in (2, 5) and tiles:
                        turn(tiles[k == 5])
                    c = slice(k * P, (k + 1) * P)
                    mm = product(nc, psum[:, TB * s + tb, :], w_hi[:, s, c], w_lo[:, s, c],
                                 h_hi[:, k, t], h_lo[:, k, t], k == 0, k == KT - 1)
                mm.then_inc(z_done, 1)

            pe.wait_ge(ident_loaded, 16)
            for n in range(4):
                turn(n)
            for n, (s, tb) in enumerate(EARLY_BLOCKS):
                pe.wait_ge(w_lo_ready, s + 1)
                pe.wait_ge(lo_ready, 8 * tb + 8)
                project_block(s, tb, (2 * n + 4, 2 * n + 5) if 2 * n + 5 < TILES else ())
            def project_pair(i):
                for s in range(2):
                    n = 2 * i + s
                    pe.wait_ge(w_lo_ready, n + 1)
                    for tb in range(TB):
                        pe.wait_ge(z_emptied, TB * n - 2 * TB + tb + 1)
                        project_block(s, tb)

            project_pair(1)
            pe.wait_ge(gate_consts, 32)
            rows = slice(4 * GATE_RANK, 6 * GATE_RANK)
            for n in range(2 * TB):
                d, tb = n // TB, n % TB
                if n >= 2:
                    pe.wait_ge(biased, n - 1)
                nc.tensor.matmul(psum[:, 6 + n % 2, :], gate_up[rows, d, :], z[rows, Z_LR, tb * BLK:(tb + 1) * BLK],
                                 start=True, stop=True).then_inc(gate_mm, 1)
            with pe.Fori(2, pairs) as i:
                project_pair(i)


SPLITS = (32, 16, 8, 4, 2, 1)
LEVELS = len(SPLITS) + 1
DIAGONAL = len(SPLITS)
DK, DV = 32, 64
ENDS = tuple(t0 // CHUNK for t0, _ in SEQS), tuple((t0 + n) // CHUNK - 1 for t0, n in SEQS)
GLA_Q_SCALE = DK ** -0.5
GATE_SCALE = 1.0 / 16.0
UNIT = 2 * P
UNITS = NT // UNIT
UNIT_CHUNKS = UNIT // CHUNK
GROUPS = 2
IN_GROUP = len(SPLITS) // GROUPS
BANKS = -(-LEVELS // 2)


def phase_gla(nc, cx, dram, gates_dram, z, psum, ident, sums):
    with ExitStack() as mem:
        sb = Region(nc, AFTER_Z, SUMS_AT)
        sem = cx.semaphore
        level_mask = sb("g_level_mask", [P, LEVELS, CHUNK])
        head_ones = sb("g_head_ones", [P, 2])
        gla_gain = sb("g_gain", [P, 1])
        w_pool = sb("g_w_pool", [P, 2, P])
        pool_scale = sb("g_pool_scale", [P, 2])
        minus_half = sb("g_minus_half", [P, 1])
        decay = sb("g_decay", [P, 2, CHUNKS])
        state = sb("g_state", [P, 2, DV, CHUNKS])
        k_decayed = sb("g_k_decayed", [P, 2, BLK])
        k_turned = sb("g_k_turned", [P, 2, 4, P])
        v_half = sb("g_v_half", [P, TILES, 2, HEADS * DV])
        expo = sb("g_expo", [P, 2, 2, IN_GROUP, UNIT])
        expo_ends = sb("g_expo_ends", [P, 2, UNIT])
        q_level = sb("g_q_level", [P, LEVELS + 2, UNIT])
        k_level = sb("g_k_level", [P, 2, len(SPLITS), UNIT])
        q_spread = sb("g_q_spread", [P, 2, LEVELS, HEADS, P])
        q_states = sb("g_q_states", [P, 3, 2, HEADS, P])
        weighted = sb("g_weighted", [P, LEVELS, HEADS * CHUNK])
        attn = sb("g_attn", [P, 2, HEADS * CHUNK])
        stats = w_pool[:, 0, 0:16]
        gate = sb("g_gate", [P, 2, BLK])
        o_sq = k_turned.rearrange("p n a e -> p n (a e)")
        pool_gate = k_level.rearrange("p s l t -> p (s l t)").rearrange("p (b m t) -> p b m t", b=TB, m=2)
        decay_spread = weighted[:, 0:6, :].rearrange("p l n -> p (l n)")

        consts_loaded = sem("g_consts_loaded")
        half_set = sem("g_half_set")
        pool_gate_loaded = sem("g_pool_gate_loaded")
        v_cleared = sem("g_v_cleared")
        q_cleared = sem("g_q_cleared")
        v_mm = sem("g_v_mm")
        v_taken = sem("g_v_taken")
        decay_ready = sem("g_decay_ready")
        k_expo = sem("g_k_expo")
        k_exp_done = sem("g_k_exp_done")
        k_scaled = sem("g_k_scaled")
        k_mm = sem("g_k_mm")
        k_taken = sem("g_k_taken")
        kv_mm = sem("g_kv_mm")
        kv_taken = sem("g_kv_taken")
        state_ready = sem("g_state_ready")
        q_expo = sem("g_q_expo")
        q_exp_done = sem("g_q_exp_done")
        q_ready = sem("g_q_ready")
        key_expo = sem("g_key_expo")
        key_exp_done = sem("g_key_exp_done")
        k_ready = sem("g_k_ready")
        q_spread_ready = sem("g_q_spread_ready")
        q_states_ready = sem("g_q_states_ready")
        states_cleared = sem("g_states_cleared")
        attn_mm = sem("g_attn_mm")
        attn_read = sem("g_attn_read")
        attn_ready = sem("g_attn_ready")
        o_mm = sem("g_o_mm")
        sq_taken = sem("g_sq_taken")
        o_taken = sem("g_o_taken")
        stats_mm = sem("g_stats_mm")
        stats_taken = sem("g_stats_taken")
        pool_step = sem("g_pool_step")
        rstd_ready = sem("g_rstd_ready")
        rstd_spread = sem("g_rstd_spread")
        spread_mm = sem("g_spread_mm")
        mixed = sem("g_mixed")
        gate_loaded = sem("g_gate_loaded")
        pool_mm = sem("g_pool_mm")
        pool_out = sem("g_pool_out")
        q, k = z[:, Z_Q, :], z[:, Z_K, :]
        BLOCK_CHUNKS = BLK // CHUNK
        N_CONSTS = 5
        STAGES = GROUPS + 1

        def part(ap, u, h, half, shift):
            ap = ap[:, u * UNIT_CHUNKS:(u + 1) * UNIT_CHUNKS, shift:shift + CHUNK]
            return ap.rearrange("p c (n a h) -> p c n a h", a=2, h=h)[:, :, :, half, :]

        def bound(ap, u, h):
            ap = ap[:, u * UNIT_CHUNKS:(u + 1) * UNIT_CHUNKS, 0:CHUNK]
            ap = ap.rearrange("p c (n a h) -> p c n a h", a=2, h=h)[:, :, :, 1, 0:1]
            return ap.broadcast_to([P, UNIT_CHUNKS, CHUNK // (2 * h), h])

        def to(slot, of_key, n, h, half):
            ap = expo[:, slot, of_key, n, :].rearrange("p (c n a h) -> p c n a h", c=UNIT_CHUNKS, a=2, h=h)
            return ap[:, :, :, half, :]

        block = mem.enter_context(nc.Block())

        @block.sync
        def _(sp):
            sp.dma_start(level_mask[:, :, :], dram["level_mask"].rearrange("p (l i) -> p l i", l=LEVELS)).then_inc(consts_loaded, 16)
            sp.dma_start(head_ones[:, :], dram["head_ones"]).then_inc(consts_loaded, 16)
            sp.dma_start(gla_gain[:, :], dram["gla_gain"]).then_inc(consts_loaded, 16)
            sp.dma_start(w_pool[:, :, :], dram["w_pool"]).then_inc(consts_loaded, 16)
            sp.dma_start(pool_scale[:, :], dram["pool_scale"]).then_inc(consts_loaded, 16)
            for b in range(TB):
                t = b * BLK
                sp.dma_start(pool_gate[:, b, :, :], gates_dram[4:6, :, t:t + BLK].rearrange("a p t -> p a t"))\
                  .then_inc(pool_gate_loaded, 16)
            for b in range(TB):
                if b:
                    sp.wait_ge(mixed, b)
                t = b * BLK
                sp.dma_start(gate[:, :, :], gates_dram[6:8, :, t:t + BLK].rearrange("a p t -> p a t"))\
                  .then_inc(gate_loaded, 16)

        @block.gpsimd
        def _(pool):
            def key_exponents(u):
                for g in range(GROUPS):
                    if u:
                        pool.wait_ge(k_ready, GROUPS * u + g - 1)
                    for n in range(IN_GROUP):
                        h = SPLITS[IN_GROUP * g + n]
                        nc.gpsimd.tensor_tensor(to(g, 1, n, h, 0), bound(sums[FWD], u, h), part(sums[FWD], u, h, 0, 1),
                                                ALU.subtract).then_inc(key_expo, 1)
                        nc.gpsimd.tensor_tensor(to(g, 1, n, h, 1), part(sums[BWD], u, h, 1, 0), bound(sums[BWD], u, h),
                                                ALU.subtract).then_inc(key_expo, 1)

            def weight_keys(u):
                for g in range(GROUPS):
                    pool.wait_ge(key_exp_done, GROUPS * u + g + 1)
                    if u == 0:
                        pool.wait_ge(pool_out, TB)
                    if u >= 2:
                        pool.wait_ge(attn_mm, BANKS * (2 * u - 2))
                    nc.gpsimd.tensor_tensor(k_level[:, u % 2, IN_GROUP * g:IN_GROUP * (g + 1), :], expo[:, g, 1, :, :],
                                            k[:, u * UNIT:(u + 1) * UNIT].unsqueeze(1).broadcast_to([P, IN_GROUP, UNIT]),
                                            ALU.mult).then_inc(k_ready, 1)

            def invert_root(b):
                pool.wait_ge(stats_taken, b + 1)
                nc.gpsimd.tensor_scalar(stats[:, :], stats[:, :], EPS, None, ALU.add).then_inc(pool_step, 1)
                pool.wait_ge(pool_step, b + 1)
                nc.gpsimd.tensor_tensor(stats[:, :], stats[:, :], minus_half[:, :].broadcast_to([P, 16]),
                                        ALU.pow).then_inc(rstd_ready, 1)

            nc.gpsimd.memset(v_half[:, TILES // 2:, :, :], 0.0).then_inc(v_cleared, 1)
            nc.gpsimd.memset(minus_half[:, :], -0.5).then_inc(half_set, 1)
            pool.wait_ge(half_set, 1)
            for n in range(2 * TB):
                pool.wait_ge(k_exp_done, n + 1)
                t = slice((n % TB) * BLK, (n % TB + 1) * BLK)
                nc.gpsimd.tensor_tensor(k_decayed[:, n % 2, :], k_decayed[:, n % 2, :], k[:, t], ALU.mult)\
                  .then_inc(k_scaled, 1)
                if n == 1:
                    key_exponents(0)
                if n == 2:
                    nc.gpsimd.memset(q_spread[:, 0, :, :, :], 0.0).then_inc(q_cleared, 1)
            nc.gpsimd.memset(q_states[:, :, :, :, :], 0.0).then_inc(states_cleared, 1)
            weight_keys(0)
            key_exponents(1)
            nc.gpsimd.memset(q_spread[:, 1, :, :, :], 0.0).then_inc(q_cleared, 1)
            for u in range(1, UNITS):
                weight_keys(u)
                if u + 1 < UNITS:
                    key_exponents(u + 1)
                if u % 2 == 1 and u >= 3:
                    invert_root(u // 2 - 1)
            invert_root(TB - 1)

        @block.scalar
        def _(act):
            def exponentials(u):
                chunks = slice(u * UNIT_CHUNKS, (u + 1) * UNIT_CHUNKS)
                for g in range(GROUPS):
                    act.wait_ge(q_expo, (2 * len(SPLITS) + 1) * u + 2 * IN_GROUP * (g + 1))
                    nc.scalar.activation(expo[:, g, 0, :, :], expo[:, g, 0, :, :], ACT.Exp, scale=GATE_SCALE)\
                      .then_inc(q_exp_done, 1)
                    act.wait_ge(key_expo, 2 * len(SPLITS) * u + 2 * IN_GROUP * (g + 1))
                    nc.scalar.activation(expo[:, g, 1, :, :], expo[:, g, 1, :, :], ACT.Exp, scale=GATE_SCALE)\
                      .then_inc(key_exp_done, 1)
                act.wait_ge(q_expo, (2 * len(SPLITS) + 1) * (u + 1))
                nc.scalar.activation(expo_ends[:, 0, :].rearrange("p (c t) -> p c t", t=CHUNK), sums[FWD][:, chunks, 1:],
                                     ACT.Exp, scale=GATE_SCALE).then_inc(q_exp_done, 1)
                nc.scalar.activation(expo_ends[:, 1, :], expo_ends[:, 1, :], ACT.Exp, scale=GATE_SCALE)\
                  .then_inc(q_exp_done, 1)

            def spread_queries(t, levels, slot, spread):
                for head in range(HEADS):
                    rows = slice(DK * head, DK * (head + 1))
                    nc.scalar.activation(slot[rows, :, head, :], q_level[rows, levels, (t % 2) * P:(t % 2 + 1) * P],
                                         ACT.Copy).then_inc(spread, 1)

            def spread_levels(t):
                act.wait_ge(q_ready, (STAGES + 1) * (t // 2 + 1))
                if t < 2:
                    act.wait_ge(q_cleared, t + 1)
                else:
                    act.wait_ge(attn_mm, BANKS * (t - 1))
                spread_queries(t, slice(0, LEVELS), q_spread[:, t % 2, :, :, :], q_spread_ready)

            def spread_states(t):
                if t == 0:
                    act.wait_ge(states_cleared, 1)
                if t >= 3:
                    act.wait_ge(o_mm, t - 2)
                spread_queries(t, slice(LEVELS, LEVELS + 2), q_states[:, t % 3, :, :, :], q_states_ready)

            def take_values(n):
                act.wait_ge(v_mm, n + 1)
                if n == 0:
                    act.wait_ge(v_cleared, 2)
                for half in range(2):
                    rows = slice(64 * half, 64 * half + 64)
                    nc.scalar.activation(v_half[rows, 2 * n:2 * n + 2, half, :],
                                         psum[rows, 6 + n % 2, :].rearrange("p (a e) -> p a e", a=2),
                                         ACT.Copy).then_inc(v_taken, 1)

            def decay_keys(n):
                tb = n % TB
                chunks = slice(tb * BLOCK_CHUNKS, (tb + 1) * BLOCK_CHUNKS)
                if n >= 2:
                    act.wait_ge(k_mm, n - 1)
                if n < TB:
                    act.wait_ge(k_expo, n + 1)
                    source = k_decayed[:, n % 2, :].rearrange("p (c t) -> p c t", t=CHUNK)
                else:
                    source = sums[BWD][:, chunks, :CHUNK]
                nc.scalar.activation(k_decayed[:, n % 2, :].rearrange("p (c t) -> p c t", t=CHUNK), source,
                                     ACT.Exp, scale=GATE_SCALE).then_inc(k_exp_done, 1)

            def take_keys(n):
                act.wait_ge(k_mm, n + 1)
                if n >= 2:
                    act.wait_ge(kv_mm, n - 1)
                nc.scalar.activation(k_turned[:, n % 2, :, :], psum[:, 6 + n % 2, :].rearrange("p (a e) -> p a e", a=4),
                                     ACT.Copy).then_inc(k_taken, 1)

            def take_states(d):
                act.wait_ge(kv_mm, TB * (d + 1))
                nc.scalar.activation(state[:, d, :, :].rearrange("p e (b c) -> p b c e", b=TB),
                                     psum[:, 3 * d:3 * d + 3, :].rearrange("p b (c e) -> p b c e", e=DV),
                                     ACT.Copy).then_inc(kv_taken, 1)
                if d:
                    act.wait_ge(state_ready, 1)
                nc.scalar.activation(decay_spread.rearrange("p (e c) -> p e c", c=CHUNKS),
                                     decay[:, d, :].unsqueeze(1).broadcast_to([P, DV, CHUNKS]), ACT.Copy)\
                  .then_inc(kv_taken, 1)

            nc.scalar.activation(decay[:, FWD, :], sums[FWD][:, :, CHUNK], ACT.Exp, scale=GATE_SCALE).then_inc(decay_ready, 1)
            nc.scalar.activation(decay[:, BWD, :], sums[BWD][:, ::-1, CHUNK], ACT.Exp, scale=GATE_SCALE).then_inc(decay_ready, 1)
            decay_keys(0)
            decay_keys(1)
            for n in range(TILES // 2):
                take_values(n)
            for n in range(2 * TB):
                take_keys(n)
                if n + 2 < 2 * TB:
                    decay_keys(n + 2)
                if n == 2:
                    exponentials(0)
                if n == 3:
                    act.wait_ge(decay_ready, 6)
                    take_states(FWD)
            spread_levels(0)
            take_states(BWD)
            spread_states(0)
            for t in range(TILES + 3):
                b = t // 4 - 1
                if t % 4 == 2 and b >= 0:
                    act.wait_ge(rstd_ready, b + 1)
                    nc.scalar.activation(o_sq[:, :, :].rearrange("p a (n e) -> p (a n) e", e=DV),
                                         stats[:, :].unsqueeze(2).broadcast_to([P, 16, DV]),
                                         ACT.Copy).then_inc(rstd_spread, 1)
                if t + 1 < TILES:
                    spread_levels(t + 1)
                    spread_states(t + 1)
                if t % 2 == 0 and t // 2 + 1 < UNITS:
                    exponentials(t // 2 + 1)
                if t % 4 == 0 and b >= 0:
                    act.wait_ge(o_mm, 4 * b + 4)
                    nc.scalar.activation(o_sq[:, :, :], psum[:, 4:6, :], ACT.Square, scale=DV ** -0.5).then_inc(sq_taken, 1)
                if t % 4 == 1 and b >= 0:
                    act.wait_ge(stats_mm, b + 1)
                    nc.scalar.activation(stats[:, :], psum[:, 6, 0:16], ACT.Copy).then_inc(stats_taken, 1)

        @block.vector
        def _(dve):
            def query_exponents(u):
                chunks = slice(u * UNIT_CHUNKS, (u + 1) * UNIT_CHUNKS)
                if u:
                    dve.wait_ge(q_ready, (STAGES + 1) * u)
                for g in range(GROUPS):
                    for n in range(IN_GROUP):
                        h = SPLITS[IN_GROUP * g + n]
                        nc.vector.tensor_tensor(to(g, 0, n, h, 1), part(sums[FWD], u, h, 1, 1), bound(sums[FWD], u, h),
                                                ALU.subtract).then_inc(q_expo, 1)
                        nc.vector.tensor_tensor(to(g, 0, n, h, 0), bound(sums[BWD], u, h), part(sums[BWD], u, h, 0, 0),
                                                ALU.subtract).then_inc(q_expo, 1)
                nc.vector.tensor_tensor(expo_ends[:, 1, :].rearrange("p (c t) -> p c t", t=CHUNK),
                                        sums[BWD][:, chunks, CHUNK:].broadcast_to([P, UNIT_CHUNKS, CHUNK]),
                                        sums[BWD][:, chunks, :CHUNK], ALU.subtract).then_inc(q_expo, 1)

            def weight_queries(u):
                tokens = slice(u * UNIT, (u + 1) * UNIT)
                if u:
                    dve.wait_ge(q_states_ready, 2 * HEADS * u)
                for g in range(GROUPS):
                    dve.wait_ge(q_exp_done, (STAGES + 1) * u + g + 1)
                    nc.vector.scalar_tensor_tensor(
                        out=q_level[:, IN_GROUP * g:IN_GROUP * (g + 1), :], in0=expo[:, g, 0, :, :], scalar=GLA_Q_SCALE,
                        in1=q[:, tokens].unsqueeze(1).broadcast_to([P, IN_GROUP, UNIT]),
                        op0=ALU.mult, op1=ALU.mult).then_inc(q_ready, 1)
                nc.vector.tensor_scalar(q_level[:, DIAGONAL, :], q[:, tokens], GLA_Q_SCALE, None, ALU.mult).then_inc(q_ready, 1)
                dve.wait_ge(q_exp_done, (STAGES + 1) * (u + 1))
                nc.vector.scalar_tensor_tensor(
                    out=q_level[:, LEVELS:, :], in0=expo_ends[:, :, :], scalar=GLA_Q_SCALE,
                    in1=q[:, tokens].unsqueeze(1).broadcast_to([P, 2, UNIT]),
                    op0=ALU.mult, op1=ALU.mult).then_inc(q_ready, 1)

            def mask(t):
                if t:
                    dve.wait_ge(attn_ready, t)
                for j in range(BANKS):
                    levels = slice(2 * j, min(2 * j + 2, LEVELS))
                    count = levels.stop - levels.start
                    dve.wait_ge(attn_mm, BANKS * t + j + 1)
                    nc.vector.tensor_tensor(
                        weighted[:, levels, :].rearrange("p l (h i) -> p l h i", h=HEADS),
                        psum[:, j, 0:count * HEADS * CHUNK].rearrange("p (l h i) -> p l h i", l=count, h=HEADS),
                        level_mask[:, levels, :].unsqueeze(2).broadcast_to([P, count, HEADS, CHUNK]),
                        ALU.mult).then_inc(attn_read, 1)
                dve.wait_ge(attn_read, BANKS * (t + 1))
                if t >= 2:
                    dve.wait_ge(o_mm, t - 1)
                nc.vector.tensor_reduce(attn[:, t % 2, :], weighted[:, :, :].rearrange("p l n -> p n l"), AX_X, ALU.add)\
                  .then_inc(attn_ready, 1)

            nc.vector.memset(v_half[:, :TILES // 2, :, :], 0.0).then_inc(v_cleared, 1)
            for n in range(TB):
                chunks = slice(n * BLOCK_CHUNKS, (n + 1) * BLOCK_CHUNKS)
                if n >= 2:
                    dve.wait_ge(k_mm, n - 1)
                nc.vector.tensor_tensor(k_decayed[:, n % 2, :].rearrange("p (c t) -> p c t", t=CHUNK),
                                        sums[FWD][:, chunks, CHUNK:].broadcast_to([P, BLOCK_CHUNKS, CHUNK]),
                                        sums[FWD][:, chunks, 1:], ALU.subtract).then_inc(k_expo, 1)
                if n == 1:
                    dve.wait_ge(decay_ready, 2)
                    firsts = ENDS[FWD], tuple(CHUNKS - 1 - c for c in ENDS[BWD])
                    for d in range(2):
                        for c in firsts[d]:
                            nc.vector.memset(decay[:, d, c:c + 1], 0.0).then_inc(decay_ready, 1)
            dve.wait_ge(consts_loaded, 16 * N_CONSTS)
            for b in range(TB):
                t = slice(b * BLK, (b + 1) * BLK)
                if b == 0:
                    dve.wait_ge(pool_gate_loaded, 16 * TB)
                dve.wait_ge(pool_mm, b + 1)
                for m in range(2):
                    ins = nc.vector.scalar_tensor_tensor(out=z[:, Z_U + m, t], in0=psum[:, 4 + m, :],
                                                         scalar=pool_scale[:, m:m + 1], in1=pool_gate[:, b, m, :],
                                                         op0=ALU.mult, op1=ALU.mult)
                ins.then_inc(pool_out, 1)
                if b == 0:
                    query_exponents(0)
            weight_queries(0)
            for d in range(2):
                dve.wait_ge(kv_taken, 2 * d + 2)
                flat = state[:, d, :, :].rearrange("p e c -> p (e c)")
                nc.vector.tensor_tensor_scan(flat, decay_spread, flat, 0.0, ALU.mult, ALU.add).then_inc(state_ready, 1)
            query_exponents(1)
            dve.wait_ge(state_ready, 2)
            for t in range(TILES + 3):
                if t < TILES:
                    mask(t)
                if t % 2 == 0 and t // 2 + 1 < UNITS:
                    weight_queries(t // 2 + 1)
                if t % 2 == 1 and t // 2 + 2 < UNITS:
                    query_exponents(t // 2 + 2)
                b = t // 4 - 1
                if t % 4 == 0 and b >= 0:
                    dve.wait_ge(sq_taken, b + 1)
                    dve.wait_ge(gate_loaded, 16 * b + 16)
                    nc.vector.scalar_tensor_tensor(out=gate[:, :, :], in0=psum[:, 4:6, :], scalar=gla_gain[:, 0:1],
                                                   in1=gate[:, :, :], op0=ALU.mult, op1=ALU.mult).then_inc(o_taken, 1)
                if t % 4 == 2 and b >= 0:
                    dve.wait_ge(spread_mm, b + 1)
                    dve.wait_ge(o_taken, b + 1)
                    nc.vector.tensor_tensor(z[:, Z_V:Z_V + 2, b * BLK:(b + 1) * BLK], gate[:, :, :], psum[:, 6:8, :],
                                            ALU.mult).then_inc(mixed, 1)

        @block.tensor
        def _(pe):
            def turn_values(n):
                if n >= 2:
                    pe.wait_ge(v_taken, 2 * n - 2)
                for a in range(4):
                    t = (2 * n + a // 2) * P
                    mm = nc.tensor.transpose(psum[:, 6 + n % 2, a * P:(a + 1) * P], z[:, Z_V + a % 2, t:t + P], ident[:, :])
                mm.then_inc(v_mm, 1)

            def turn_keys(n):
                pe.wait_ge(k_scaled, n + 1)
                if n < 2:
                    pe.wait_ge(v_taken, TILES + 2 * n - 2)
                else:
                    pe.wait_ge(k_taken, n - 1)
                for a in range(4):
                    mm = nc.tensor.transpose(psum[:, 6 + n % 2, a * P:(a + 1) * P], k_decayed[:, n % 2, a * P:(a + 1) * P],
                                             ident[:, :])
                mm.then_inc(k_mm, 1)

            def add_up(n):
                d, tb = n // TB, n % TB
                if n == 0:
                    pe.wait_ge(v_taken, TILES)
                pe.wait_ge(k_taken, n + 1)
                for a in range(4):
                    tile = 4 * tb + a
                    for head in range(HEADS):
                        rows = slice(DK * head, DK * (head + 1))
                        for half in range(2):
                            c = 2 * tile + half
                            at = c if d == FWD else CHUNKS - 1 - c
                            mm = nc.tensor.matmul(psum[rows, 3 * d + at // 8, (at % 8) * DV:(at % 8 + 1) * DV],
                                                  k_turned[:, n % 2, a, rows],
                                                  v_half[:, tile, half, head * DV:(head + 1) * DV],
                                                  start=True, stop=True, skip_group_check=True)
                mm.then_inc(kv_mm, 1)

            def attend(t):
                u = t // 2
                for j in range(BANKS):
                    if j == 0:
                        pe.wait_ge(q_spread_ready, HEADS * (t + 1))
                    if j in (0, 1):
                        pe.wait_ge(k_ready, GROUPS * u + j + 1)
                    if t:
                        pe.wait_ge(attn_read, BANKS * (t - 1) + j + 1)
                    for lv in range(2 * j, min(2 * j + 2, LEVELS)):
                        for half in range(2):
                            at = (t % 2) * P + half * CHUNK
                            keys = k_level[:, u % 2, lv, at:at + CHUNK] if lv < DIAGONAL else \
                                k[:, u * UNIT + at:u * UNIT + at + CHUNK]
                            cols = slice((lv % 2) * HEADS * CHUNK, (lv % 2 + 1) * HEADS * CHUNK)
                            mm = nc.tensor.matmul(psum[64 * half:64 * half + 64, j, cols]
                                                  .rearrange("p (h i) -> p h i", h=HEADS), keys,
                                                  q_spread[:, t % 2, lv, :, half * CHUNK:(half + 1) * CHUNK],
                                                  start=True, stop=True, skip_group_check=True)
                    mm.then_inc(attn_mm, 1)

            def output(t):
                pe.wait_ge(attn_ready, t + 1)
                pe.wait_ge(q_states_ready, HEADS * (t + 1))
                if t == 0:
                    pe.wait_ge(state_ready, 2)
                    pe.wait_ge(pool_out, TB)
                elif t % 4 == 0:
                    pe.wait_ge(o_taken, t // 4)
                for half in range(2):
                    c = 2 * t + half
                    cols = slice((t % 4) * P + half * CHUNK, (t % 4) * P + (half + 1) * CHUNK)
                    dirs = [d for d in range(2) if c not in ENDS[d]]
                    for n in range(1 + len(dirs)):
                        for head in range(HEADS):
                            out = psum[64 * (head % 2):64 * (head % 2) + 64, 4 + head // 2, cols]
                            if n == 0:
                                weights, moving = v_half[:, t, half, head * DV:(head + 1) * DV], \
                                    attn[:, t % 2, head * CHUNK:(head + 1) * CHUNK]
                            else:
                                d = dirs[n - 1]
                                at = c - 1 if d == FWD else CHUNKS - 2 - c
                                weights = state[:, d, :, at]
                                moving = q_states[:, t % 3, d, head, half * CHUNK:(half + 1) * CHUNK]
                            mm = nc.tensor.matmul(out, weights, moving, start=(n == 0), stop=(n == len(dirs)),
                                                  skip_group_check=True)
                mm.then_inc(o_mm, 1)

            for n in range(TILES // 2):
                turn_values(n)
            pe.wait_ge(consts_loaded, 16 * N_CONSTS)
            for b in range(TB):
                if b:
                    pe.wait_ge(pool_out, b)
                for m in range(2):
                    mm = nc.tensor.matmul(psum[:, 4 + m, :], w_pool[:, m, :], z[:, Z_U + m, b * BLK:(b + 1) * BLK],
                                          start=True, stop=True)
                mm.then_inc(pool_mm, 1)
                turn_keys(b)
                if b:
                    add_up(b - 1)
            pe.wait_ge(pool_out, TB)
            for n in range(TB, 2 * TB):
                turn_keys(n)
                add_up(n - 1)
            add_up(2 * TB - 1)
            for t in range(TILES + 3):
                b = t // 4 - 1
                if t < TILES:
                    if t == 0:
                        pe.wait_ge(kv_taken, 3)
                    attend(t)
                if t % 4 == 1 and b >= 0:
                    pe.wait_ge(sq_taken, b + 1)
                    if b:
                        pe.wait_ge(mixed, b)
                    for tt in range(4):
                        for pair in range(2):
                            n = pair * 4 + tt
                            mm = nc.tensor.matmul(psum[:, 6, 2 * n:2 * n + 2], o_sq[:, pair, tt * P:(tt + 1) * P],
                                                  head_ones[:, :], start=True, stop=True)
                    mm.then_inc(stats_mm, 1)
                if 0 < t <= TILES:
                    output(t - 1)
                if t % 4 == 2 and b >= 0:
                    pe.wait_ge(rstd_spread, b + 1)
                    for pair in range(2):
                        for tt in range(4):
                            mm = nc.tensor.matmul(psum[:, 6 + pair, tt * P:(tt + 1) * P],
                                                  o_sq[:, pair, tt * P:(tt + 1) * P], ident[:, :], start=True, stop=True)
                    mm.then_inc(spread_mm, 1)


NOPE, ROPE = 128, 64
HALF_ROPE = ROPE // 2
MLA_SCALE = (NOPE + ROPE) ** -0.5


def phase_mla_prepare(nc, cx, dram, rope_dram, z, psum, ident, keep):
    with ExitStack() as mem:
        sem = cx.semaphore
        sb = Region(nc, keep.next_at)
        w_uq_t = sb("p_w_uq_t", [P, HEADS, 2, P])
        w_uk_t = sb("p_w_uk_t", [P, HEADS, P])
        w_v = sb("p_w_v", [P, HEADS * P])
        w_rope = sb("p_w_rope", [P, 2, 2, P])
        w_rope_hi = sb("p_w_rope_hi", [P, 2, 2, P], F32R)
        w_rope_lo = sb("p_w_rope_lo", [P, 2, 2, P], F32R)
        cos = sb("p_cos", [P, NT])
        sin = sb("p_sin", [P, NT])
        big = sb("p_big", [P, NT])
        k_swapped = sb("p_k_swapped", [ROPE, NT])
        over_mixed = Region(nc, MLA_AT, MLA_AT + MLA_BYTES)
        rope_half = {(n, part): over_mixed(f"p_rope{n}{part}", [P, NT], F32R) for n in range(2) for part in ("hi", "lo")}
        over_tokens = Region(nc, keep.tokens_at)
        squares = [Region(nc, keep.w_q_at)("p_squares0", [P, NT])] + \
            [over_tokens(f"p_squares{n}", [P, NT]) for n in (1, 2)]
        turned = [[sb(f"p_turned{slot}{n}", [P, BLK]) for n in range(4)] for slot in range(2)]
        ones = sb("p_ones", [P, 1])
        minus_half = sb("p_minus_half", [P, 1])
        mean_sq = sb("p_mean_sq", [P, 2 * TILES])
        q_gain = sb("p_q_gain", [P, 2])
        kv_gain = sb("p_kv_gain", [P, 1])

        rope_weights_loaded = sem("p_rope_weights_loaded")
        weights_loaded = sem("p_weights_loaded")
        tables_loaded = sem("p_tables_loaded")
        swapped = sem("p_swapped")
        ones_set = sem("p_ones_set")
        sq_ready = sem("p_sq_ready")
        kv_sq_mm = sem("p_kv_sq_mm")
        q_sq_mm = sem("p_q_sq_mm")
        mean_ready = sem("p_mean_ready")
        pool_step = sem("p_pool_step")
        spread_ready = sem("p_spread_ready")
        spread_mm = sem("p_spread_mm")
        w_rope_hi_ready = sem("p_w_rope_hi_ready")
        w_rope_lo_ready = sem("p_w_rope_lo_ready")
        cq_hi_ready = sem("p_cq_hi_ready")
        cq_lo_ready = sem("p_cq_lo_ready")
        w_q_mm = sem("p_w_q_mm")
        w_q_hi_ready = sem("p_w_q_hi_ready")
        w_v_hi_ready = sem("p_w_v_hi_ready")
        late_lo_ready = sem("p_late_lo_ready")
        ckv_ready = sem("p_ckv_ready")
        ckv_hi_ready = sem("p_ckv_hi_ready")
        tokens_mm = sem("p_tokens_mm")
        tokens_hi_ready = sem("p_tokens_hi_ready")
        k_step = sem("p_k_step")
        k_rope_hi = sem("p_k_rope_hi")
        k_stacked = sem("p_k_stacked")
        rope_mm = sem("p_rope_mm")
        rope_parts = sem("p_rope_parts")
        rope_turned = sem("p_rope_turned")
        rope_hi = sem("p_rope_hi")
        rope_lo = sem("p_rope_lo")
        rope_stored = sem("p_rope_stored")
        cq, ckv = z[:, Z_CQ:Z_CQ + 2, :], z[:, Z_CKV, :]
        KV, Q = 0, 1

        block = mem.enter_context(nc.Block())

        @block.sync
        def _(sp):
            for to, of in ((w_rope[:, :, :, :], dram["w_rope"]), (q_gain[:, :], dram["q_gain"]),
                           (kv_gain[:, :], dram["kv_gain"])):
                sp.dma_start(to, of).then_inc(rope_weights_loaded, 16)
            sp.dma_start(k_swapped[0:HALF_ROPE, :], z[HALF_ROPE:ROPE, Z_LR, :]).then_inc(swapped, 16)
            sp.dma_start(k_swapped[HALF_ROPE:ROPE, :], z[0:HALF_ROPE, Z_LR, :]).then_inc(swapped, 16)
            for to, of in ((cos[:, :], dram["rope_cos"]), (sin[:, :], dram["rope_sin"])):
                sp.dma_start(to, of).then_inc(tables_loaded, 16)
            for to, of in ((w_uq_t[:, :, :, :], dram["w_uq_t"]), (w_uk_t[:, :, :], dram["w_uk_t"]),
                           (w_v[:, :], dram["w_uv"])):
                sp.dma_start(to, of).then_inc(weights_loaded, 16)
            for tb in range(TB):
                t = slice(tb * BLK, (tb + 1) * BLK)
                for n in range(4):
                    part, half = ("hi", "lo")[n // 2], n % 2
                    sp.wait_ge(rope_hi if part == "hi" else rope_lo, 2 * tb + half + 1)
                    sp.dma_start(rope_dram[:, n * HALF_ROPE:(n + 1) * HALF_ROPE, t],
                                 rope_half[half, part][:, t].bitcast(F32)).then_inc(rope_stored, 16)
            sp.wait_ge(k_rope_hi, 1)
            sp.dma_start(keep.k_rope[ROPE:P, :].bitcast(F32), keep.k_rope[0:ROPE, :].bitcast(F32)).then_inc(k_stacked, 16)
            sp.wait_ge(rope_stored, 64 * TB)
            sp.wait_ge(k_stacked, 16)

        @block.gpsimd
        def _(pool):
            nc.gpsimd.memset(ones[:, :], 1.0).then_inc(ones_set, 1)
            nc.gpsimd.memset(minus_half[:, :], -0.5).then_inc(ones_set, 1)
            pool.wait_ge(w_rope_hi_ready, 1)
            nc.gpsimd.tensor_tensor(w_rope_lo[:, :, :, :], w_rope[:, :, :, :], w_rope_hi[:, :, :, :].bitcast(F32),
                                    ALU.subtract).then_inc(w_rope_lo_ready, 1)
            pool.wait_ge(ones_set, 2)
            def invert_root(n):
                of = mean_sq[:, n * TILES:(n + 1) * TILES]
                pool.wait_ge(mean_ready, n + 1)
                nc.gpsimd.tensor_scalar(of, of, EPS, None, ALU.add).then_inc(pool_step, 1)
                pool.wait_ge(pool_step, 2 * n + 1)
                nc.gpsimd.tensor_tensor(of, of, minus_half[:, :].broadcast_to([P, TILES]), ALU.pow).then_inc(pool_step, 1)

            invert_root(KV)
            pool.wait_ge(w_v_hi_ready, 1)
            nc.gpsimd.tensor_tensor(keep.w_v_lo[:, :], w_v[:, :], keep.w_v_hi[:, :].bitcast(F32), ALU.subtract)\
              .then_inc(late_lo_ready, 1)
            pool.wait_ge(k_rope_hi, 1)
            nc.gpsimd.tensor_tensor(keep.k_rope_lo[:, :], k_swapped[:, :], keep.k_rope[0:ROPE, :].bitcast(F32),
                                    ALU.subtract).then_inc(late_lo_ready, 1)
            invert_root(Q)
            pool.wait_ge(pool_step, 4)
            nc.gpsimd.tensor_scalar(keep.q_scale[:, :], mean_sq[:, Q * TILES:], MLA_SCALE, None, ALU.mult)\
              .then_inc(late_lo_ready, 1)
            pool.wait_ge(ckv_hi_ready, 1)
            nc.gpsimd.tensor_tensor(keep.ckv_lo[:, :], big[:, :], keep.ckv_hi[:, :].bitcast(F32), ALU.subtract)\
              .then_inc(late_lo_ready, 1)

        @block.scalar
        def _(act):
            nc.scalar.activation(squares[0][:, :], ckv, ACT.Square, scale=P ** -0.5).then_inc(sq_ready, 1)
            act.wait_ge(rope_weights_loaded, 48)
            nc.scalar.activation(w_rope_hi[:, :, :, :], w_rope[:, :, :, :], ACT.Copy).then_inc(w_rope_hi_ready, 1)
            for n in range(2):
                nc.scalar.activation(keep.cq_hi[:, n, :], cq[:, n, :], ACT.Copy, scale=q_gain[:, n:n + 1])\
                  .then_inc(cq_hi_ready, 1)
            act.wait_ge(kv_sq_mm, 1)
            nc.scalar.activation(mean_sq[:, :TILES], psum[:, 6, 0:TILES], ACT.Copy).then_inc(mean_ready, 1)
            for n in range(2):
                nc.scalar.activation(squares[1 + n][:, :], cq[:, n, :], ACT.Square, scale=(2 * P) ** -0.5).then_inc(sq_ready, 1)
            act.wait_ge(pool_step, 2)
            nc.scalar.activation(big[:, :].rearrange("p (a b) -> p a b", b=P),
                                 mean_sq[:, :TILES].unsqueeze(2).broadcast_to([P, TILES, P]), ACT.Copy)\
              .then_inc(spread_ready, 1)
            act.wait_ge(weights_loaded, 48)
            nc.scalar.activation(keep.w_v_hi[:, :], w_v[:, :], ACT.Copy).then_inc(w_v_hi_ready, 1)
            for tb in range(TB):
                t = slice(tb * BLK, (tb + 1) * BLK)
                if tb == 2:
                    act.wait_ge(ckv_ready, 1)
                    nc.scalar.activation(keep.ckv_hi[:, :], big[:, :], ACT.Copy).then_inc(ckv_hi_ready, 1)
                    act.wait_ge(k_step, 4)
                    nc.scalar.activation(keep.k_rope[0:ROPE, :], k_swapped[:, :], ACT.Copy).then_inc(k_rope_hi, 1)
                    act.wait_ge(q_sq_mm, 1)
                    nc.scalar.activation(mean_sq[:, TILES:], psum[:, 7, 0:TILES], ACT.Copy).then_inc(mean_ready, 1)
                for n in range(2):
                    act.wait_ge(rope_turned, 2 * tb + n + 1)
                    nc.scalar.activation(rope_half[n, "hi"][:, t], turned[tb % 2][2 * n][:, :], ACT.Copy).then_inc(rope_hi, 1)
            act.wait_ge(w_q_mm, 1)
            nc.scalar.activation(keep.w_q_hi[:, :, :, :], psum[:, 2:4, :].rearrange("p a (h k c) -> p (a h) k c", k=2, c=P),
                                 ACT.Copy).then_inc(w_q_hi_ready, 1)
            act.wait_ge(tokens_mm, 1)
            nc.scalar.activation(keep.tokens_hi[:, :, :].rearrange("p (a t) d -> p a (t d)", a=TB), psum[:, 4:7, :],
                                 ACT.Copy).then_inc(tokens_hi_ready, 1)

        @block.vector
        def _(dve):
            for n in range(2):
                dve.wait_ge(cq_hi_ready, n + 1)
                nc.vector.scalar_tensor_tensor(out=keep.cq_lo[:, n, :], in0=cq[:, n, :], scalar=q_gain[:, n:n + 1],
                                               in1=keep.cq_hi[:, n, :].bitcast(F32), op0=ALU.mult, op1=ALU.subtract)\
                  .then_inc(cq_lo_ready, 1)

            def split_rope(tb):
                t = slice(tb * BLK, (tb + 1) * BLK)
                for n in range(2):
                    dve.wait_ge(rope_hi, 2 * tb + n + 1)
                    nc.vector.tensor_tensor(rope_half[n, "lo"][:, t], turned[tb % 2][2 * n][:, :],
                                            rope_half[n, "hi"][:, t].bitcast(F32), ALU.subtract).then_inc(rope_lo, 1)

            dve.wait_ge(swapped, 32)
            dve.wait_ge(tables_loaded, 32)
            k_raw = z[0:ROPE, Z_LR, :]
            nc.vector.tensor_tensor(k_swapped[:, :], k_swapped[:, :], sin[0:ROPE, :], ALU.mult).then_inc(k_step, 1)
            nc.vector.tensor_tensor(k_raw, k_raw, cos[0:ROPE, :], ALU.mult).then_inc(k_step, 1)
            for tb in range(TB):
                t = slice(tb * BLK, (tb + 1) * BLK)
                one, two = psum[:, 2 * (tb % 2), :], psum[:, 2 * (tb % 2) + 1, :]
                parts = turned[tb % 2]
                if tb == 2:
                    dve.wait_ge(spread_mm, 1)
                    nc.vector.scalar_tensor_tensor(out=big[:, :].rearrange("p (a t) -> p a t", a=TB),
                                                   in0=ckv.rearrange("p (a t) -> p a t", a=TB), scalar=kv_gain[:, 0:1],
                                                   in1=psum[:, 4:7, :], op0=ALU.mult, op1=ALU.mult).then_inc(ckv_ready, 1)
                    dve.wait_ge(k_step, 2)
                    for n, op in enumerate((ALU.subtract, ALU.add)):
                        rows = slice(n * HALF_ROPE, (n + 1) * HALF_ROPE)
                        nc.vector.tensor_tensor(k_swapped[rows, :], z[rows, Z_LR, :], k_swapped[rows, :], op).then_inc(k_step, 1)
                dve.wait_ge(rope_mm, tb + 1)
                if tb >= 2:
                    dve.wait_ge(rope_lo, 2 * tb - 2)
                for part, (half, table) in zip(parts, ((one, cos), (two, sin), (two, cos), (one, sin))):
                    nc.vector.tensor_tensor(part[:, :], half, table[:, t], ALU.mult).then_inc(rope_parts, 1)
                if tb:
                    split_rope(tb - 1)
                for n, op in enumerate((ALU.subtract, ALU.add)):
                    dve.wait_ge(rope_parts, 4 * tb + 2 * n + 2)
                    nc.vector.tensor_tensor(parts[2 * n][:, :], parts[2 * n][:, :], parts[2 * n + 1][:, :], op)\
                      .then_inc(rope_turned, 1)
            split_rope(TB - 1)
            dve.wait_ge(w_q_hi_ready, 1)
            nc.vector.tensor_tensor(keep.w_q_lo[:, :, :, :], psum[:, 2:4, :].rearrange("p a (h k c) -> p (a h) k c", k=2, c=P),
                                    keep.w_q_hi[:, :, :, :].bitcast(F32), ALU.subtract).then_inc(late_lo_ready, 1)
            dve.wait_ge(tokens_hi_ready, 1)
            nc.vector.tensor_tensor(keep.tokens_lo[:, :, :].rearrange("p (a t) d -> p a (t d)", a=TB), psum[:, 4:7, :],
                                    keep.tokens_hi[:, :, :].rearrange("p (a t) d -> p a (t d)", a=TB).bitcast(F32),
                                    ALU.subtract).then_inc(late_lo_ready, 1)

        @block.tensor
        def _(pe):
            def sum_squares(n, bank, first, last):
                pe.wait_ge(sq_ready, n + 1)
                for t in range(TILES):
                    mm = nc.tensor.matmul(psum[:, bank, t:t + 1], squares[n][:, t * P:(t + 1) * P], ones[:, :],
                                          start=(first and t == 0), stop=(last and t == TILES - 1), skip_group_check=True)
                return mm

            def rope_queries(tb):
                t = slice(tb * BLK, (tb + 1) * BLK)
                for n in range(2):
                    for k in range(2):
                        mm = product(nc, psum[:, 2 * (tb % 2) + n, :], w_rope_hi[:, n, k, :], w_rope_lo[:, n, k, :],
                                     keep.cq_hi[:, k, t], keep.cq_lo[:, k, t], k == 0, k == 1)
                mm.then_inc(rope_mm, 1)

            pe.wait_ge(ones_set, 2)
            sum_squares(0, 6, True, True).then_inc(kv_sq_mm, 1)
            pe.wait_ge(w_rope_lo_ready, 1)
            pe.wait_ge(cq_lo_ready, 2)
            rope_queries(0)
            rope_queries(1)
            sum_squares(1, 7, True, False)
            pe.wait_ge(spread_ready, 1)
            for t in range(TILES):
                mm = nc.tensor.matmul(psum[:, 4 + t // 4, (t % 4) * P:(t % 4 + 1) * P], big[:, t * P:(t + 1) * P],
                                      ident[:, :], start=True, stop=True)
            mm.then_inc(spread_mm, 1)
            pe.wait_ge(rope_turned, 2)
            rope_queries(2)
            sum_squares(2, 7, False, True).then_inc(q_sq_mm, 1)
            pe.wait_ge(weights_loaded, 48)
            pe.wait_ge(rope_turned, 4)
            for h in range(HEADS):
                for k in range(2):
                    n = 2 * h + k
                    mm = nc.tensor.matmul(psum[:, 2 + n // 4, (n % 4) * P:(n % 4 + 1) * P], w_uq_t[:, h, k, :],
                                          w_uk_t[:, h, :], start=True, stop=True)
            mm.then_inc(w_q_mm, 1)
            pe.wait_ge(ckv_ready, 1)
            for t in range(TILES):
                mm = nc.tensor.transpose(psum[:, 4 + t // 4, (t % 4) * P:(t % 4 + 1) * P], big[:, t * P:(t + 1) * P],
                                         ident[:, :])
            mm.then_inc(tokens_mm, 1)


class MlaKeep:

    def __init__(self, nc):
        low = Region(nc, Z_Q * NT * 4, Z_Q * NT * 4 + 2 * NT * 4)
        high = Region(nc, MLA_AT)
        self.mixed = high("mla_mixed", [P, HEADS, NT])
        self.cq_hi = high("mla_cq_hi", [P, 2, NT], F32R)
        self.cq_lo = high("mla_cq_lo", [P, 2, NT], F32R)
        self.w_q_at = high.at
        self.w_q_hi = high("mla_w_q_hi", [P, HEADS, 2, P], F32R)
        self.w_q_lo = high("mla_w_q_lo", [P, HEADS, 2, P], F32R)
        self.ckv_hi = high("mla_ckv_hi", [P, NT], F32R)
        self.ckv_lo = high("mla_ckv_lo", [P, NT], F32R)
        self.tokens_at = high.at
        self.tokens_hi = high("mla_tokens_hi", [P, TILES, P], F32R)
        self.tokens_lo = high("mla_tokens_lo", [P, TILES, P], F32R)
        self.w_v_hi = high("mla_w_v_hi", [P, HEADS * P], F32R)
        self.w_v_lo = high("mla_w_v_lo", [P, HEADS * P], F32R)
        self.q_scale = high("mla_q_scale", [P, TILES])
        self.next_at = high.at
        self.k_rope = low("mla_k_rope", [P, NT], F32R)
        self.k_rope_lo = low("mla_k_rope_lo", [ROPE, NT], F32R)
        self.low_free = Region(nc, Z_AT, Z_Q * NT * 4)
        self.w_out = Region(nc, MLA_AT + MLA_BYTES)("o_w_raw", [P, KT, D_MODEL])


SEQ_TILES = tuple((t0 // P, n // P) for t0, n in SEQS)
QUERY_TILES = [(f + n, f, count) for f, count in SEQ_TILES for n in range(count)]
STEPS = HEADS * TILES
SLOTS = 3
PAIR = 2 * P
PAIRS = STEPS // 2
TURN_LAG, VALUES_LAG, OUTPUT_LAG, GATHER_LAG = 2, 4, 5, 6
PROJECT_AT = {5: 0, 7: 1, 9: 2}


def turn_order():
    count, tile_end, query_end = 0, {}, {}
    for b in range(TB):
        count += 1
        query_end[0, b] = count
    for m in range(TURN_LAG, STEPS + TURN_LAG):
        if m // TILES + 1 < HEADS and m % TILES in PROJECT_AT:
            count += 1
            query_end[m // TILES + 1, PROJECT_AT[m % TILES]] = count
        count += QUERY_TILES[(m - TURN_LAG) % TILES][2] // 4
        tile_end[m - TURN_LAG] = count
    return tile_end, query_end


TILE_END, QUERY_END = turn_order()


def turned_banks(m):
    count = QUERY_TILES[m % TILES][2] // 4
    return [(n, TILE_END[m] - count + n + 1) for n in range(count)]


def projected_at(m):
    if m // TILES + 1 < HEADS and m % TILES in PROJECT_AT:
        return [(m // TILES + 1, PROJECT_AT[m % TILES])]
    return []


def pair_at(m, lag):
    return [(m - lag) // 2] if (m - lag) % 2 and 0 < m - lag < STEPS else []


def phase_mla_attend(nc, cx, rope_dram, gates_dram, w_out_dram, w_out_loaded, psum, ident, keep):
    with ExitStack() as mem:
        sem = cx.semaphore
        sb = Region(nc, keep.next_at)
        q_rope = keep.low_free("a_q_rope", [P, NT], F32R)
        q_hi = sb("a_q_hi", [P, 2, NT], F32R)
        q_lo = sb("a_q_lo", [P, 2, NT], F32R)
        turned_hi = sb("a_turned_hi", [P, 2, KT, PAIR], F32R)
        turned_lo = sb("a_turned_lo", [P, 2, KT, PAIR], F32R)
        latent_hi = sb("a_latent_hi", [P, 2, PAIR], F32R)
        latent_lo = sb("a_latent_lo", [P, 2, PAIR], F32R)
        top = sb("a_top", [P, STEPS])
        bias = sb("a_bias", [P, STEPS])
        total = sb("a_total", [P, STEPS])
        share = sb("a_share", [P, STEPS])
        latents = Region(nc, Z_CQ * NT * 4, AFTER_Z)
        gate = latents("a_gate", [P, 2, PAIR])
        weights = latents("a_weights", [P, SLOTS, 1024])

        rope_loaded = [sem(f"a_rope_loaded{n}") for n in range(TB)]
        gate_loaded = [sem(f"a_gate_loaded{n}") for n in range(2)]
        scores_done = sem("a_scores_done")
        top_ready = sem("a_top_ready")
        bias_ready = sem("a_bias_ready")
        exp_done = sem("a_exp_done")
        share_ready = sem("a_share_ready")
        turned = sem("a_turned")
        turned_hi_ready = sem("a_turned_hi_ready")
        turned_lo_ready = sem("a_turned_lo_ready")
        values_done = sem("a_values_done")
        latent_hi_ready = sem("a_latent_hi_ready")
        latent_lo_ready = sem("a_latent_lo_ready")
        output_done = sem("a_output_done")
        gate_shared = sem("a_gate_shared")
        gathered = sem("a_gathered")

        block = mem.enter_context(nc.Block())

        @block.sync
        def _(sp):
            def load_rope(h, b):
                t = slice(b * BLK, (b + 1) * BLK)
                sp.dma_start(q_rope[:, t].bitcast(F32), rope_dram[h, :, t]).then_inc(rope_loaded[b], 16)

            for b in range(TB):
                load_rope(0, b)
            for h in range(HEADS):
                for b in range(TB):
                    for p in range(2 * TB * h + 2 * b, 2 * TB * h + 2 * b + 2):
                        if p >= 2:
                            sp.wait_ge(gathered, p - 1)
                        t = (p % (2 * TB)) * PAIR
                        sp.dma_start(gate[:, p % 2, :], gates_dram[h, :, t:t + PAIR]).then_inc(gate_loaded[p % 2], 16)
                    if (h, b) == (HEADS - 1, 1):
                        sp.wait_ge(turned, QUERY_END[HEADS - 1, TB - 1])
                        for k in range(KT):
                            sp.dma_start(keep.w_out[:, k, :], w_out_dram[k * P:(k + 1) * P, :]).then_inc(w_out_loaded[k], 16)
                    if h + 1 < HEADS:
                        sp.wait_ge(scores_done, TILES * h + 4 * b + 4)
                        load_rope(h + 1, b)

        @block.scalar
        def _(act):
            def project(h, b):
                act.wait_ge(turned, QUERY_END[h, b])
                if h >= 2:
                    act.wait_ge(scores_done, TILES * (h - 2) + 4 * b + 4)
                nc.scalar.activation(q_hi[:, h % 2, b * BLK:(b + 1) * BLK], psum[:, 4 + QUERY_END[h, b] % 2, :],
                                     ACT.Copy).then_inc(turned_hi_ready, 1)

            for b in range(TB):
                project(0, b)
            for m in range(STEPS + GATHER_LAG):
                if m < STEPS:
                    tile, _, count = QUERY_TILES[m % TILES]
                    banks = slice(2 * (m % 2), 2 * (m % 2) + count // 4)
                    act.wait_ge(bias_ready, m + 1)
                    if m >= SLOTS:
                        act.wait_ge(turned, TILE_END[m - SLOTS])
                    nc.scalar.activation(weights[:, m % SLOTS, 0:count * P].rearrange("p (a k) -> p a k", k=BLK),
                                         psum[:, banks, :], ACT.Exp, bias=bias[:, m:m + 1],
                                         scale=keep.q_scale[:, tile:tile + 1], accum_out=total[:, m:m + 1])\
                      .then_inc(exp_done, 1)
                for h, b in projected_at(m):
                    project(h, b)
                for p in pair_at(m, VALUES_LAG):
                    act.wait_ge(values_done, p + 1)
                    nc.scalar.activation(latent_hi[:, p % 2, :], psum[:, 6 + p % 2, :PAIR], ACT.Copy)\
                      .then_inc(latent_hi_ready, 1)
                if 0 <= m - TURN_LAG < STEPS:
                    tile = m - TURN_LAG
                    p = tile // 2
                    if tile % 2 == 0 and p >= 2:
                        act.wait_ge(values_done, p - 1)
                    for n, item in turned_banks(tile):
                        act.wait_ge(turned, item)
                        nc.scalar.activation(turned_hi[:, p % 2, 4 * n:4 * n + 4, (tile % 2) * P:(tile % 2 + 1) * P],
                                             psum[:, 4 + item % 2, :].rearrange("p (k q) -> p k q", k=4),
                                             ACT.Copy).then_inc(turned_hi_ready, 1)

        @block.vector
        def _(dve):
            def project(h, b):
                t = slice(b * BLK, (b + 1) * BLK)
                dve.wait_ge(turned_hi_ready, QUERY_END[h, b])
                nc.vector.tensor_tensor(q_lo[:, h % 2, t], psum[:, 4 + QUERY_END[h, b] % 2, :],
                                        q_hi[:, h % 2, t].bitcast(F32), ALU.subtract).then_inc(turned_lo_ready, 1)

            for b in range(TB):
                project(0, b)
            for m in range(STEPS + GATHER_LAG):
                if m < STEPS:
                    tile, _, count = QUERY_TILES[m % TILES]
                    banks = slice(2 * (m % 2), 2 * (m % 2) + count // 4)
                    dve.wait_ge(scores_done, m + 1)
                    nc.vector.tensor_reduce(top[:, m:m + 1], psum[:, banks, :], mybir.AxisListType.XY, ALU.max)\
                      .then_inc(top_ready, 1)
                    dve.wait_ge(top_ready, m + 1)
                    nc.vector.tensor_scalar(bias[:, m:m + 1], top[:, m:m + 1], keep.q_scale[:, tile:tile + 1], -1.0,
                                            ALU.mult, ALU.mult).then_inc(bias_ready, 1)
                for p in pair_at(m, GATHER_LAG):
                    h, t = p // (2 * TB), (p % (2 * TB)) * PAIR
                    dve.wait_ge(gate_loaded[p % 2], 16 * (p // 2) + 16)
                    dve.wait_ge(output_done, p + 1)
                    nc.vector.tensor_tensor(gate[:, p % 2, :], gate[:, p % 2, :], psum[:, 6 + p % 2, PAIR:], ALU.mult)\
                      .then_inc(gate_shared, 1)
                    dve.wait_ge(gate_shared, p + 1)
                    nc.vector.tensor_tensor(keep.mixed[:, h, t:t + PAIR], psum[:, 6 + p % 2, :PAIR],
                                            gate[:, p % 2, :], ALU.mult).then_inc(gathered, 1)
                for h, b in projected_at(m):
                    project(h, b)
                for p in pair_at(m, VALUES_LAG):
                    dve.wait_ge(latent_hi_ready, p + 1)
                    nc.vector.tensor_tensor(latent_lo[:, p % 2, :], psum[:, 6 + p % 2, :PAIR],
                                            latent_hi[:, p % 2, :].bitcast(F32), ALU.subtract)\
                      .then_inc(latent_lo_ready, 1)
                if 0 <= m - TURN_LAG < STEPS:
                    tile = m - TURN_LAG
                    dve.wait_ge(exp_done, tile + 1)
                    nc.vector.reciprocal(share[:, tile:tile + 1], total[:, tile:tile + 1]).then_inc(share_ready, 1)
                    for n, item in turned_banks(tile):
                        dve.wait_ge(turned_hi_ready, item)
                        at = (slice(None), (tile // 2) % 2, slice(4 * n, 4 * n + 4),
                              slice((tile % 2) * P, (tile % 2 + 1) * P))
                        nc.vector.tensor_tensor(turned_lo[at], psum[:, 4 + item % 2, :].rearrange("p (k q) -> p k q", k=4),
                                                turned_hi[at].bitcast(F32), ALU.subtract).then_inc(turned_lo_ready, 1)

        @block.tensor
        def _(pe):
            def project(h, b):
                item = QUERY_END[h, b]
                if item > 2:
                    pe.wait_ge(turned_lo_ready, item - 2)
                t = slice(b * BLK, (b + 1) * BLK)
                for k in range(2):
                    mm = product(nc, psum[:, 4 + item % 2, :], keep.w_q_hi[:, h, k, :], keep.w_q_lo[:, h, k, :],
                                 keep.cq_hi[:, k, t], keep.cq_lo[:, k, t], k == 0, k == 1)
                mm.then_inc(turned, 1)

            def scores(m):
                h, g = m // TILES, m % TILES
                tile, first, count = QUERY_TILES[g]
                q = slice(tile * P, (tile + 1) * P)
                if g % 4 == 0:
                    pe.wait_ge(rope_loaded[g // 4], 16 * (h + 1))
                    pe.wait_ge(turned_lo_ready, QUERY_END[h, g // 4])
                if m >= 2:
                    pe.wait_ge(exp_done, m - 1)
                for n in range(count // 4):
                    k = slice(first * P + n * BLK, first * P + (n + 1) * BLK)
                    out = psum[:, 2 * (m % 2) + n, :]
                    product(nc, out, q_hi[:, h % 2, q], q_lo[:, h % 2, q], keep.ckv_hi[:, k], keep.ckv_lo[:, k], True, False)
                    nc.tensor.matmul(out, q_rope[:, q], keep.k_rope[:, k], start=False, stop=False)
                    mm = nc.tensor.matmul(out, q_rope[0:ROPE, q], keep.k_rope_lo[:, k], start=False, stop=True)
                mm.then_inc(scores_done, 1)

            def turn(m):
                pe.wait_ge(exp_done, m + 1)
                for n, item in turned_banks(m):
                    pe.wait_ge(turned_lo_ready, item - 2)
                    for k in range(4):
                        mm = nc.tensor.transpose(psum[:, 4 + item % 2, k * P:(k + 1) * P],
                                                 weights[:, m % SLOTS, (4 * n + k) * P:(4 * n + k + 1) * P], ident[:, :])
                    mm.then_inc(turned, 1)

            def values(p):
                _, first, count = QUERY_TILES[(2 * p) % TILES]
                if p >= 2:
                    pe.wait_ge(gathered, p - 1)
                pe.wait_ge(turned_lo_ready, TILE_END[2 * p + 1])
                for k in range(count):
                    mm = product(nc, psum[:, 6 + p % 2, :PAIR], keep.tokens_hi[:, first + k, :],
                                 keep.tokens_lo[:, first + k, :], turned_hi[:, p % 2, k, :], turned_lo[:, p % 2, k, :],
                                 k == 0, k == count - 1)
                mm.then_inc(values_done, 1)

            def output(p):
                h = p // (2 * TB)
                pe.wait_ge(share_ready, 2 * p + 2)
                pe.wait_ge(latent_lo_ready, p + 1)
                for n in range(2):
                    nc.tensor.matmul(psum[:, 6 + p % 2, PAIR + n * P:PAIR + (n + 1) * P],
                                     share[:, 2 * p + n:2 * p + n + 1].broadcast_to([P, P]), ident[:, :],
                                     start=True, stop=True)
                product(nc, psum[:, 6 + p % 2, :PAIR], keep.w_v_hi[:, h * P:(h + 1) * P], keep.w_v_lo[:, h * P:(h + 1) * P],
                        latent_hi[:, p % 2, :], latent_lo[:, p % 2, :]).then_inc(output_done, 1)

            for b in range(TB):
                project(0, b)
            for m in range(STEPS + GATHER_LAG):
                if m < STEPS:
                    scores(m)
                for h, b in projected_at(m):
                    project(h, b)
                for p in pair_at(m, VALUES_LAG):
                    values(p)
                if 0 <= m - TURN_LAG < STEPS:
                    turn(m - TURN_LAG)
                for p in pair_at(m, OUTPUT_LAG):
                    output(p)


def phase_output(nc, cx, w_loaded, final_g_dram, x_dram, y_dram, z, keep, psum):
    with ExitStack() as mem:
        sem = cx.semaphore
        mla_mixed, w_raw = keep.mixed, keep.w_out
        sb = Region(nc, MLA_AT + MLA_BYTES + KT * D_MODEL * 4)
        w_hi = sb("o_w_hi", [P, KT, D_MODEL], F32R)
        w_lo = sb("o_w_lo", [P, KT, D_MODEL], F32R)
        m_hi = sb("o_m_hi", [P, 2, KT, P], F32R)
        m_lo = sb("o_m_lo", [P, 2, KT, P], F32R)
        y = sb("o_y", [P, 2, D_MODEL])
        low = Region(nc, Z_AT, Z_V * NT * 4)
        g_row = low("o_g_row", [P, D_MODEL])
        x_in = low("o_x_in", [P, 2, D_MODEL])
        squares = Region(nc, Z_CQ * NT * 4, AFTER_Z)("o_squares", [P, 2, D_MODEL])
        mean_sq = sb("o_mean_sq", [P, 2])
        rstd = sb("o_rstd", [P, 2])
        eps = sb("o_eps", [P, 1])
        minus_half = sb("o_minus_half", [P, 1])

        g_loaded = sem("o_g_loaded")
        x_loaded = [sem(f"o_x_loaded{n}") for n in range(2)]
        y_stored = [sem(f"o_y_stored{n}") for n in range(2)]
        w_hi_ready = sem("o_w_hi_ready")
        w_lo_ready = sem("o_w_lo_ready")
        w_lo_pool = sem("o_w_lo_pool")
        half_set = sem("o_half_set")
        m_hi_ready = sem("o_m_hi_ready")
        m_lo_ready = sem("o_m_lo_ready")
        out_mm = sem("o_out_mm")
        summed = sem("o_summed")
        squares_done = sem("o_squares_done")
        eps_added = sem("o_eps_added")
        rstd_ready = sem("o_rstd_ready")
        y_ready = sem("o_y_ready")
        pairs = TILES // 2

        block = mem.enter_context(nc.Block())

        @block.sync
        def _(sp):
            sp.dma_start(g_row[:, :], final_g_dram.partition_broadcast(P)).then_inc(g_loaded, 16)
            for s in range(2):
                sp.dma_start(x_in[:, s, :], x_dram[rows_of(s), :]).then_inc(x_loaded[s], 16)
            with sp.Fori(1, pairs) as i:
                for s in range(2):
                    sp.wait_ge(summed, 4 * i + 2 * s - 2)
                    sp.dma_start(x_in[:, s, :], x_dram[rows_of(2 * i + s), :]).then_inc(x_loaded[s], 16)

        @block.gpsimd
        def _(pool):
            for k in range(1, KT, 3):
                pool.wait_ge(w_hi_ready, k + 1)
                nc.gpsimd.tensor_tensor(w_lo[:, k, :], w_raw[:, k, :], w_hi[:, k, :].bitcast(F32), ALU.subtract)\
                  .then_inc(w_lo_pool, 1)
            nc.gpsimd.memset(minus_half[:, :], -0.5).then_inc(half_set, 1)
            nc.gpsimd.memset(eps[:, :], EPS).then_inc(half_set, 1)
            pool.wait_ge(half_set, 2)
            with pool.Fori(0, pairs) as i:
                for s in range(2):
                    n, slot = 2 * i + s, slice(s, s + 1)
                    pool.wait_ge(squares_done, n + 1)
                    nc.gpsimd.tensor_tensor(rstd[:, slot], mean_sq[:, slot], eps[:, :], ALU.add).then_inc(eps_added, 1)
                    pool.wait_ge(eps_added, n + 1)
                    nc.gpsimd.tensor_tensor(rstd[:, slot], rstd[:, slot], minus_half[:, :],
                                            ALU.pow).then_inc(rstd_ready, 1)

        @block.scalar
        def _(act):
            def take_hi(i, s, first):
                n = 2 * i + s
                if not first:
                    act.wait_ge(out_mm, 2 * n - 2)
                nc.scalar.activation(m_hi[:, s, 0:4, :], mla_mixed[:, :, rows_of(n)], ACT.Copy).then_inc(m_hi_ready, 1)
                nc.scalar.activation(m_hi[:, s, 4:8, :], z[:, Z_V:Z_V + 4, rows_of(n)], ACT.Copy).then_inc(m_hi_ready, 1)

            def finish(i, s, first):
                n = 2 * i + s
                if not first:
                    act.wait_ge(eps_added, n - 1)
                act.wait_ge(summed, 2 * n + 2)
                nc.scalar.activation(squares[:, s, :], y[:, s, :], ACT.Square, scale=D_MODEL ** -0.5,
                                     accum_out=mean_sq[:, s:s + 1]).then_inc(squares_done, 1)

            def store(i, s):
                n = 2 * i + s
                act.wait_ge(y_ready, n + 1)
                act.dma_start(y_dram[rows_of(n), :], y[:, s, :]).then_inc(y_stored[s], 16)

            for k in range(KT):
                act.wait_ge(w_loaded[k], 16)
                if k < 2:
                    take_hi(0, k, True)
                nc.scalar.activation(w_hi[:, k, :], w_raw[:, k, :], ACT.Copy).then_inc(w_hi_ready, 1)
            finish(0, 0, True)
            take_hi(1, 0, False)
            store(0, 0)
            finish(0, 1, True)
            take_hi(1, 1, False)
            store(0, 1)
            with act.Fori(1, pairs - 1) as i:
                for s in range(2):
                    finish(i, s, False)
                    take_hi(i + 1, s, False)
                    store(i, s)
            for s in range(2):
                finish(pairs - 1, s, False)
                store(pairs - 1, s)
            for s in range(2):
                act.wait_ge(y_stored[s], 16 * pairs)

        @block.vector
        def _(dve):
            def take_lo(i, s):
                n = 2 * i + s
                dve.wait_ge(m_hi_ready, 2 * n + 1)
                nc.vector.tensor_tensor(m_lo[:, s, 0:4, :], mla_mixed[:, :, rows_of(n)], m_hi[:, s, 0:4, :].bitcast(F32),
                                        ALU.subtract).then_inc(m_lo_ready, 1)
                dve.wait_ge(m_hi_ready, 2 * n + 2)
                nc.vector.tensor_tensor(m_lo[:, s, 4:8, :], z[:, Z_V:Z_V + 4, rows_of(n)], m_hi[:, s, 4:8, :].bitcast(F32),
                                        ALU.subtract).then_inc(m_lo_ready, 1)

            def add_input(i, s, first):
                n = 2 * i + s
                dve.wait_ge(x_loaded[s], 16 * i + 16)
                if not first:
                    dve.wait_ge(y_stored[s], 16 * i)
                for half in range(2):
                    dve.wait_ge(out_mm, 2 * n + half + 1)
                    cols = slice(half * BLK, (half + 1) * BLK)
                    nc.vector.tensor_tensor(y[:, s, cols], psum[:, 2 * s + half, :], x_in[:, s, cols], ALU.add)\
                      .then_inc(summed, 1)

            def normalise(i, s):
                n = 2 * i + s
                dve.wait_ge(rstd_ready, n + 1)
                nc.vector.scalar_tensor_tensor(out=y[:, s, :], in0=y[:, s, :], scalar=rstd[:, s:s + 1],
                                               in1=g_row[:, :], op0=ALU.mult, op1=ALU.mult).then_inc(y_ready, 1)

            take_lo(0, 0)
            for k in range(KT):
                if k % 3 != 1:
                    dve.wait_ge(w_hi_ready, k + 1)
                    nc.vector.tensor_tensor(w_lo[:, k, :], w_raw[:, k, :], w_hi[:, k, :].bitcast(F32), ALU.subtract)\
                      .then_inc(w_lo_ready, 1)
            take_lo(0, 1)
            dve.wait_ge(g_loaded, 16)
            for s in range(2):
                add_input(0, s, True)
                take_lo(1, s)
                normalise(0, s)
            with dve.Fori(1, pairs - 1) as i:
                for s in range(2):
                    add_input(i, s, False)
                    take_lo(i + 1, s)
                    normalise(i, s)
            for s in range(2):
                add_input(pairs - 1, s, False)
                normalise(pairs - 1, s)

        @block.tensor
        def _(pe):
            def multiply(i, s, first):
                n = 2 * i + s
                pe.wait_ge(m_lo_ready, 2 * n + 2)
                for half in range(2):
                    if not first:
                        pe.wait_ge(summed, 2 * n - 3 + half)
                    cols = slice(half * BLK, (half + 1) * BLK)
                    for k in range(KT):
                        if first and s == 0 and half == 0:
                            if k % 3 == 1:
                                pe.wait_ge(w_lo_pool, k // 3 + 1)
                            else:
                                pe.wait_ge(w_lo_ready, k + 1 - (k + 1) // 3)
                        mm = product(nc, psum[:, 2 * s + half, :], m_hi[:, s, k, :], m_lo[:, s, k, :],
                                     w_hi[:, k, cols], w_lo[:, k, cols], k == 0, k == KT - 1)
                    mm.then_inc(out_mm, 1)

            for s in range(2):
                multiply(0, s, True)
            with pe.Fori(1, pairs) as i:
                for s in range(2):
                    multiply(i, s, False)


class Semaphores:

    def __init__(self, nc, stack):
        self.nc, self.stack = nc, stack

    def semaphore(self, name):
        return self.stack.enter_context(self.nc.semaphore(name))


def hymba_encoder_kernel(nc, dram, y_dram):
    with ExitStack() as whole:
        cx = Semaphores(nc, whole)
        scratch = lambda name, shape, dt: nc.dram_tensor(name, shape, dt, kind="Internal").ap()
        psum = whole.enter_context(nc.psum_tensor("psum", [P, 8, BLK], F32))
        ident = Region(nc, SBUF_BYTES, SBUF_BYTES + P * 4)("ident", [P, P])
        gates_dram = scratch("gates_scratch", (Z_GATES, P, NT), F32)
        rope_dram = scratch("rope_scratch", (HEADS, P, NT), F32)
        z = Region(nc, Z_AT)("z", [P, Z_PLAIN, NT])
        h_mem = Region(nc, AFTER_Z)
        h_hi = h_mem("h_hi", [P, KT, NT], F32R)
        h_lo = h_mem("h_lo", [P, KT, NT], F32R)
        sums_mem = Region(nc, SUMS_AT)
        sums = [sums_mem(f"gate_sums{d}", [P, CHUNKS, CHUNK + 1]) for d in range(2)]
        phase_project(nc, cx, dram, gates_dram, h_hi, h_lo, z, psum, ident, sums)
        phase_gla(nc, cx, dram, gates_dram, z, psum, ident, sums)
        keep = MlaKeep(nc)
        phase_mla_prepare(nc, cx, dram, rope_dram, z, psum, ident, keep)
        w_out_loaded = [cx.semaphore(f"w_out_loaded{k}") for k in range(KT)]
        phase_mla_attend(nc, cx, rope_dram, gates_dram, dram["w_out"], w_out_loaded, psum, ident, keep)
        phase_output(nc, cx, w_out_loaded, dram["final_norm_g"], dram["x"], y_dram, z, keep, psum)


POOL_WINDOWS = (2, 4, 8, 16)
ROPE_BASE = 10000.0
IN_COLUMNS = ((Z_LR, 384, 448, 0), (Z_LR, 1984, 2016, 64),
              (Z_Q, 1472, 1600, 0), (Z_K, 1600, 1728, 0), (Z_V, 1728, 1984, 0),
              (Z_U, 960, 1216, 0),
              (Z_FIRST_GATE, 448, 960, 0), (Z_FIRST_GATE + 4, 1216, 1472, 0), (Z_FIRST_GATE + 6, 2016, 2272, 0),
              (Z_CQ + Z_GATES, 0, 256, 0), (Z_CKV + Z_GATES, 256, 384, 0))


def shape_tables(np):
    lane = np.arange(P)
    edge = np.ones((P, 2, 2, POOL_PAD), np.float32)
    mean = np.zeros((P, 2), np.float32)
    for g, w in enumerate(POOL_WINDOWS):
        u, rows = g // 2, slice(64 * (g % 2), 64 * (g % 2) + 64)
        mean[rows, u] = 1.0 / w
        for t in range(POOL_PAD):
            edge[rows, u, 0, t] = w / (w // 2 + min(t, w // 2))
            edge[rows, u, 1, t] = w / (w // 2 + min(POOL_PAD - t, w // 2))
    level_mask = np.zeros((P, LEVELS, CHUNK), np.float32)
    for key in range(P):
        for query in range(CHUNK):
            apart = (key % CHUNK) ^ query
            level_mask[key, LEVELS - 1 - apart.bit_length(), query] = 1.0 if apart else 2.0
    inverse = (1.0 / ROPE_BASE ** (np.arange(0, ROPE, 2, dtype=np.float32) / np.float32(ROPE))).astype(np.float32)
    position = np.concatenate([np.arange(n) for _, n in SEQS]).astype(np.float32)
    angle = inverse[:, None] * position[None]
    return {
        "ident": np.eye(P, dtype=np.float32),
        "pool_edge": edge,
        "pool_mean": mean,
        "level_mask": level_mask.reshape(P, LEVELS * CHUNK),
        "pair_mask": ((lane[:, None] // DK) % 2 == lane[None, :] // DV).astype(np.float32),
        "head_ones": (lane[:, None] // DV == np.arange(2)).astype(np.float32),
        "rope_cos": np.tile(np.cos(angle), (HEADS, 1)),
        "rope_sin": np.tile(np.sin(angle), (HEADS, 1)),
    }


def lay_out(np, inp):
    w_in = inp["w_in"][0]
    columns = np.zeros((D_MODEL, Z_TILES * P), np.float32)
    for tile, start, end, at in IN_COLUMNS:
        columns[:, tile * P + at:tile * P + at + end - start] = w_in[:, start:end]
    gate_up = np.zeros((32, 2, P), np.float32)
    gate_up[:16, FWD], gate_up[16:, BWD] = inp["gk_up_fwd"][0], inp["gk_up_bwd"][0]
    w_pool = np.zeros((P, 2, P), np.float32)
    for g in range(len(POOL_WINDOWS)):
        at = 64 * (g % 2)
        w_pool[at:at + 64, g // 2, at:at + 64] = inp["w_pool"][0, g]
    w_uq = inp["w_uq"][0].reshape(2 * P, HEADS, NOPE + ROPE)
    w_rope = w_uq[:, :, NOPE:].reshape(2, P, HEADS, 2, HALF_ROPE)
    w_ukv = inp["w_ukv"][0].reshape(P, HEADS, 2 * P)
    w_out = inp["w_out"][0]
    return {
        "x": np.concatenate([inp["x_prompt"][0], inp["x_sample"][0]], 0),
        "w_z": columns.reshape(KT, P, Z_TILES, P).transpose(2, 1, 0, 3).reshape(Z_TILES, P, D_MODEL),
        "norm_g": inp["norm_g"][0],
        "gate_up": gate_up,
        "gate_bias": np.stack([inp["gk_bias_fwd"][0], inp["gk_bias_bwd"][0]], 1),
        "gla_gain": np.tile(inp["gla_norm_g"][0], 2)[:, None],
        "w_pool": w_pool,
        "pool_scale": inp["pool_scale"][0].reshape(2, P).T,
        "w_uq_t": w_uq[:, :, :NOPE].transpose(2, 1, 0).reshape(P, HEADS, 2, P),
        "w_uk_t": w_ukv[:, :, :NOPE].transpose(2, 1, 0),
        "w_rope": w_rope.transpose(1, 3, 0, 2, 4).reshape(P, 2, 2, P),
        "w_uv": w_ukv[:, :, NOPE:].reshape(P, HEADS * P),
        "q_gain": inp["q_norm_g"][0].reshape(2, P).T,
        "kv_gain": inp["kv_norm_g"][0][:, None],
        "w_out": np.concatenate([w_out[:512], w_out[768:], w_out[512:768]], 0),
        "final_norm_g": inp["final_norm_g"],
    }


def kernel(**inputs):
    import numpy as np
    import concourse.bacc as bacc
    from concourse.bass_utils import run_bass_kernel_spmd

    inputs = {name: np.asarray(a) for name, a in inputs.items()}
    nc = bacc.Bacc("TRN2", target_bir_lowering=False, num_devices=1)
    arrays, dram = {}, {}
    for name, a in {**lay_out(np, inputs), **shape_tables(np)}.items():
        a = np.ascontiguousarray(a)
        arrays[f"in_{name}_dram"] = a
        dram[name] = nc.dram_tensor(f"in_{name}_dram", a.shape, mybir.dt.from_np(a.dtype), kind="ExternalInput").ap()
    y = nc.dram_tensor("out_dram", (NT, D_MODEL), F32, kind="ExternalOutput").ap()
    hymba_encoder_kernel(nc, dram, y)
    got = run_bass_kernel_spmd(nc, [arrays], core_ids=[0]).results[0]["out_dram"]
    return tuple(got[start:start + n][None] for start, n in SEQS)
```
